# Optimizing a Trainium2 kernel written in Bass

```python
import jax, jax.numpy as jnp
from jax import lax
import numpy as np

D_MODEL = 1024
BATCH = 1
SEQ = 1024
DEPTH = 1

POOL_WIDTH = 256
POOL_GROUPS = 4
POOL_GROUP_DIM = POOL_WIDTH // POOL_GROUPS
POOL_WINDOWS = (2, 4, 8, 16)
GDN_HEADS = 6
GDN_HEAD_DIM = 128
GDN_WIDTH = GDN_HEADS * GDN_HEAD_DIM
D_MIX = POOL_WIDTH + GDN_WIDTH
CONV_WIDTH = 4
CHUNK = 64
D_FF = -(-8 * D_MODEL // (3 * 256)) * 256
IN_COLS = POOL_WIDTH + 4 * GDN_WIDTH + 2 * GDN_HEADS
N_MOD = 6
EPS = 1e-6

kernel_name = 'hybrid_pool_gdn_adaln_block'

def rms_norm(x, gain=None):
    xf = x.astype(jnp.float32)
    y = xf * lax.rsqrt(jnp.mean(xf * xf, axis=-1, keepdims=True) + EPS)
    if gain is not None:
        y = y * gain.astype(jnp.float32)
    return y

def l2_normalize(x):
    return x * lax.rsqrt(jnp.sum(x * x, axis=-1, keepdims=True) + EPS)

def modulate(h, shift, scale):
    return h * (1.0 + scale) + shift

def pool_mixer(u, w_pool, pool_scale):
    B, S, _ = u.shape
    uf = u.astype(jnp.float32).reshape(B, S, POOL_GROUPS, POOL_GROUP_DIM)
    csum = jnp.cumsum(uf, axis=1)
    pos = jnp.arange(1, S + 1, dtype=jnp.float32)
    outs = []
    for gi, w in enumerate(POOL_WINDOWS):
        cs = csum[:, :, gi]
        lag = jnp.pad(cs[:, :S - w], ((0, 0), (w, 0), (0, 0)))
        mean = (cs - lag) / jnp.minimum(pos, w)[None, :, None]
        outs.append(mean - uf[:, :, gi])
    pooled = jnp.stack(outs, axis=2)
    mixed = jnp.einsum('bsgc,gcd->bsgd', pooled, w_pool.astype(jnp.float32))
    mixed = rms_norm(mixed.reshape(B, S, POOL_WIDTH))
    return mixed * pool_scale.astype(jnp.float32)

def causal_depthwise_conv(x, w):
    C = x.shape[-1]
    return lax.conv_general_dilated(
        x, w[:, None, :], window_strides=(1,), padding=[(CONV_WIDTH - 1, 0)],
        dimension_numbers=('NWC', 'WIO', 'NWC'), feature_group_count=C)

def chunk_gated_delta_rule(q, k, v, g, beta):
    B, S, H, Dk = q.shape
    Dv = v.shape[-1]
    N = S // CHUNK
    to_chunks = lambda t: t.reshape(B, N, CHUNK, H, -1).transpose(0, 3, 1, 2, 4)
    q, k, v = to_chunks(q), to_chunks(k), to_chunks(v)
    g = jnp.cumsum(g.reshape(B, N, CHUNK, H).transpose(0, 3, 1, 2), axis=-1)
    beta = beta.reshape(B, N, CHUNK, H).transpose(0, 3, 1, 2)
    idx = jnp.arange(CHUNK)
    causal = idx[:, None] >= idx[None, :]
    strict = idx[:, None] > idx[None, :]
    gdiff = g[..., :, None] - g[..., None, :]
    decay = jnp.where(causal, jnp.exp(jnp.where(causal, gdiff, 0.0)), 0.0)
    kb = k * beta[..., None]
    lower = jnp.where(strict, jnp.einsum('bhnid,bhnjd->bhnij', kb, k) * decay, 0.0)
    eye = jnp.eye(CHUNK, dtype=jnp.float32)
    rhs = jnp.concatenate([v * beta[..., None], kb * jnp.exp(g)[..., None]], axis=-1)
    sol = lax.linalg.triangular_solve(eye + lower, rhs, left_side=True, lower=True,
                                      unit_diagonal=True)
    u, w = sol[..., :Dv], sol[..., Dv:]
    qk = jnp.einsum('bhnid,bhnjd->bhnij', q, k) * decay
    xs = tuple(jnp.moveaxis(t, 2, 0) for t in (q, k, u, w, g, qk))

    def step(state, inp):
        q_c, k_c, u_c, w_c, g_c, qk_c = inp
        v_new = u_c - jnp.einsum('bhik,bhkv->bhiv', w_c, state)
        o_c = (jnp.einsum('bhik,bhkv->bhiv', q_c * jnp.exp(g_c)[..., None], state)
               + jnp.einsum('bhij,bhjv->bhiv', qk_c, v_new))
        g_last = g_c[..., -1:]
        state = (state * jnp.exp(g_last)[..., None]
                 + jnp.einsum('bhik,bhiv->bhkv', k_c * jnp.exp(g_last - g_c)[..., None], v_new))
        return state, o_c

    state0 = jnp.zeros((B, H, Dk, Dv), jnp.float32)
    _, o = lax.scan(step, state0, xs)
    return o.transpose(1, 0, 3, 2, 4).reshape(B, S, H, Dv)

def gated_deltanet_mixer(qkv, z, b, a, conv_w, a_log, dt_bias, o_gain):
    B, S, _ = qkv.shape
    qkv = jax.nn.silu(causal_depthwise_conv(qkv.astype(jnp.float32), conv_w.astype(jnp.float32)))
    q, k, v = jnp.split(qkv, 3, axis=-1)
    q = l2_normalize(q.reshape(B, S, GDN_HEADS, GDN_HEAD_DIM)) * (GDN_HEAD_DIM ** -0.5)
    k = l2_normalize(k.reshape(B, S, GDN_HEADS, GDN_HEAD_DIM))
    v = v.reshape(B, S, GDN_HEADS, GDN_HEAD_DIM)
    beta = jax.nn.sigmoid(b.astype(jnp.float32))
    g = -jnp.exp(a_log.astype(jnp.float32)) * jax.nn.softplus(a.astype(jnp.float32) + dt_bias.astype(jnp.float32))
    o = chunk_gated_delta_rule(q, k, v, g, beta)
    o = rms_norm(o, o_gain) * jax.nn.silu(z.reshape(B, S, GDN_HEADS, GDN_HEAD_DIM).astype(jnp.float32))
    return o.reshape(B, S, GDN_WIDTH)

def setup_inputs(seed: int = 0) -> dict:
    key = jax.random.key(seed)
    ks = jax.random.split(key, 20)
    f32 = jnp.float32
    nrm = lambda k, shape, s: jax.random.normal(k, shape, f32) * s
    dt = jnp.exp(jax.random.uniform(ks[7], (DEPTH, GDN_HEADS), f32, np.log(1e-3), np.log(1e-1)))
    return {
        'x': nrm(ks[0], (BATCH, SEQ, D_MODEL), 1.0),
        'c': nrm(ks[1], (BATCH, D_MODEL), 1.0),
        'w_ada': nrm(ks[2], (DEPTH, D_MODEL, N_MOD * D_MODEL), 0.5 * D_MODEL ** -0.5),
        'b_ada': nrm(ks[3], (DEPTH, N_MOD * D_MODEL), 0.01),
        'norm_mix_gain': 1.0 + nrm(ks[4], (DEPTH, D_MODEL), 0.1),
        'w_in': nrm(ks[5], (DEPTH, D_MODEL, IN_COLS), D_MODEL ** -0.5),
        'conv_w': nrm(ks[6], (DEPTH, CONV_WIDTH, 3 * GDN_WIDTH), CONV_WIDTH ** -0.5),
        'a_log': jnp.log(jax.random.uniform(ks[8], (DEPTH, GDN_HEADS), f32, 1.0, 16.0)),
        'dt_bias': dt + jnp.log(-jnp.expm1(-dt)),
        'gdn_norm_gain': 1.0 + nrm(ks[9], (DEPTH, GDN_HEAD_DIM), 0.1),
        'w_pool': nrm(ks[10], (DEPTH, POOL_GROUPS, POOL_GROUP_DIM, POOL_GROUP_DIM), POOL_GROUP_DIM ** -0.5),
        'pool_scale': 1.0 + nrm(ks[11], (DEPTH, POOL_WIDTH), 0.1),
        'w_out': nrm(ks[12], (DEPTH, D_MIX, D_MODEL), D_MIX ** -0.5),
        'norm_ffn_gain': 1.0 + nrm(ks[13], (DEPTH, D_MODEL), 0.1),
        'w_gate_up': nrm(ks[14], (DEPTH, D_MODEL, 2 * D_FF), D_MODEL ** -0.5),
        'w_down': nrm(ks[15], (DEPTH, D_FF, D_MODEL), D_FF ** -0.5),
        'norm_final_gain': 1.0 + nrm(ks[16], (D_MODEL,), 0.1),
    }

def reference(x, c, w_ada, b_ada, norm_mix_gain, w_in, conv_w, a_log, dt_bias,
              gdn_norm_gain, w_pool, pool_scale, w_out, norm_ffn_gain, w_gate_up,
              w_down, norm_final_gain):
    out_dtype = x.dtype
    h = x.astype(jnp.float32)
    cond = jax.nn.silu(c.astype(jnp.float32))
    splits = [POOL_WIDTH, POOL_WIDTH + 3 * GDN_WIDTH, POOL_WIDTH + 4 * GDN_WIDTH,
              POOL_WIDTH + 4 * GDN_WIDTH + GDN_HEADS]
    for l in range(DEPTH):
        mod = cond @ w_ada[l] + b_ada[l]
        sh_m, sc_m, gt_m, sh_f, sc_f, gt_f = jnp.split(mod[:, None, :], N_MOD, axis=-1)
        hn = modulate(rms_norm(h, norm_mix_gain[l]), sh_m, sc_m)
        proj = hn @ w_in[l]
        u, qkv, z, b, a = jnp.split(proj, splits, axis=-1)
        y_pool = pool_mixer(u, w_pool[l], pool_scale[l])
        y_gdn = gated_deltanet_mixer(qkv, z, b, a, conv_w[l], a_log[l], dt_bias[l],
                                     gdn_norm_gain[l])
        mix = jnp.concatenate([y_pool, y_gdn], axis=-1) @ w_out[l]
        h = h + gt_m * mix
        hn = modulate(rms_norm(h, norm_ffn_gain[l]), sh_f, sc_f)
        gate, up = jnp.split(hn @ w_gate_up[l], 2, axis=-1)
        h = h + gt_f * ((jax.nn.silu(gate) * up) @ w_down[l])
    return rms_norm(h, norm_final_gain).astype(out_dtype)


_drawn_inputs = setup_inputs


def setup_inputs(seed=0):
    import zlib

    import numpy as np

    out = dict(_drawn_inputs(seed))
    spreads = {}
    factors = {'b_ada': 4.99, 'gdn_norm_gain': 3.075, 'pool_scale': 3.764}
    for name, (base, spread) in spreads.items():
        noise = np.random.default_rng([zlib.crc32(name.encode()), seed]).standard_normal(out[name].shape)
        drawn = base * np.exp(spread * noise) if base else spread * noise
        out[name] = __import__('jax').numpy.asarray(drawn.astype(out[name].dtype))
    for name, factor in factors.items():
        out[name] = (out[name] * factor).astype(out[name].dtype)
    return out
```

```python
import concourse.bass as bass
from concourse import mybir
from concourse.alu_op_type import AluOpType as ALU
from contextlib import ExitStack

F32 = mybir.dt.float32
F32R = mybir.dt.float32r
BF16 = mybir.dt.bfloat16
I16 = mybir.dt.int16
ACT = mybir.ActivationFunctionType
AX = mybir.AxisListType

P = 128
D_MODEL, SEQ = 1024, 1024
KT = D_MODEL // P
NC = SEQ // P
POOL_W, HEADS, HD = 256, 6, 128
GDN_W = HEADS * HD
CONV = 4
D_FF = 2816
FT = D_FF // P
IN_COLS = POOL_W + 4 * GDN_W + 2 * HEADS
EPS = 1e-6
PT = POOL_W // P
QKVT = 3 * GDN_W // P
ZT = GDN_W // P
G3 = 3
GW = G3 * P
HALF = 512
LEVELS = 7
PAD = 16
SMALL_A = 3 * KT + 6 * KT
CA_C, CA_GM, CA_GF, CA_B = 0, KT, 2 * KT, 3 * KT
CB_CONV, CB_PS, CB_GG = 0, CONV * QKVT, CONV * QKVT + PT
SMALL_B = CB_GG + 1
WINDOWS = (2, 4, 8, 16)
BA_COL = IN_COLS - P
BA_ROW = P - 2 * HEADS - 96
KB = 1024
SBUF_BASE, SBUF_END = 16512, 212832


def settled(eng, value):
    return value if isinstance(value, int) else eng.compute_val(value)


class Chain:

    def __init__(self, eng, sem):
        self.eng, self.sem, self.n, self.dyn, self.n0 = eng, sem, 0, 0, 0

    def link(self, ins):
        self.n += 1
        ins.then_inc(self.sem, 1)
        self.eng.wait_ge(self.sem, self.n + self.dyn)

    def enter(self, trip, per):
        self.n0, self.dyn = self.n, trip * per

    def leave(self, trips, per):
        assert self.n - self.n0 == per, (self.n - self.n0, per)
        self.n, self.dyn = self.n0 + trips * per, 0


def hybrid_block(nc, x, c, w_ada, b_ada, norm_mix_gain, w_in, conv_w, a_log, dt_bias, gdn_gain,
                 w_pool, pool_scale, w_out, norm_ffn_gain, w_gate_up, w_down, norm_final_gain,
                 out, qkvz_d, h2_d):
    x2, out2 = x[0], out[0]
    wada, win, wout, wgu, wdn = w_ada[0], w_in[0], w_out[0], w_gate_up[0], w_down[0]

    def at(name, off, free, dt=F32):
        return nc.alloc_sbuf_tensor_at(name, [P] + list(free), dt, offset=SBUF_BASE + off)

    off = [0]

    def small(name, free, dt=F32):
        n = 2 if dt == BF16 else 4
        for f in free:
            n *= f
        t = at(name, off[0], free, dt)
        off[0] += (n + 31) // 32 * 32
        assert off[0] <= 8 * KB + 512, off
        return t

    ident = small("ident", [P])
    tri = small("tri", [P])
    below = small("below", [P])
    ones = small("ones", [P])
    lmask = small("lmask", [LEVELS, P], BF16)
    cols_a = small("cols_a", [SMALL_A])
    cols_b = small("cols_b", [SMALL_B])
    mcol = small("mcol", [2 * KT])
    gcol = small("gcol", [KT])
    fcol = small("fcol", [2 * KT])
    gcol_f = small("gcol_f", [KT])
    ba = small("ba", [NC, 2 * HEADS])
    al_b = small("al_b", [HEADS])
    dt_b = small("dt_b", [HEADS])
    spt = small("spt", [3, NC, HEADS])
    NSC = 5
    S_BETA, S_G, S_EG, S_ED, S_EL = range(NSC)
    allsc = small("allsc", [NC, NSC, HEADS])
    sc = [small(f"sc{s}", [NSC, HEADS]) for s in range(2)]
    rr = [small(f"rr{s}", [2 * HEADS]) for s in range(2)]
    ssb = small("ssb", [2 * HEADS])
    nbk = small("nbk", [HEADS])
    kdec = small("kdec", [HEADS])
    rq2 = [small(f"rq2{s}", [HEADS]) for s in range(2)]
    sso = small("sso", [HEADS])
    oc = small("oc", [4, HEADS])
    ssx = small("ssx", [NC])
    rst = small("rst", [NC])
    ssx2 = small("ssx2", [2])
    rst2 = small("rst2", [2])
    mhalf = small("mhalf", [2 * HEADS])
    epsh = small("epsh", [HEADS])
    rcnt = small("rcnt", [PT, PAD])
    ssf = small("ssf", [2 * NC])

    B0 = 8 * KB + 512
    gate_m = at("gate_m", B0, [D_MODEL])
    gate_f = at("gate_f", B0 + 4 * KB, [D_MODEL])
    C0 = B0 + 8 * KB
    D0 = C0 + 64 * KB
    hn_hi = at("hn_hi", C0, [KT, SEQ], F32R)
    hn_f = at("hn_f", C0 + 32 * KB, [KT, SEQ])
    hn_lo = at("hn_lo", C0 + 32 * KB, [KT, SEQ], F32R)
    WS = 4
    w_raw = [at(f"w_raw{s}", D0 + 8 * KB * s, [KT, P]) for s in range(WS)]
    w_lo = [at(f"w_lo{s}", D0 + 8 * KB * s, [KT, P], F32R) for s in range(WS)]
    w_hi = [at(f"w_hi{s}", D0 + 8 * KB * s + 4 * KB, [KT, P], F32R) for s in range(WS)]
    ypool = at("ypool", D0 + 32 * KB, [PT, SEQ])
    E0 = D0 + 40 * KB
    SW = PAD + SEQ
    seqb = [at(f"seqb{s}", E0 + 4 * SW * s, [SW]) for s in range(2)]
    acc = [at(f"acc{s}", E0 + 4 * SW * (2 + s), [SW]) for s in range(2)]
    E1 = E0 + 16 * SW
    act_o = [at(f"act_o{s}", E1 + 4 * KB * s, [SEQ]) for s in range(2)]
    ada_w = [at(f"ada_w{s}", E1 + 8 * KB + 8 * KB * s, [2 * D_MODEL]) for s in range(2)]
    ada_acc = at("ada_acc", E1 + 24 * KB, [4 * D_MODEL])
    x_sl = [at(f"x_sl{t}", E1 + 40 * KB + 4 * KB * t if t < 5 else
               (E1 + 4 * KB * (t - 5) if t < 7 else D0 + 32 * KB), [D_MODEL]) for t in range(NC)]
    wpb = at("wpb", E1 + 60 * KB, [PT, P])
    rows_a = at("rows_a", E1 + 61 * KB, [P])
    rows_b = at("rows_b", E1 + 61 * KB + 512, [P])
    assert E1 + 62 * KB <= SBUF_END
    wo_hi = at("wo_hi", C0, [KT, D_MODEL], F32R)
    wo_raw = at("wo_raw", C0 + 32 * KB, [KT, D_MODEL])
    wo_lo = at("wo_lo", C0 + 32 * KB, [KT, D_MODEL], F32R)
    h2n_f = at("h2n_f", D0, [KT, SEQ])
    h2n_lo = at("h2n_lo", D0, [KT, SEQ], F32R)
    stage = [at(f"stage{s}", E0 + 12 * KB * s, [QKVT + ZT, P]) for s in range(2)]
    pos = [E0 + 24 * KB]

    def temp(name, free=(HEADS, P), dt=F32, alias=None):
        n = 4 * free[0] * free[1]
        o = pos[0] if alias is None else alias
        t = at(name, o, list(free), dt)
        if alias is None:
            pos[0] += n
        return t, o

    Tm, o_T = temp("Tm")
    Xm, o_X = temp("Xm")
    slg, _ = temp("slg", alias=o_T)
    kb, _ = temp("kb", alias=o_X)
    sqb, _ = temp("sqb", (2 * HEADS, P), alias=o_T)
    Em, _ = temp("Em")
    NA, _ = temp("NA")
    Um = [temp(f"Um{s}")[0] for s in range(2)]
    QD = [temp(f"QD{s}")[0] for s in range(2)]
    Kd = [temp(f"Kd{s}")[0] for s in range(2)]
    Vb = [temp(f"Vb{s}")[0] for s in range(2)]
    KbT = [temp(f"KbT{s}")[0] for s in range(2)]
    Sm, _ = temp("Sm")
    Rm, _ = temp("Rm")
    om, _ = temp("om")
    y_hi, o_yh = temp("y_hi", (KT, P), F32R)
    y_lo, o_yl = temp("y_lo", (KT, P), F32R)
    xn2, _ = temp("xn2", (KT, P), alias=o_yh)
    junk2, _ = temp("junk2", (KT, P), alias=o_yl)
    xt, _ = temp("xt", (KT, P))
    assert pos[0] <= SBUF_END
    h2n_hi = at("h2n_hi", C0, [KT, SEQ], F32R)
    u_raw = [at(f"u_raw{s}", C0 + 32 * KB + 8 * KB * s, [KT, P]) for s in range(WS)]
    u_lo = [at(f"u_lo{s}", C0 + 32 * KB + 8 * KB * s, [KT, P], F32R) for s in range(WS)]
    u_hi = [at(f"u_hi{s}", C0 + 36 * KB + 8 * KB * s, [KT, P], F32R) for s in range(WS)]
    hid = at("hid", D0 + 32 * KB, [FT, SEQ])
    assert D0 + 32 * KB + 88 * KB <= SBUF_END
    silu_t = at("silu_t", B0, [SEQ])
    DS = 4
    d_raw = [at(f"d_raw{s}", C0 + 12 * KB * s, [D_MODEL]) for s in range(DS)]
    d_lo = [at(f"d_lo{s}", C0 + 12 * KB * s, [D_MODEL], F32R) for s in range(DS)]
    d_hi = [at(f"d_hi{s}", C0 + 12 * KB * s + 4 * KB, [D_MODEL], F32R) for s in range(DS)]
    a_hi = [at(f"a_hi{s}", C0 + 12 * KB * s + 8 * KB, [HALF], F32R) for s in range(DS)]
    a_lo = [at(f"a_lo{s}", C0 + 12 * KB * s + 10 * KB, [HALF], F32R) for s in range(DS)]
    h_re = [at(f"h_re{s}", D0 + 4 * KB * s, [D_MODEL]) for s in range(4)]
    fin = [at(f"fin{s}", C0 + 48 * KB + 4 * KB * s, [D_MODEL]) for s in range(4)]
    fgain = at("fgain", D0 + 24 * KB, [D_MODEL])
    fjunk = at("fjunk", D0 + 28 * KB, [D_MODEL])

    ctx = ExitStack()
    with ctx:
        ps = ctx.enter_context(nc.psum_tensor("ps", [P, 8, HALF], F32))

        def sem(name):
            return ctx.enter_context(nc.semaphore(name))

        def bank2(b):
            return ps[:, b:b + 2, :].rearrange("p a n -> p (a n)")

        def grp(b):
            return ps[:, b, 0:GW]

        def grp3(b):
            return ps[:, b, 0:GW].rearrange("p (h n) -> p h n", h=G3)

        def bc(t, g):
            return t[:, G3 * g:G3 * g + G3].unsqueeze(2).to_broadcast([P, G3, P])

        def flat(t, g=None):
            v = t[:, :, :] if g is None else t[:, G3 * g:G3 * g + G3, :]
            return v.rearrange("p h n -> p (h n)")

        s_small = sem("small_loaded")
        s_x = sem("x_loaded")
        s_xsq = sem("x_tile_squared")
        s_h2sq = sem("h2_squared")
        s_fsq = sem("final_squared")
        s_xs = [sem(f"x_loaded{t}") for t in range(NC)]
        s_ada = [sem(f"ada_loaded{s}") for s in range(2)]
        s_w = [sem(f"w_in_loaded{s}") for s in range(WS)]
        s_wo = sem("w_out_loaded")
        s_const = sem("constants_ready")
        s_pool_chain = sem("pool_chain")
        s_dve_chain = sem("dve_chain")
        s_act_chain = sem("act_chain")
        s_rows_tr = sem("small_rows_transposed")
        s_cols = sem("small_columns_ready")
        s_cs = sem("c_silu_ready")
        s_ss = sem("x_square_sum_ready")
        s_rst = sem("x_rstd_ready")
        s_xn = sem("x_normalised")
        s_xtr = sem("x_transposed")
        s_xev = sem("x_transpose_evacuated")
        s_ada_used = sem("ada_piece_used")
        s_ada_mm = sem("ada_columns_summed")
        s_hf = sem("hn_modulated")
        s_hhi = sem("hn_hi_ready")
        s_hlo = sem("hn_lo_ready")
        s_wsplit = sem("w_in_split")
        s_proj = sem("projected")
        s_evac = sem("projection_evacuated")
        s_seq = sem("sequence_tile_used")
        s_conv = sem("conv_ready")
        s_aout = sem("activated_tile_ready")
        s_spill = [sem(f"tile_spilled{s}") for s in range(2)]
        s_batr = sem("ba_transposed")
        s_pmm = sem("pool_mixed")
        s_psq = sem("pool_squares_ready")
        s_pss = sem("pool_square_sums")
        s_pst = sem("pool_sum_ready")
        s_prs = sem("pool_rstd_ready")
        s_gmm = sem("gate_columns_summed")
        s_gev = sem("gate_columns_read")
        s_sp = sem("softplus_steps")
        s_spa = sem("softplus_activation")
        s_gmx = sem("decay_sums")
        s_ex = sem("decay_exponentials")
        s_scr = sem("scalars_ready")

        block = ctx.enter_context(nc.Block())

        s_stg = [sem(f"chunk_staged{s}") for s in range(2)]
        s_xin = sem("x_chunk_loaded")
        s_h2st = sem("h2_stored")
        (s_sq, s_ktr, s_vtr, s_ssr, s_rr, s_scc, s_vb, s_kbd, s_kdd, s_kbtr, s_kbT, s_slg, s_arg,
         s_exp, s_e, s_ti, s_kk, s_qk, s_na, s_qd, s_y, s_t, s_utr, s_u, s_xmm, s_xc) = [
            sem(n) for n in (
                "qk_squared", "k_transposed", "v_transposed", "square_sums_read", "norms_ready",
                "chunk_scalars_ready", "v_beta_ready", "k_beta_ready", "k_decay_ready",
                "kb_transposed", "kbT_ready", "decay_weights_ready", "decay_args", "decay_exp",
                "decay_ready", "inverse_init", "kk_products", "qk_products", "na_ready", "qd_ready",
                "level_product", "inverse_updated", "inverse_transposed", "u_ready",
                "level_x_product", "level_x_ready")]
        (s_s, s_ks, s_o1, s_r, s_o1c, s_vmm, s_v, s_o2, s_sd, s_o, s_sso, s_on, s_otr, s_yf,
         s_yhi, s_ylo, s_op, s_h2, s_ssx2, s_rst2, s_xn2, s_htr, s_h2n) = [
            sem(n) for n in (
                "state_ready", "k_state_product", "q_state_product", "rhs_ready", "o1_copied",
                "v_new_product", "v_new_ready", "o2_product", "state_delta", "o_ready",
                "o_square_sums", "o_normalised", "o_transposed", "y_ready", "y_hi_ready",
                "y_lo_ready", "mix_product", "h2_ready", "h2_square_sum", "h2_rstd",
                "h2_normalised", "h2_transposed", "h2_transpose_evacuated")]
        s_wosp = sem("w_out_split")
        s_wohi = sem("w_out_hi")
        s_u_ld = [sem(f"gate_up_loaded{s}") for s in range(WS)]
        s_uhi = sem("gate_up_hi")
        s_ulo = sem("gate_up_lo")
        s_f_hf = sem("ffn_modulated")
        s_f_hi = sem("ffn_hi_ready")
        s_f_lo = sem("ffn_lo_ready")
        s_gu = sem("gate_up_product")
        s_sil = sem("gate_activated")
        s_hid = sem("hidden_ready")
        s_d_ld = [sem(f"down_loaded{s}") for s in range(DS)]
        s_dhi = sem("down_hi")
        s_dlo = sem("down_lo")
        s_down = sem("down_step_done")
        s_dmm = sem("down_product")
        s_dev = sem("down_evacuated")
        s_hre = [sem(f"h2_reloaded{s}") for s in range(4)]
        s_fg = sem("final_gain_loaded")
        s_fh = sem("final_h_ready")
        s_fss = sem("final_square_sum")
        s_frs = sem("final_rstd")
        s_fin = sem("final_ready")
        s_out = sem("output_stored")

        def w_cols(t):
            return t * P if t < PT else (BA_COL if t == PT else (t - 1) * P)

        NT = PT + 1 + QKVT + ZT
        T0 = PT + 1
        spill3 = qkvz_d.rearrange("t p n -> p t n")

        @block.sync
        def _(sp):
            for r, (src, n) in enumerate(((c, KT), (norm_mix_gain, KT), (norm_ffn_gain, KT))):
                sp.dma_start(rows_a[r * KT:r * KT + n, :],
                             src.rearrange("o (r p) -> (o r) p", p=P)).then_inc(s_small, 16)
            sp.dma_start(rows_a[CA_B:SMALL_A, :],
                         b_ada.rearrange("o (r p) -> (o r) p", p=P)).then_inc(s_small, 16)
            sp.dma_start(rows_b[0:CB_PS, :],
                         conv_w.rearrange("o t (r p) -> (o t r) p", p=P)).then_inc(s_small, 16)
            sp.dma_start(rows_b[CB_PS:CB_GG, :],
                         pool_scale.rearrange("o (r p) -> (o r) p", p=P)).then_inc(s_small, 16)
            sp.dma_start(rows_b[CB_GG:SMALL_B, :], gdn_gain).then_inc(s_small, 16)
            for t in range(NC):
                sp.dma_start(x_sl[t][:, :], x2[t * P:(t + 1) * P, :]).then_inc(s_xs[t], 16)
            sp.dma_start(al_b[:, :], a_log.to_broadcast([P, HEADS])).then_inc(s_x, 16)
            sp.dma_start(dt_b[:, :], dt_bias.to_broadcast([P, HEADS])).then_inc(s_x, 16)
            sp.dma_start(gate_m[:, :], b_ada[:, 2 * D_MODEL:3 * D_MODEL].to_broadcast(
                [P, D_MODEL])).then_inc(s_x, 16)
            sp.dma_start(gate_f[:, :], b_ada[:, 5 * D_MODEL:6 * D_MODEL].to_broadcast(
                [P, D_MODEL])).then_inc(s_x, 16)
            for k in range(KT):
                if k >= 2:
                    sp.wait_ge(s_ada_used, k - 1)
                sp.dma_start(ada_w[k % 2][:, :],
                             wada[k * P:(k + 1) * P, 0:2 * D_MODEL]).then_inc(s_ada[k % 2], 16)
                if k == 1:
                    for t in range(4):
                        sp.dma_start(w_raw[t][:, :, :], win[:, w_cols(t):w_cols(t) + P].rearrange(
                            "(k p) n -> p k n", p=P)).then_inc(s_w[t], 16)
            sp.wait_ge(s_const, 2)
            for g in range(4):
                o = 64 * (g % 2)
                sp.dma_start(wpb[o:o + 64, g // 2, o:o + 64], w_pool[0, g]).then_inc(s_x, 16)
            with_loop = (NT - 4) // 4
            with sp.Fori(0, with_loop) as i:
                for j in range(4):
                    sp.wait_ge(s_proj, i * 4 + (j + 1))
                    sp.dma_start(w_raw[j][:, :, :],
                                 win[:, bass.ds(i * (4 * P) + (j + 3) * P, P)].rearrange(
                                     "(k p) n -> p k n", p=P)).then_inc(s_w[j], 16)
            for t in range(4 + 4 * with_loop, NT):
                sp.wait_ge(s_proj, t - 3)
                sp.dma_start(w_raw[t % 4][:, :, :], win[:, w_cols(t):w_cols(t) + P].rearrange(
                    "(k p) n -> p k n", p=P)).then_inc(s_w[t % 4], 16)
            sp.wait_ge(s_proj, NT)
            for s in range(2):
                sp.wait_ge(s_spill[s], 16 * (QKVT + ZT) // 2)
            sp.wait_ge(s_prs, 2)
            sp.wait_ge(s_gev, 2)

            def stage_load(cc, s):
                sp.dma_start(stage[s][:, :, :],
                             spill3[:, :, bass.ds(cc * P, P)]).then_inc(s_stg[s], 16)

            def x_load(cc):
                sp.dma_start(xt[:, :, :].rearrange("p k n -> p (k n)"),
                             x2[bass.ds(cc * P, P), :]).then_inc(s_xin, 16)

            def h2_store(cc):
                sp.wait_ge(s_h2, cc + 1)
                sp.dma_start(h2_d[bass.ds(cc * P, P), :],
                             xt[:, :, :].rearrange("p k n -> p (k n)")).then_inc(s_h2st, 16)

            stage_load(0, 0)
            sp.dma_start(wo_raw[:, :, :],
                         wout.rearrange("(k p) n -> p k n", p=P)).then_inc(s_wo, 16)
            stage_load(1, 1)
            x_load(0)

            def step(cc, s):
                sp.wait_ge(s_yf, cc * 2)
                if s is not None:
                    stage_load(cc + 1, s)
                h2_store(cc - 1)
                sp.wait_ge(s_h2st, cc * 16)
                sp.wait_ge(s_xn2, cc)
                x_load(cc)

            with sp.Fori(0, 3) as i:
                step(i * 2 + 1, 0)
                step(i * 2 + 2, 1)
            step(7, None)
            h2_store(7)

            def gu_load(f, s, up):
                sp.dma_start(u_raw[s][:, :, :], wgu[:, bass.ds(f * P + up * D_FF, P)].rearrange(
                    "(k p) n -> p k n", p=P)).then_inc(s_u_ld[s], 16)

            sp.wait_ge(s_op, NC)
            for f in range(2):
                for up in range(2):
                    gu_load(f, 2 * f + up, up)
            with sp.Fori(0, FT // 2 - 1) as i:
                for j in range(2):
                    sp.wait_ge(s_gu, i * 2 + (j + 1))
                    for up in range(2):
                        gu_load(i * 2 + (2 + j), 2 * j + up, up)

            def d_load(k, s):
                sp.dma_start(d_raw[s][:, :], wdn[bass.ds(k * P, P), :]).then_inc(s_d_ld[s], 16)

            sp.wait_ge(s_h2st, NC * 16)
            sp.wait_ge(s_gu, FT)
            for k in range(DS):
                d_load(k, k)
            sp.dma_start(fgain[:, :], norm_final_gain.unsqueeze(0).to_broadcast(
                [P, D_MODEL])).then_inc(s_fg, 16)
            for t in range(4):
                sp.dma_start(h_re[t][:, :], h2_d[t * P:(t + 1) * P, :]).then_inc(s_hre[t], 16)
            with sp.Fori(0, 4) as i:
                for j in range(4):
                    sp.wait_ge(s_down, i * 4 + (j + 1))
                    d_load(i * 4 + (j + 4), j)
            for n in (20, 21):
                sp.wait_ge(s_down, n - 3)
                d_load(n, n % 4)
            def second_pass(first, end):
                with sp.Fori(first, end) as i:
                    for j in range(4):
                        sp.wait_ge(s_down, i * 4 + (j + 19))
                        d_load(i * 4 + j, (j + 22) % 4)

            def store(t):
                sp.wait_ge(s_fin, t + 1)
                sp.dma_start(out2[t * P:(t + 1) * P, :], fin[t % 4][:, :]).then_inc(s_out, 16)

            second_pass(0, 2)
            for t in range(4):
                store(t)
                sp.dma_start(h_re[t][:, :],
                             h2_d[(4 + t) * P:(5 + t) * P, :]).then_inc(s_hre[t], 16)
            second_pass(2, 5)
            for n in (42, 43):
                sp.wait_ge(s_down, n - 3)
                d_load(n - 22, n % 4)
            for t in range(4, NC):
                store(t)
            sp.wait_ge(s_out, 16 * NC)

        @block.gpsimd
        def _(pool):
            g = nc.gpsimd
            ch = Chain(pool, s_pool_chain)
            ch.link(g.memset(ones[:, :], 1.0))
            one = ones[:, :]
            g.affine_select(out=ident[:, :], in_=one, compare_op=ALU.is_equal, fill=0.0, base=0,
                            pattern=[[1, P]], channel_multiplier=-1)
            ch.link(g.memset(mhalf[:, :], -0.5))
            g.memset(epsh[:, :], EPS * HD)
            g.affine_select(out=tri[:, :], in_=one, compare_op=ALU.is_ge, fill=0.0, base=0,
                            pattern=[[1, P]], channel_multiplier=-1)
            g.affine_select(out=below[:, :], in_=one, compare_op=ALU.is_gt, fill=0.0, base=0,
                            pattern=[[-1, P]], channel_multiplier=1).then_inc(s_const, 1)
            ch.link(g.memset(wpb[:, :, :], 0.0))
            for lv in range(LEVELS):
                b = 1 << lv
                m = lmask[:, lv, :].rearrange("p (a h r) -> p a h r", h=2, r=b)
                o = one.rearrange("p (a h r) -> p a h r", h=2, r=b)
                ch.link(g.affine_select(out=m, in_=o, compare_op=ALU.is_ge, fill=0.0, base=-b,
                                        pattern=[[-2 * b, P // (2 * b)], [-2 * P, 2], [0, b]],
                                        channel_multiplier=1))
                ch.link(g.affine_select(out=m, in_=m, compare_op=ALU.is_ge, fill=0.0,
                                        base=2 * b - 1,
                                        pattern=[[2 * b, P // (2 * b)], [0, 2], [0, b]],
                                        channel_multiplier=-1))
            for t in range(PT):
                for hf in range(2):
                    w = WINDOWS[2 * t + hf]
                    rows = slice(64 * hf, 64 * hf + 64)
                    for j in range(w - 1):
                        g.memset(rcnt[rows, t, j:j + 1], 1.0 / (j + 1))
                    ch.link(g.memset(rcnt[rows, t, w - 1:PAD], 1.0 / w))
            g.memset(seqb[0][:, 0:PAD], 0.0)
            g.memset(seqb[1][:, 0:PAD], 0.0).then_inc(s_const, 1)
            for t in range(NC):
                pool.wait_ge(s_ss, t + 1)
                g.tensor_tensor(rst[:, t:t + 1], ssx[:, t:t + 1], mhalf[:, 0:1],
                                ALU.pow).then_inc(s_rst, 1)

            def split(s, count):
                count = settled(pool, count)
                pool.wait_ge(s_const, 1)
                pool.wait_ge(s_w[s], count)
                ch.link(g.tensor_copy(w_hi[s][:, :, :], w_raw[s][:, :, :]))
                g.tensor_tensor(w_lo[s][:, :, :], w_raw[s][:, :, :],
                                w_hi[s][:, :, :].bitcast(F32), ALU.subtract).then_inc(s_wsplit, 1)

            for t in range(T0):
                split(t, 16)
            with pool.Fori(0, 6) as i:
                ch.enter(i, 4)
                for j in range(4):
                    split((3 + j) % 4, i * 16 + (16 if j == 0 else 32))
            ch.leave(6, 4)
            pool.wait_ge(s_pst, 1)
            g.tensor_tensor(ssf[:, NC:2 * NC], ssf[:, 0:NC], mhalf[:, 0:NC],
                            ALU.pow).then_inc(s_psq, 1)

            pool.wait_ge(s_scr, 1)

            def p_part(cc, s, first):
                pool.wait_ge(s_ssr, cc + 1)
                g.tensor_tensor(rr[s][:, :], ssb[:, :], mhalf[:, :], ALU.pow).then_inc(s_rr, 1)
                for gr in range(2):
                    g.tensor_tensor(slg[:, G3 * gr:G3 * gr + G3, :],
                                    below[:, :].unsqueeze(1).to_broadcast([P, G3, P]),
                                    bc(sc[s][:, S_G, :], gr), ALU.mult).then_inc(s_slg, 1)
                for gr in range(2):
                    count = settled(pool, cc * 2 + (gr + 1))
                    pool.wait_ge(s_const, 1)
                    pool.wait_ge(s_arg, count)
                    g.tensor_copy(Tm[:, G3 * gr:G3 * gr + G3, :],
                                  ident[:, :].unsqueeze(1).to_broadcast([P, G3, P])
                                  ).then_inc(s_ti, 1)
                for gr in range(2):
                    e = Em[:, G3 * gr:G3 * gr + G3, :]
                    pool.wait_ge(s_exp, cc * 2 + (gr + 1))
                    ch.link(g.tensor_tensor(e, e, tri[:, :].unsqueeze(1).to_broadcast(
                        [P, G3, P]), ALU.mult))
                    g.tensor_tensor(e, e, bc(rr[s][:, HEADS:], gr), ALU.mult).then_inc(s_e, 1)

            def r_part(cc, s):
                pool.wait_ge(s_sso, cc * 2 + 2)
                ch.link(g.tensor_tensor(oc[:, 0, :], sso[:, :], rq2[s][:, :], ALU.mult))
                ch.link(g.tensor_tensor(oc[:, 1, :], oc[:, 0, :], epsh[:, :], ALU.add))
                ch.link(g.tensor_tensor(oc[:, 2, :], oc[:, 1, :], mhalf[:, 0:HEADS], ALU.pow))
                ch.link(g.tensor_tensor(oc[:, 3, :], oc[:, 2, :], rr[s][:, 0:HEADS], ALU.mult))
                for gr in range(2):
                    o = om[:, G3 * gr:G3 * gr + G3, :]
                    g.tensor_tensor(o, o, bc(oc[:, 3, :], gr), ALU.mult).then_inc(s_on, 1)

            def r_tail(cc):
                pool.wait_ge(s_ssx2, cc + 1)
                g.tensor_tensor(rst2[:, 0:1], ssx2[:, 1:2], mhalf[:, 0:1],
                                ALU.pow).then_inc(s_rst2, 1)

            def body(cc, s):
                p_part(cc, s, False)
                r_part(cc - 1, 1 - s)
                r_tail(cc - 1)

            p_part(0, 0, True)
            PER = 2 * (2 + 4)
            with pool.Fori(0, 3) as i:
                ch.enter(i, PER)
                body(i * 2 + 1, 1)
                body(i * 2 + 2, 0)
            ch.leave(3, PER)
            body(7, 1)
            r_part(7, 1)
            r_tail(7)
            for t in range(NC):
                pool.wait_ge(s_fss, t + 1)
                g.tensor_tensor(ssf[:, NC + t:NC + t + 1], ssf[:, t:t + 1], mhalf[:, 0:1],
                                ALU.pow).then_inc(s_frs, 1)

        @block.scalar
        def _(act):
            a = nc.scalar
            ch = Chain(act, s_act_chain)
            act.wait_ge(s_cols, 1)
            a.activation(cols_a[:, CA_C:CA_C + KT], cols_a[:, CA_C:CA_C + KT],
                         ACT.Silu).then_inc(s_cs, 1)
            for t in range(NC):
                act.wait_ge(s_xs[t], 16)
                if t:
                    act.wait_ge(s_xsq, t)
                a.activation(bank2(4), x_sl[t][:, :], ACT.Square,
                             accum_out=ssx[:, t:t + 1]).then_inc(s_xsq, 1)
            for t in range(NC):
                act.wait_ge(s_xtr, t + 1)
                a.activation(hn_f[:, :, t * P:(t + 1) * P],
                             bank2(2 * (t % 2)).rearrange("p (k n) -> p k n", k=KT),
                             ACT.Copy).then_inc(s_xev, 1)
            for k in range(KT):
                act.wait_ge(s_hf, k + 1)
                a.activation(hn_hi[:, k, :], hn_f[:, k, :], ACT.Copy).then_inc(s_hhi, 1)

            def evac(t, slot, used):
                act.wait_ge(s_proj, t + 1)
                if used is not None:
                    act.wait_ge(*used)
                a.activation(seqb[slot][:, PAD:], bank2(2 * slot), ACT.Copy).then_inc(s_evac, 1)

            evac(0, 0, None)
            evac(1, 1, None)
            act.wait_ge(s_proj, 3)
            act.wait_ge(s_seq, 1)
            a.activation(seqb[0][0:32, PAD:], bank2(0)[96:128, :], ACT.Copy).then_inc(s_evac, 1)

            def ada_load(k):
                for s in range(2):
                    act.wait_ge(s_ada_used, k * 2 + (KT - 1 + s))
                    act.dma_start(ada_w[s][:, :],
                                  wada[bass.ds(k * P, P), (2 + 2 * s) * D_MODEL:
                                       (4 + 2 * s) * D_MODEL]).then_inc(s_ada[s], 16)

            def spill(n, slot):
                act.dma_start(qkvz_d[bass.ds(n, 1), :, :].rearrange("a p n -> p (a n)"),
                              act_o[slot][:, :]).then_inc(s_spill[slot], 16)

            def qkv(n, guard_spill):
                t = n + T0
                slot = qkv.slot
                evac(t, slot, (s_seq, n + PT) if isinstance(n, int) and n < 2 else
                     (s_conv, n - 1))
                act.wait_ge(s_conv, n + 1)
                if guard_spill is not None:
                    act.wait_ge(s_spill[1 - slot], guard_spill)
                a.activation(act_o[1 - slot][:, :], acc[1 - slot][:, 0:SEQ],
                             ACT.Silu).then_inc(s_aout, 1)
                act.wait_ge(s_aout, n + 1)
                spill(n, 1 - slot)

            ada_load(0)
            for n in range(2):
                qkv.slot = (n + 1) % 2
                qkv(n, None)
            with act.Fori(1, 8) as i:
                ada_load(i)
                for j in range(2):
                    qkv.slot = (j + 1) % 2
                    qkv(i * 2 + j, i * 16)
            for n in range(16, 18):
                qkv.slot = (n + 1) % 2
                qkv(n, (n // 2) * 16)
            with act.Fori(0, 3) as i:
                for j in range(2):
                    n = i * 2 + (j + QKVT)
                    slot = (j + 1) % 2
                    act.wait_ge(s_proj, i * 2 + (j + QKVT + T0 + 1))
                    act.wait_ge(s_spill[1 - slot], i * 16 + 16 * QKVT // 2)
                    a.activation(act_o[1 - slot][:, :], bank2(2 * slot),
                                 ACT.Silu).then_inc(s_evac, 1)
                    act.wait_ge(s_evac, i * 2 + (j + QKVT + T0 + 1))
                    spill(n, 1 - slot)
            act.wait_ge(s_pmm, 1)
            act.wait_ge(s_conv, QKVT)
            for t in range(PT):
                ch.link(a.activation(ypool[:, t, :], bank2(4 + 2 * t), ACT.Copy))
                a.activation(seqb[t][:, PAD:], ypool[:, t, :], ACT.Square).then_inc(s_pss, 1)
            act.wait_ge(s_sp, 1)
            a.activation(spt[:, 0, :, :], spt[:, 0, :, :], ACT.Exp, scale=-1.0).then_inc(s_spa, 1)
            a.activation(allsc[:, :, S_BETA, :], ba[:, :, 0:HEADS], ACT.Exp,
                         scale=-1.0).then_inc(s_spa, 1)
            act.wait_ge(s_x, 128)
            a.activation(al_b[:, :], al_b[:, :], ACT.Exp).then_inc(s_spa, 1)
            act.wait_ge(s_sp, 2)
            a.activation(spt[:, 0, :, :], spt[:, 0, :, :], ACT.Ln).then_inc(s_spa, 1)
            act.wait_ge(s_gmx, 1)
            n48 = NC * HEADS
            a.activation(allsc[:, :, S_EG, :], ps[:, 0, 0:n48].rearrange(
                "p (c h) -> p c h", h=HEADS), ACT.Exp)
            a.activation(allsc[:, :, S_ED, :], ps[:, 0, n48:2 * n48].rearrange(
                "p (c h) -> p c h", h=HEADS), ACT.Exp)
            a.activation(allsc[:, :, S_EL, :], ps[:, 0, 2 * n48:3 * n48].rearrange(
                "p (c h) -> p c h", h=HEADS), ACT.Exp).then_inc(s_ex, 1)

            def squares(cc, s, dma):
                act.wait_ge(s_stg[s], dma)
                if cc is not None:
                    act.wait_ge(s_u, cc * (2 * LEVELS))
                a.activation(flat(sqb), stage[s][:, 0:2 * HEADS, :].rearrange(
                    "p h n -> p (h n)"), ACT.Square).then_inc(s_sq, 1)

            def p_kbT(cc, s):
                for gr in range(2):
                    act.wait_ge(s_kbtr, cc * 2 + (gr + 1))
                    a.activation(flat(KbT[s], gr), grp(2 * gr), ACT.Copy).then_inc(s_kbT, 1)

            def p_exp(cc, guard):
                for gr in range(2):
                    act.wait_ge(s_arg, cc * 2 + (gr + 1))
                    if guard:
                        act.wait_ge(s_qd, cc * 2)
                    a.activation(flat(Em, gr), grp(2 * gr + 1), ACT.Exp).then_inc(s_exp, 1)

            def level_u(cc, s, lv):
                for gr in range(2):
                    act.wait_ge(s_utr, cc * (2 * LEVELS) + (2 * lv + gr + 1))
                    a.activation(flat(Um[s], gr), grp(2 * gr), ACT.Copy).then_inc(s_u, 1)

            def level_x(cc, lv):
                for gr in range(2):
                    act.wait_ge(s_xmm, cc * (2 * LEVELS - 2) + (2 * (lv - 1) + gr + 1))
                    a.activation(flat(Xm, gr), grp(2 * gr), ACT.Copy).then_inc(s_xc, 1)

            def r_o1(cc, guard):
                for gr in range(2):
                    act.wait_ge(s_o1, cc * 2 + (gr + 1))
                    if guard:
                        act.wait_ge(s_ylo, cc * 2)
                    a.activation(flat(om, gr), grp(5 + 2 * gr), ACT.Copy).then_inc(s_o1c, 1)

            def r_v(cc):
                for gr in range(2):
                    act.wait_ge(s_vmm, cc * 2 + (gr + 1))
                    a.activation(flat(Rm, gr), grp(4 + 2 * gr), ACT.Copy).then_inc(s_v, 1)

            def r_sso(cc):
                for gr in range(2):
                    act.wait_ge(s_o, cc * 2 + (gr + 1))
                    for h in range(G3 * gr, G3 * gr + G3):
                        last = a.activation(junk2[:, h, :], om[:, h, :], ACT.Square,
                                            accum_out=sso[:, h:h + 1])
                    last.then_inc(s_sso, 1)

            def r_yhi(cc):
                a.activation(y_hi[:, 0:PT, :], ypool[:, :, bass.ds(cc * P, P)],
                             ACT.Copy).then_inc(s_yhi, 1)
                for gr in range(2):
                    act.wait_ge(s_yf, cc * 2 + (gr + 1))
                    a.activation(y_hi[:, PT + G3 * gr:PT + G3 * gr + G3, :],
                                 om[:, G3 * gr:G3 * gr + G3, :], ACT.Copy).then_inc(s_yhi, 1)

            def r_ssx(cc):
                act.wait_ge(s_h2, cc + 1)
                a.activation(flat(junk2), flat(xt), ACT.Square,
                             accum_out=ssx2[:, 0:1]).then_inc(s_h2sq, 1)

            def r_h2n(cc):
                for h in range(2):
                    act.wait_ge(s_htr, cc * 2 + (h + 1))
                    a.activation(h2n_f[:, 4 * h:4 * h + 4, bass.ds(cc * P, P)],
                                 ps[:, 4 + 2 * h, :].rearrange("p (k n) -> p k n", k=4),
                                 ACT.Copy).then_inc(s_h2n, 1)

            def body(cc, s, dma):
                squares(cc, s, dma)
                r_o1(cc - 1, not (isinstance(cc, int) and cc == 1))
                p_kbT(cc, s)
                p_exp(cc, True)
                r_v(cc - 1)
                level_u(cc, s, 0)
                r_sso(cc - 1)
                for lv in range(1, LEVELS):
                    level_x(cc, lv)
                    level_u(cc, s, lv)
                    if lv == 2:
                        r_yhi(cc - 1)
                r_ssx(cc - 1)
                r_h2n(cc - 1)

            def wo_hi_copy(k):
                a.activation(wo_hi[:, k, :], wo_raw[:, k, :], ACT.Copy).then_inc(s_wohi, 1)

            squares(None, 0, 16)
            p_kbT(0, 0)
            p_exp(0, False)
            level_u(0, 0, 0)
            act.wait_ge(s_wo, 16)
            for lv in range(1, LEVELS):
                level_x(0, lv)
                for k in ((0, 1) if lv == 1 else (lv,)):
                    wo_hi_copy(k)
                level_u(0, 0, lv)
            wo_hi_copy(KT - 1)
            body(1, 1, 16)
            body(2, 0, 32)
            with act.Fori(1, 3) as i:
                body(i * 2 + 1, 1, i * 16 + 16)
                body(i * 2 + 2, 0, i * 16 + 32)
            body(7, 1, 64)
            r_o1(7, True)
            r_v(7)
            r_sso(7)
            r_yhi(7)
            r_ssx(7)
            r_h2n(7)

            def f_hi(k):
                act.wait_ge(s_f_hf, k + 1)
                a.activation(h2n_hi[:, k, :], h2n_f[:, k, :], ACT.Copy).then_inc(s_f_hi, 1)

            def u_hi_copy(s, dma):
                act.wait_ge(s_u_ld[s], dma)
                a.activation(u_hi[s][:, :, :], u_raw[s][:, :, :], ACT.Copy).then_inc(s_uhi, 1)

            u_hi_copy(0, 16)
            u_hi_copy(1, 16)
            for k in range(KT):
                f_hi(k)
            u_hi_copy(2, 16)
            u_hi_copy(3, 16)

            def silu(f, guard):
                act.wait_ge(s_gu, f + 1)
                if guard:
                    act.wait_ge(s_hid, f)
                a.activation(silu_t[:, :], bank2(silu.b), ACT.Silu).then_inc(s_sil, 1)

            silu.b = 0
            act.wait_ge(s_h2, NC)
            silu(0, False)
            u_hi_copy(0, 32)
            u_hi_copy(1, 32)
            silu.b = 4
            silu(1, True)
            u_hi_copy(2, 32)
            u_hi_copy(3, 32)
            with act.Fori(1, FT // 2 - 1) as i:
                silu.b = 0
                silu(i * 2, True)
                u_hi_copy(0, i * 16 + 32)
                u_hi_copy(1, i * 16 + 32)
                silu.b = 4
                silu(i * 2 + 1, True)
                u_hi_copy(2, i * 16 + 32)
                u_hi_copy(3, i * 16 + 32)
            silu.b = 0
            silu(FT - 2, True)
            silu.b = 4
            silu(FT - 1, True)

            def d_hi_copy(k, h, s, dma, used):
                act.wait_ge(s_d_ld[s], dma)
                if used is not None:
                    act.wait_ge(s_down, used)
                a.activation(d_hi[s][:, :], d_raw[s][:, :], ACT.Copy)
                a.activation(a_hi[s][:, :], hid[:, bass.ds(k, 1), h * HALF:(h + 1) * HALF].rearrange(
                    "p a n -> p (a n)"), ACT.Copy).then_inc(s_dhi, 1)

            act.wait_ge(s_hid, FT)
            act.wait_ge(s_gu, FT)
            for n in range(4):
                d_hi_copy(n, 0, n, 16, None)
            with act.Fori(1, 5) as i:
                for j in range(4):
                    d_hi_copy(i * 4 + j, 0, j, i * 16 + 16, i * 4 + (j - 3))
            for n in range(20, 24):
                d_hi_copy(n % FT, n // FT, n % 4, 16 * (n // 4 + 1), n - 3)

            def out_sq(t):
                act.wait_ge(s_fh, t + 1)
                a.activation(fjunk[:, :], h_re[t % 4][:, :], ACT.Square,
                             accum_out=ssf[:, t:t + 1]).then_inc(s_fsq, 1)

            for n in range(24, 28):
                d_hi_copy(n - FT, 1, n % 4, 16 * (n // 4 + 1), n - 3)
            for t in range(4):
                if t > 0:
                    act.wait_ge(s_fsq, t)
                out_sq(t)
            with act.Fori(7, 11) as i:
                for j in range(4):
                    d_hi_copy(i * 4 + (j - 22), 1, j, i * 16 + 16, i * 4 + (j - 3))
            for t in range(4, 8):
                act.wait_ge(s_fsq, t)
                out_sq(t)

        @block.vector
        def _(dve):
            v = nc.vector
            ch = Chain(dve, s_dve_chain)
            dve.wait_ge(s_rows_tr, 1)
            v.tensor_copy(cols_a[:, :], ps[:, 6, 0:SMALL_A])
            v.tensor_copy(cols_b[:, :], ps[:, 6, P:P + SMALL_B]).then_inc(s_cols, 1)
            for t in range(NC):
                dve.wait_ge(s_xsq, t + 1)
                v.tensor_scalar(ssx[:, t:t + 1], ssx[:, t:t + 1], 1.0 / D_MODEL, EPS,
                                ALU.mult, ALU.add).then_inc(s_ss, 1)
                dve.wait_ge(s_rst, t + 1)
                v.tensor_scalar(x_sl[t][:, :], x_sl[t][:, :], rst[:, t:t + 1], None,
                                ALU.mult).then_inc(s_xn, 1)
            dve.wait_ge(s_cs, 1)
            for k in range(KT):
                dve.wait_ge(s_ada[k % 2], 16 * (k // 2 + 1))
                ccol = cols_a[:, CA_C + k:CA_C + k + 1]
                if k == 0:
                    v.tensor_scalar(ada_acc[:, 0:2 * D_MODEL], ada_w[0][:, :], ccol, None,
                                    ALU.mult).then_inc(s_ada_used, 1)
                else:
                    dve.wait_ge(s_ada_used, k)
                    v.scalar_tensor_tensor(out=ada_acc[:, 0:2 * D_MODEL], in0=ada_w[k % 2][:, :],
                                           scalar=ccol, in1=ada_acc[:, 0:2 * D_MODEL],
                                           op0=ALU.mult, op1=ALU.add).then_inc(s_ada_used, 1)

            def modulation(mc, gc, base, gain, waitv):
                dve.wait_ge(s_ada_mm, waitv)
                ch.link(v.tensor_tensor(mc[:, :], ps[:, 7, 0:2 * KT],
                                        cols_a[:, CA_B + base:CA_B + base + 2 * KT], ALU.add))
                ch.link(v.scalar_tensor_tensor(out=gc[:, :], in0=mc[:, KT:2 * KT], scalar=1.0,
                                               in1=cols_a[:, gain:gain + KT], op0=ALU.add,
                                               op1=ALU.mult))

            def modulate(hf, hl, hh, mc, gc, s_f, s_h, s_l):
                for k in range(KT + 1):
                    if k < KT:
                        v.tensor_scalar(hf[:, k, :], hf[:, k, :], gc[:, k:k + 1], mc[:, k:k + 1],
                                        ALU.mult, ALU.add).then_inc(s_f, 1)
                    if k > 0:
                        dve.wait_ge(s_h, k)
                        v.tensor_tensor(hl[:, k - 1, :], hf[:, k - 1, :],
                                        hh[:, k - 1, :].bitcast(F32),
                                        ALU.subtract).then_inc(s_l, 1)

            modulation(mcol, gcol, 0, CA_GM, 1)
            dve.wait_ge(s_xev, NC)
            modulate(hn_f, hn_lo, hn_hi, mcol, gcol, s_hf, s_hhi, s_hlo)

            dve.wait_ge(s_const, 2)
            for t in range(PT):
                dve.wait_ge(s_evac, t + 1)
                u = seqb[t]
                cur = u
                rows = slice(0, P)
                done = {}
                for n, sh in enumerate((1, 2) if t == 0 else (1, 2, 4, 8)):
                    dst = acc[n % 2]
                    w = 2 * sh
                    r = rows if w <= WINDOWS[2 * t] else slice(64, P)
                    lo = w - 1
                    ch.link(v.tensor_tensor(dst[r, lo:SW], cur[r, lo:SW], cur[r, lo - sh:SW - sh],
                                            ALU.add))
                    cur = dst
                    for hf in range(2):
                        if WINDOWS[2 * t + hf] == w:
                            done[hf] = dst
                for hf in range(2):
                    w = WINDOWS[2 * t + hf]
                    r = slice(64 * hf, 64 * hf + 64)
                    s_ = done[hf]
                    v.scalar_tensor_tensor(out=ypool[r, t, PAD:SEQ], in0=s_[r, 2 * PAD:SW],
                                           scalar=1.0 / w, in1=u[r, 2 * PAD:SW], op0=ALU.mult,
                                           op1=ALU.subtract)
                    ch.link(v.tensor_tensor(ypool[r, t, 0:PAD], s_[r, PAD:2 * PAD],
                                            rcnt[r, t, :], ALU.mult))
                    last = v.tensor_tensor(ypool[r, t, 0:PAD], ypool[r, t, 0:PAD],
                                           u[r, PAD:2 * PAD], ALU.subtract)
                    if hf == 0:
                        ch.link(last)
                last.then_inc(s_seq, 1)
            dve.wait_ge(s_batr, 1)
            v.tensor_copy(ba[:, :, :], ps[:, 6, 0:32 * NC].rearrange(
                "p (c r) -> p c r", r=32)[:, :, BA_ROW:BA_ROW + 2 * HEADS]).then_inc(s_seq, 1)

            def conv(n, dyn):
                slot, o = (n + 1) % 2, n % 2
                t = dyn + (T0 + 1)
                dve.wait_ge(s_evac, t)
                if conv.guard is not None:
                    dve.wait_ge(s_aout, conv.guard)
                src, dst = seqb[slot], acc[o]

                cb = cols_b
                for j in (3, 2, 1, 0):
                    col = cb[:, bass.ds(dyn + j * QKVT, 1)]
                    s_ = src[:, PAD - 3 + j:PAD - 3 + j + SEQ]
                    if j == 3:
                        ch.link(v.tensor_scalar(dst[:, 0:SEQ], s_, col, None, ALU.mult))
                    else:
                        last = v.scalar_tensor_tensor(out=dst[:, 0:SEQ], in0=s_, scalar=col,
                                                      in1=dst[:, 0:SEQ], op0=ALU.mult,
                                                      op1=ALU.add)
                        if j > 0:
                            ch.link(last)
                last.then_inc(s_conv, 1)

            def ada_rest(k, first):
                ccol = cols_a[:, bass.ds(k + CA_C, 1)]
                for s in range(2):
                    dst = ada_acc[:, 2 * s * D_MODEL:2 * (s + 1) * D_MODEL]
                    dve.wait_ge(s_ada[s], k * 16 + 80)
                    if first:
                        v.tensor_scalar(dst, ada_w[s][:, :], ccol, None,
                                        ALU.mult).then_inc(s_ada_used, 1)
                    else:
                        dve.wait_ge(s_ada_used, k * 2 + (KT - 1 + s))
                        v.scalar_tensor_tensor(out=dst, in0=ada_w[s][:, :], scalar=ccol, in1=dst,
                                               op0=ALU.mult, op1=ALU.add).then_inc(s_ada_used, 1)

            for n in range(2):
                conv.guard = None
                conv(n, n)
            ada_rest(0, True)
            with dve.Fori(1, 8) as i:
                ch.enter(i - 1, 6)
                for j in range(2):
                    conv.guard = i * 2 + (j - 1)
                    conv(j, i * 2 + j)
                ada_rest(i, False)
            ch.leave(7, 6)
            for n in (16, 17):
                conv.guard = n - 1
                conv(n, n)
            modulation(fcol, gcol_f, 3 * KT, CA_GF, 2)
            dve.wait_ge(s_x, 128)
            for gt, gate in enumerate((gate_m, gate_f)):
                dve.wait_ge(s_gmm, gt + 1)
                v.tensor_tensor(gate[:, :], gate[:, :], bank2(4), ALU.add).then_inc(s_gev, 1)
            aa = ba[:, :, HEADS:2 * HEADS]
            ch.link(v.tensor_tensor(spt[:, 1, :, :], aa,
                                    dt_b[:, :].unsqueeze(1).to_broadcast([P, NC, HEADS]), ALU.add))
            ch.link(v.tensor_scalar(spt[:, 2, :, :], spt[:, 1, :, :], -1.0, None, ALU.mult))
            v.tensor_tensor(spt[:, 0, :, :], spt[:, 1, :, :], spt[:, 2, :, :],
                            ALU.max).then_inc(s_sp, 1)
            dve.wait_ge(s_spa, 3)
            ch.link(v.tensor_scalar(allsc[:, :, S_BETA, :], allsc[:, :, S_BETA, :], 1.0, None,
                                    ALU.add))
            ch.link(v.reciprocal(allsc[:, :, S_BETA, :], allsc[:, :, S_BETA, :]))
            v.tensor_scalar(spt[:, 0, :, :], spt[:, 0, :, :], 1.0, None, ALU.add).then_inc(s_sp, 1)
            ch.link(v.tensor_scalar(spt[:, 1, :, :], spt[:, 1, :, :], 0.0, None, ALU.max))
            dve.wait_ge(s_spa, 4)
            ch.link(v.tensor_tensor(spt[:, 2, :, :], spt[:, 1, :, :], spt[:, 0, :, :], ALU.add))
            ch.link(v.tensor_tensor(spt[:, 1, :, :], spt[:, 2, :, :],
                                    al_b[:, :].unsqueeze(1).to_broadcast([P, NC, HEADS]),
                                    ALU.mult))
            ch.link(v.tensor_scalar(spt[:, 0, :, :], spt[:, 1, :, :], -1.0, None, ALU.mult))
            v.tensor_copy(allsc[:, :, S_G, :], spt[:, 0, :, :]).then_inc(s_sp, 1)
            dve.wait_ge(s_pmm, 2)
            v.tensor_scalar(ssf[:, 0:NC], ps[:, 4, 0:NC], 1.0 / POOL_W, EPS, ALU.mult,
                            ALU.add).then_inc(s_pst, 1)
            dve.wait_ge(s_pmm, 3)
            for t in range(PT):
                last = v.scalar_tensor_tensor(out=ypool[:, t, :], in0=ypool[:, t, :],
                                              scalar=cols_b[:, CB_PS + t:CB_PS + t + 1],
                                              in1=bank2(6), op0=ALU.mult, op1=ALU.mult)
                last.then_inc(s_prs, 1)
            dve.wait_ge(s_ex, 1)
            v.memset(Sm[:, :, :], 0.0).then_inc(s_scr, 1)

            def p_head(cc, s):
                dve.wait_ge(s_vtr, cc * 2 + 2)
                ch.link(v.tensor_copy(sc[s][:, :, :], allsc[:, bass.ds(cc, 1), :, :].rearrange(
                    "p a b h -> p (a b) h")))
                v.tensor_scalar(ssb[:, :], ps[:, 3, GW:GW + 2 * HEADS], EPS, None,
                                ALU.add).then_inc(s_ssr, 1)
                for gr in range(2):
                    v.tensor_tensor(Vb[s][:, G3 * gr:G3 * gr + G3, :], grp3(2 * gr + 1),
                                    bc(sc[s][:, S_BETA, :], gr), ALU.mult).then_inc(s_vb, 1)

            def p_k(cc, s):
                dve.wait_ge(s_rr, cc + 1)
                rk = rr[s][:, HEADS:2 * HEADS]
                rq = rr[s][:, 0:HEADS]
                v.scalar_tensor_tensor(out=nbk[:, :], in0=rk, scalar=-1.0,
                                       in1=sc[s][:, S_BETA, :], op0=ALU.mult, op1=ALU.mult)
                v.scalar_tensor_tensor(out=rq2[s][:, :], in0=rq,
                                       scalar=1.0 / HD, in1=rq, op0=ALU.mult, op1=ALU.mult)
                ch.link(v.tensor_tensor(kdec[:, :], rk, sc[s][:, S_ED, :], ALU.mult))
                for gr in range(2):
                    v.tensor_tensor(kb[:, G3 * gr:G3 * gr + G3, :], grp3(2 * gr), bc(nbk, gr),
                                    ALU.mult)
                    v.tensor_tensor(Kd[s][:, G3 * gr:G3 * gr + G3, :], grp3(2 * gr),
                                    bc(kdec, gr), ALU.mult).then_inc(s_kdd, 1)

            def p_na(cc, s):
                for gr in range(2):
                    dve.wait_ge(s_kk, cc * 2 + (gr + 1))
                    dve.wait_ge(s_e, cc * 2 + (gr + 1))
                    v.tensor_tensor(flat(NA, gr), grp(2 * gr), flat(Em, gr),
                                    ALU.mult).then_inc(s_na, 1)
                for gr in range(2):
                    dve.wait_ge(s_qk, cc * 2 + (gr + 1))
                    v.tensor_tensor(flat(QD[s], gr), grp(2 * gr + 1), flat(Em, gr),
                                    ALU.mult).then_inc(s_qd, 1)

            def level_t(cc, lv):
                for gr in range(2):
                    count = settled(dve, cc * (2 * LEVELS) + (2 * lv + gr + 1))
                    dve.wait_ge(s_const, 2)
                    dve.wait_ge(s_y, count)
                    if lv == 0:
                        dve.wait_ge(s_ti, cc * 2 + (gr + 1))
                    v.copy_predicated(Tm[:, G3 * gr:G3 * gr + G3, :],
                                      lmask[:, lv, :].bitcast(I16).unsqueeze(1).to_broadcast(
                                          [P, G3, P]), grp3(2 * gr + 1)).then_inc(s_t, 1)

            def r_rhs(cc, s):
                for gr in range(2):
                    dve.wait_ge(s_ks, cc * 2 + (gr + 1))
                    for n in range(G3):
                        h = G3 * gr + n
                        last = v.scalar_tensor_tensor(
                            out=Rm[:, h, :], in0=ps[:, 4 + 2 * gr, n * P:(n + 1) * P],
                            scalar=sc[s][:, S_EG, h:h + 1], in1=Vb[s][:, h, :],
                            op0=ALU.mult, op1=ALU.add)
                    last.then_inc(s_r, 1)

            def r_state(cc, s):
                for gr in range(2):
                    dve.wait_ge(s_sd, cc * 2 + (gr + 1))
                    for n in range(G3):
                        h = G3 * gr + n
                        last = v.scalar_tensor_tensor(
                            out=Sm[:, h, :], in0=Sm[:, h, :], scalar=sc[s][:, S_EL, h:h + 1],
                            in1=ps[:, 4 + 2 * gr, n * P:(n + 1) * P], op0=ALU.mult, op1=ALU.add)
                    last.then_inc(s_s, 1)
                for gr in range(2):
                    dve.wait_ge(s_o2, cc * 2 + (gr + 1))
                    for n in range(G3):
                        h = G3 * gr + n
                        last = v.scalar_tensor_tensor(
                            out=om[:, h, :], in0=om[:, h, :], scalar=sc[s][:, S_EG, h:h + 1],
                            in1=ps[:, 5 + 2 * gr, n * P:(n + 1) * P], op0=ALU.mult, op1=ALU.add)
                    last.then_inc(s_o, 1)

            def r_y(cc, s):
                for gr in range(2):
                    dve.wait_ge(s_otr, cc * 2 + (gr + 1))
                    z = stage[s][:, QKVT + G3 * gr:QKVT + G3 * gr + G3, :].rearrange(
                        "p h n -> p (h n)")
                    v.scalar_tensor_tensor(out=flat(om, gr), in0=grp(5 + 2 * gr),
                                           scalar=cols_b[:, CB_GG:CB_GG + 1], in1=z,
                                           op0=ALU.mult, op1=ALU.mult).then_inc(s_yf, 1)
                dve.wait_ge(s_yhi, cc * 3 + 1)
                v.tensor_tensor(y_lo[:, 0:PT, :], ypool[:, :, bass.ds(cc * P, P)],
                                y_hi[:, 0:PT, :].bitcast(F32), ALU.subtract)
                for gr in range(2):
                    dve.wait_ge(s_yhi, cc * 3 + (gr + 2))
                    r = slice(PT + G3 * gr, PT + G3 * gr + G3)
                    v.tensor_tensor(y_lo[:, r, :], om[:, G3 * gr:G3 * gr + G3, :],
                                    y_hi[:, r, :].bitcast(F32), ALU.subtract).then_inc(s_ylo, 1)

            def r_h2(cc):
                dve.wait_ge(s_op, cc + 1)
                x_ = flat(xt)
                t_ = flat(xn2)
                v.tensor_tensor(t_[:, 0:HALF], ps[:, 4, :], gate_m[:, 0:HALF], ALU.mult)
                ch.link(v.tensor_tensor(t_[:, HALF:], ps[:, 6, :], gate_m[:, HALF:], ALU.mult))
                dve.wait_ge(s_xin, cc * 16 + 16)
                v.tensor_tensor(x_, x_, t_, ALU.add).then_inc(s_h2, 1)

            def r_xn(cc):
                dve.wait_ge(s_h2sq, cc + 1)
                v.tensor_scalar(ssx2[:, 1:2], ssx2[:, 0:1], 1.0 / D_MODEL, EPS, ALU.mult,
                                ALU.add).then_inc(s_ssx2, 1)
                dve.wait_ge(s_rst2, cc + 1)
                v.tensor_scalar(flat(xn2), flat(xt), rst2[:, 0:1], None,
                                ALU.mult).then_inc(s_xn2, 1)

            def body(cc, s):
                p_head(cc, s)
                r_rhs(cc - 1, 1 - s)
                p_k(cc, s)
                p_na(cc, s)
                r_state(cc - 1, 1 - s)
                level_t(cc, 0)
                level_t(cc, 1)
                level_t(cc, 2)
                r_y(cc - 1, 1 - s)
                for lv in range(3, 7):
                    level_t(cc, lv)
                r_h2(cc - 1)
                r_xn(cc - 1)

            def wo_lo_sub(k):
                dve.wait_ge(s_wohi, k + 1)
                v.tensor_tensor(wo_lo[:, k, :], wo_raw[:, k, :], wo_hi[:, k, :].bitcast(F32),
                                ALU.subtract).then_inc(s_wosp, 1)

            p_head(0, 0)
            p_k(0, 0)
            p_na(0, 0)
            level_t(0, 0)
            for lv in range(1, LEVELS):
                level_t(0, lv)
                wo_lo_sub(lv - 1)
            wo_lo_sub(KT - 2)
            wo_lo_sub(KT - 1)
            PER = 2 * 3
            with dve.Fori(0, 3) as i:
                ch.enter(i, PER)
                body(i * 2 + 1, 1)
                body(i * 2 + 2, 0)
            ch.leave(3, PER)
            body(7, 1)
            r_rhs(7, 1)
            r_state(7, 1)
            r_y(7, 1)
            r_h2(7)
            r_xn(7)

            def u_lo_sub(s, n):
                dve.wait_ge(s_uhi, n)
                v.tensor_tensor(u_lo[s][:, :, :], u_raw[s][:, :, :],
                                u_hi[s][:, :, :].bitcast(F32), ALU.subtract).then_inc(s_ulo, 1)

            u_lo_sub(0, 1)
            u_lo_sub(1, 2)
            dve.wait_ge(s_h2n, 2 * NC)
            modulate(h2n_f, h2n_lo, h2n_hi, fcol, gcol_f, s_f_hf, s_f_hi, s_f_lo)
            u_lo_sub(2, 3)
            u_lo_sub(3, 4)

            def hidden(f, b):
                dve.wait_ge(s_sil, f + 1)
                v.tensor_tensor(hid[:, bass.ds(f, 1), :].rearrange("p a n -> p (a n)"),
                                silu_t[:, :], bank2(b + 2), ALU.mult).then_inc(s_hid, 1)

            with dve.Fori(0, FT // 2 - 1) as i:
                hidden(i * 2, 0)
                u_lo_sub(0, i * 4 + 5)
                u_lo_sub(1, i * 4 + 6)
                hidden(i * 2 + 1, 4)
                u_lo_sub(2, i * 4 + 7)
                u_lo_sub(3, i * 4 + 8)
            hidden(FT - 2, 0)
            hidden(FT - 1, 4)

            def d_lo_sub(k, h, s, n):
                dve.wait_ge(s_dhi, n)
                v.tensor_tensor(d_lo[s][:, :], d_raw[s][:, :], d_hi[s][:, :].bitcast(F32),
                                ALU.subtract)
                v.tensor_tensor(a_lo[s][:, :],
                                hid[:, bass.ds(k, 1), h * HALF:(h + 1) * HALF].rearrange(
                                    "p a n -> p (a n)"), a_hi[s][:, :].bitcast(F32),
                                ALU.subtract).then_inc(s_dlo, 1)

            with dve.Fori(0, 5) as i:
                for j in range(4):
                    d_lo_sub(i * 4 + j, 0, j, i * 4 + (j + 1))
            for n in range(20, 24):
                d_lo_sub(n % FT, n // FT, n % 4, n + 1)
            dve.wait_ge(s_fg, 16)


            def residual(t):
                if t % 4 < 3:
                    dve.wait_ge(s_dmm, 3 * (t // 4) + t % 4 + 1)
                else:
                    dve.wait_ge(s_down, FT * (t // 4 + 1))
                if t >= 4:
                    dve.wait_ge(s_out, 16 * 4)
                v.tensor_tensor(fin[t % 4][:, :], bank2(2 * (t % 4)), gate_f[:, :],
                                ALU.mult).then_inc(s_dev, 1)
                dve.wait_ge(s_dev, t + 1)
                dve.wait_ge(s_hre[t % 4], 16 * (t // 4 + 1))
                v.tensor_tensor(h_re[t % 4][:, :], h_re[t % 4][:, :], fin[t % 4][:, :],
                                ALU.add).then_inc(s_fh, 1)

            def finish(t):
                dve.wait_ge(s_fsq, t + 1)
                v.tensor_scalar(ssf[:, t:t + 1], ssf[:, t:t + 1], 1.0 / D_MODEL, EPS,
                                ALU.mult, ALU.add).then_inc(s_fss, 1)
                dve.wait_ge(s_frs, t + 1)
                v.scalar_tensor_tensor(out=fin[t % 4][:, :], in0=h_re[t % 4][:, :],
                                       scalar=ssf[:, NC + t:NC + t + 1], in1=fgain[:, :],
                                       op0=ALU.mult, op1=ALU.mult).then_inc(s_fin, 1)

            for t in range(4):
                residual(t)
            for n in range(24, 28):
                d_lo_sub(n - FT, 1, n % 4, n + 1)
            for t in range(4):
                finish(t)
            with dve.Fori(7, 11) as i:
                for j in range(4):
                    d_lo_sub(i * 4 + (j - 22), 1, j, i * 4 + (j + 1))
            residual(4)
            for t in range(5, NC):
                residual(t)
                finish(t - 1)
            finish(NC - 1)

        @block.tensor
        def _(pe):
            t_ = nc.tensor
            pe.wait_ge(s_small, 16 * 7)
            pe.wait_ge(s_const, 1)
            t_.transpose(ps[:, 6, 0:SMALL_A], rows_a[0:SMALL_A, :], ident[0:SMALL_A, 0:SMALL_A])
            t_.transpose(ps[:, 6, P:P + SMALL_B], rows_b[0:SMALL_B, :],
                         ident[0:SMALL_B, 0:SMALL_B]).then_inc(s_rows_tr, 1)
            for t in range(NC):
                pe.wait_ge(s_xn, t + 1)
                if t >= 2:
                    pe.wait_ge(s_xev, t - 1)
                for k in range(KT):
                    last = t_.transpose(bank2(2 * (t % 2))[:, k * P:(k + 1) * P],
                                        x_sl[t][:, k * P:(k + 1) * P], ident[:, :])
                last.then_inc(s_xtr, 1)

            def ada_columns(base):
                for n in range(2 * KT):
                    last = t_.matmul(ps[:, 7, n:n + 1],
                                     ada_acc[:, base + n * P:base + (n + 1) * P],
                                     ones[:, 0:1], start=True, stop=True)
                last.then_inc(s_ada_mm, 1)

            pe.wait_ge(s_ada_used, KT)
            ada_columns(0)

            def project(slot, bank, hi, lo):
                for k in range(KT):
                    if project.first:
                        pe.wait_ge(s_hlo, k + 1)
                    for n, (w, h) in enumerate(((w_lo, hi), (w_hi, lo), (w_hi, hi))):
                        for b in range(2):
                            last = t_.matmul(ps[:, bank + b, :], w[slot][:, k, :],
                                             h[:, k, b * HALF:(b + 1) * HALF],
                                             start=(k == 0 and n == 0),
                                             stop=(k == KT - 1 and n == 2))
                project.first = False
                last.then_inc(s_proj, 1)

            project.first = True
            for t in range(T0):
                pe.wait_ge(s_wsplit, t + 1)
                if t >= 2:
                    pe.wait_ge(s_evac, t - 1)
                elif t == 0:
                    pe.wait_ge(s_xev, NC)
                project(t, 2 * (t % 2), hn_hi, hn_lo)
            pe.wait_ge(s_evac, 3)
            for cc in range(NC):
                last = t_.transpose(ps[:, 6, 32 * cc:32 * cc + 32],
                                    seqb[0][0:32, PAD + cc * P:PAD + (cc + 1) * P],
                                    ident[0:32, 0:32])
            last.then_inc(s_batr, 1)
            with pe.Fori(0, 6) as i:
                for j in range(4):
                    pe.wait_ge(s_wsplit, i * 4 + (T0 + j + 1))
                    pe.wait_ge(s_evac, i * 4 + (T0 + j - 1))
                    project((T0 + j) % 4, 2 * ((T0 + j) % 2), hn_hi, hn_lo)
            pe.wait_ge(s_ada_used, 3 * KT)
            ada_columns(D_MODEL)
            for gt in range(2):
                if gt:
                    pe.wait_ge(s_gev, 1)
                for b in range(2):
                    last = t_.matmul(ps[:, 4 + b, :], ones[:, :],
                                     ada_acc[:, gt * 3 * D_MODEL + b * HALF:
                                             gt * 3 * D_MODEL + (b + 1) * HALF],
                                     start=True, stop=True)
                last.then_inc(s_gmm, 1)
            pe.wait_ge(s_gev, 2)
            pe.wait_ge(s_x, 128)
            pe.wait_ge(s_cs, 1)
            for t in range(PT):
                for b in range(2):
                    last = t_.matmul(ps[:, 4 + 2 * t + b, :], wpb[:, t, :],
                                     ypool[:, t, b * HALF:(b + 1) * HALF], start=True, stop=True)
            last.then_inc(s_pmm, 1)
            pe.wait_ge(s_pss, PT)
            for n in range(NC):
                for t in range(PT):
                    last = t_.matmul(ps[:, 4, n:n + 1],
                                     seqb[t][:, PAD + n * P:PAD + (n + 1) * P], ones[:, 0:1],
                                     start=(t == 0), stop=(t == PT - 1))
            last.then_inc(s_pmm, 1)
            pe.wait_ge(s_psq, 1)
            for n in range(NC):
                last = t_.matmul(bank2(6)[:, n * P:(n + 1) * P],
                                 ssf[:, NC + n:NC + n + 1].to_broadcast([P, P]), ident[:, :],
                                 start=True, stop=True)
            last.then_inc(s_pmm, 1)
            pe.wait_ge(s_sp, 3)
            pe.wait_ge(s_evac, NT)
            n48 = NC * HEADS
            for n, m in enumerate((tri, below, ones)):
                last = t_.matmul(ps[:, 0, n * n48:(n + 1) * n48], m[:, :],
                                 spt[:, 0, :, :].rearrange("p c h -> p (c h)"),
                                 start=True, stop=True)
            last.then_inc(s_gmx, 1)
            pe.wait_ge(s_scr, 1)

            def p_tr(cc, s, dma):
                pe.wait_ge(s_stg[s], dma)
                for gr in range(2):
                    if not (isinstance(cc, int) and cc == 0):
                        pe.wait_ge(s_u, cc * (2 * LEVELS) + (gr - 1))
                    for n in range(G3):
                        last = t_.transpose(ps[:, 2 * gr, n * P:(n + 1) * P],
                                            stage[s][:, HEADS + G3 * gr + n, :], ident[:, :])
                    last.then_inc(s_ktr, 1)
                for gr in range(2):
                    if gr == 1:
                        pe.wait_ge(s_sq, cc + 1)
                        for h in range(2 * HEADS):
                            t_.matmul(ps[:, 3, GW + h:GW + h + 1], sqb[:, h, :], ones[:, 0:1],
                                      start=True, stop=True)
                    for n in range(G3):
                        last = t_.transpose(ps[:, 2 * gr + 1, n * P:(n + 1) * P],
                                            stage[s][:, 2 * HEADS + G3 * gr + n, :], ident[:, :])
                    last.then_inc(s_vtr, 1)

            def p_kb(cc):
                for gr in range(2):
                    pe.wait_ge(s_kdd, cc * 2 + (gr + 1))
                    for n in range(G3):
                        last = t_.transpose(ps[:, 2 * gr, n * P:(n + 1) * P],
                                            kb[:, G3 * gr + n, :], ident[:, :])
                    last.then_inc(s_kbtr, 1)

            def p_arg(cc):
                for gr in range(2):
                    pe.wait_ge(s_slg, cc * 2 + (gr + 1))
                    pe.wait_ge(s_vb, cc * 2 + (gr + 1))
                    for n in range(G3):
                        last = t_.matmul(ps[:, 2 * gr + 1, n * P:(n + 1) * P],
                                         slg[:, G3 * gr + n, :], tri[:, :], start=True, stop=True)
                    last.then_inc(s_arg, 1)

            def p_kk(cc, s):
                for gr in range(2):
                    pe.wait_ge(s_kbT, cc * 2 + (gr + 1))
                    for n in range(G3):
                        h = G3 * gr + n
                        last = t_.matmul(ps[:, 2 * gr, n * P:(n + 1) * P],
                                         stage[s][:, HEADS + h, :], KbT[s][:, h, :],
                                         start=True, stop=True)
                    last.then_inc(s_kk, 1)
                for gr in range(2):
                    pe.wait_ge(s_exp, cc * 2 + (gr + 1))
                    for n in range(G3):
                        h = G3 * gr + n
                        last = t_.matmul(ps[:, 2 * gr + 1, n * P:(n + 1) * P],
                                         stage[s][:, HEADS + h, :], stage[s][:, h, :],
                                         start=True, stop=True)
                    last.then_inc(s_qk, 1)

            def level_y0(cc):
                for gr in range(2):
                    pe.wait_ge(s_na, cc * 2 + (gr + 1))
                    pe.wait_ge(s_qd, cc * 2 + (gr + 1))
                    for n in range(G3):
                        last = t_.transpose(ps[:, 2 * gr + 1, n * P:(n + 1) * P],
                                            NA[:, G3 * gr + n, :], ident[:, :])
                    last.then_inc(s_y, 1)

            def level_x(cc, lv):
                for gr in range(2):
                    pe.wait_ge(s_u, cc * (2 * LEVELS) + (2 * (lv - 1) + gr + 1))
                    for n in range(G3):
                        h = G3 * gr + n
                        last = t_.matmul(ps[:, 2 * gr, n * P:(n + 1) * P], NA[:, h, :],
                                         Tm[:, h, :], start=True, stop=True)
                    last.then_inc(s_xmm, 1)

            def level_y(cc, s, lv):
                for gr in range(2):
                    pe.wait_ge(s_xc, cc * (2 * LEVELS - 2) + (2 * (lv - 1) + gr + 1))
                    for n in range(G3):
                        h = G3 * gr + n
                        last = t_.matmul(ps[:, 2 * gr + 1, n * P:(n + 1) * P], Um[s][:, h, :],
                                         Xm[:, h, :], start=True, stop=True)
                    last.then_inc(s_y, 1)

            def level_tr(cc, lv):
                for gr in range(2):
                    pe.wait_ge(s_t, cc * (2 * LEVELS) + (2 * lv + gr + 1))
                    for n in range(G3):
                        last = t_.transpose(ps[:, 2 * gr, n * P:(n + 1) * P],
                                            Tm[:, G3 * gr + n, :], ident[:, :])
                    last.then_inc(s_utr, 1)

            def r1(cc, s, first):
                for gr in range(2):
                    if not first:
                        pe.wait_ge(s_s, cc * 2 + (gr - 1))
                        pe.wait_ge(s_h2n, cc * 2)
                    for n in range(G3):
                        h = G3 * gr + n
                        last = t_.matmul(ps[:, 4 + 2 * gr, n * P:(n + 1) * P], KbT[s][:, h, :],
                                         Sm[:, h, :], start=True, stop=True)
                    last.then_inc(s_ks, 1)
                for gr in range(2):
                    for n in range(G3):
                        h = G3 * gr + n
                        last = t_.matmul(ps[:, 5 + 2 * gr, n * P:(n + 1) * P], stage[s][:, h, :],
                                         Sm[:, h, :], start=True, stop=True)
                    last.then_inc(s_o1, 1)

            def r2(cc, s):
                for gr in range(2):
                    pe.wait_ge(s_r, cc * 2 + (gr + 1))
                    for n in range(G3):
                        h = G3 * gr + n
                        last = t_.matmul(ps[:, 4 + 2 * gr, n * P:(n + 1) * P], Um[s][:, h, :],
                                         Rm[:, h, :], start=True, stop=True)
                    last.then_inc(s_vmm, 1)

            def r3(cc, s):
                for gr in range(2):
                    pe.wait_ge(s_v, cc * 2 + (gr + 1))
                    for n in range(G3):
                        h = G3 * gr + n
                        last = t_.matmul(ps[:, 4 + 2 * gr, n * P:(n + 1) * P], Kd[s][:, h, :],
                                         Rm[:, h, :], start=True, stop=True)
                    last.then_inc(s_sd, 1)
                for gr in range(2):
                    pe.wait_ge(s_o1c, cc * 2 + (gr + 1))
                    for n in range(G3):
                        h = G3 * gr + n
                        last = t_.matmul(ps[:, 5 + 2 * gr, n * P:(n + 1) * P], QD[s][:, h, :],
                                         Rm[:, h, :], start=True, stop=True)
                    last.then_inc(s_o2, 1)

            def r4(cc):
                for gr in range(2):
                    pe.wait_ge(s_on, cc * 2 + (gr + 1))
                    for n in range(G3):
                        last = t_.transpose(ps[:, 5 + 2 * gr, n * P:(n + 1) * P],
                                            om[:, G3 * gr + n, :], ident[:, :])
                    last.then_inc(s_otr, 1)

            def mix(cc, k):
                if k == 0:
                    pe.wait_ge(s_ylo, cc * 2 + 2)
                    pe.wait_ge(s_s, cc * 2 + 2)
                if mix.first:
                    pe.wait_ge(s_wosp, k + 1)
                for n, (y, w) in enumerate(((y_lo, wo_hi), (y_hi, wo_lo), (y_hi, wo_hi))):
                    for b in range(2):
                        last = t_.matmul(ps[:, 4 + 2 * b, :], y[:, k, :],
                                         w[:, k, b * HALF:(b + 1) * HALF],
                                         start=(k == 0 and n == 0),
                                         stop=(k == KT - 1 and n == 2))
                if k == KT - 1:
                    last.then_inc(s_op, 1)

            def r6(cc):
                pe.wait_ge(s_xn2, cc + 1)
                for h in range(2):
                    for n in range(4):
                        last = t_.transpose(ps[:, 4 + 2 * h, n * P:(n + 1) * P],
                                            xn2[:, 4 * h + n, :], ident[:, :])
                    last.then_inc(s_htr, 1)

            def body(cc, s, dma, first):
                mix.first = first
                p_tr(cc, s, dma)
                r1(cc - 1, 1 - s, first)
                p_kb(cc)
                p_arg(cc)
                r2(cc - 1, 1 - s)
                p_kk(cc, s)
                r3(cc - 1, 1 - s)
                level_y0(cc)
                level_tr(cc, 0)
                level_x(cc, 1)
                level_y(cc, s, 1)
                level_tr(cc, 1)
                level_x(cc, 2)
                level_y(cc, s, 2)
                level_tr(cc, 2)
                r4(cc - 1)
                for lv in range(3, LEVELS):
                    level_x(cc, lv)
                    if lv < 6:
                        mix(cc - 1, 3 * (lv - 3))
                    level_y(cc, s, lv)
                    if lv < 6:
                        mix(cc - 1, 3 * (lv - 3) + 1)
                    level_tr(cc, lv)
                    if lv < 5:
                        mix(cc - 1, 3 * (lv - 3) + 2)
                r6(cc - 1)

            p_tr(0, 0, 16)
            p_kb(0)
            p_arg(0)
            p_kk(0, 0)
            level_y0(0)
            level_tr(0, 0)
            for lv in range(1, LEVELS):
                level_x(0, lv)
                level_y(0, 0, lv)
                level_tr(0, lv)
            body(1, 1, 16, True)
            body(2, 0, 32, False)
            with pe.Fori(1, 3) as i:
                body(i * 2 + 1, 1, i * 16 + 16, False)
                body(i * 2 + 2, 0, i * 16 + 32, False)
            body(7, 1, 64, False)
            r1(7, 1, False)
            r2(7, 1)
            r3(7, 1)
            r4(7)
            for k in range(KT):
                mix(7, k)
            r6(7)

            def gate_up(f, b, s0, lo_n, first):
                for up in range(2):
                    pe.wait_ge(s_ulo, lo_n + up)
                    for k in range(KT):
                        if first and up == 0:
                            pe.wait_ge(s_f_lo, k + 1)
                        for n, (w, h) in enumerate(((u_lo, h2n_hi), (u_hi, h2n_lo),
                                                    (u_hi, h2n_hi))):
                            for c2 in range(2):
                                last = t_.matmul(ps[:, b + 2 * up + c2, :],
                                                 w[s0 + up][:, k, :],
                                                 h[:, k, c2 * HALF:(c2 + 1) * HALF],
                                                 start=(k == 0 and n == 0),
                                                 stop=(k == KT - 1 and n == 2))
                last.then_inc(s_gu, 1)

            gate_up(0, 0, 0, 1, True)
            pe.wait_ge(s_h2n, 2 * NC)
            gate_up(1, 4, 2, 3, False)
            with pe.Fori(1, FT // 2) as i:
                for j in range(2):
                    pe.wait_ge(s_hid, i * 2 + (j - 1))
                    gate_up(i * 2 + j, 4 * j, 2 * j, i * 4 + (2 * j + 1), False)

            def down(n, s, first, last_k, waits):
                pe.wait_ge(s_dlo, n + 1)
                for tt in range(4):
                    if waits is not None:
                        pe.wait_ge(s_dev, waits + tt)
                    for m, (h, w) in enumerate(((a_lo, d_hi), (a_hi, d_lo), (a_hi, d_hi))):
                        for b in range(2):
                            ins = t_.matmul(ps[:, 2 * tt + b, :], h[s][:, tt * P:(tt + 1) * P],
                                            w[s][:, b * HALF:(b + 1) * HALF],
                                            start=(first and m == 0), stop=(last_k and m == 2))
                    if last_k and tt < 3:
                        ins.then_inc(s_dmm, 1)
                ins.then_inc(s_down, 1)

            pe.wait_ge(s_hid, FT)
            down(0, 0, True, False, None)
            for n in range(1, 4):
                down(n, n, False, False, None)
            with pe.Fori(1, 5) as i:
                for j in range(4):
                    down(i * 4 + j, j, False, False, None)
            down(20, 0, False, False, None)
            down(21, 1, False, True, None)
            down(22, 2, True, False, 1)
            down(23, 3, False, False, None)
            with pe.Fori(6, 10) as i:
                for j in range(4):
                    down(i * 4 + j, j, False, False, None)
            for n in range(40, 43):
                down(n, n % 4, False, False, None)
            down(43, 3, False, True, None)


_INS = ["x", "c", "w_ada", "b_ada", "norm_mix_gain", "w_in", "conv_w", "a_log", "dt_bias",
        "gdn_norm_gain", "w_pool", "pool_scale", "w_out", "norm_ffn_gain", "w_gate_up", "w_down",
        "norm_final_gain"]


def kernel(**inputs):
    import numpy as _np
    import concourse.bacc as _bacc
    from concourse.bass_utils import run_bass_kernel_spmd as _run

    nc = _bacc.Bacc("TRN2", target_bir_lowering=False, num_devices=1)
    arrays, args = {}, []
    for name in _INS:
        arr = _np.ascontiguousarray(inputs[name])
        arrays[f"in_{name}"] = arr
        args.append(nc.dram_tensor(f"in_{name}", arr.shape, F32, kind="ExternalInput").ap())
    args.append(nc.dram_tensor("out_0", (1, SEQ, D_MODEL), F32, kind="ExternalOutput").ap())
    args.append(nc.dram_tensor("qkvz_spill", (QKVT + ZT, P, SEQ), F32).ap())
    args.append(nc.dram_tensor("h2_spill", (SEQ, D_MODEL), F32).ap())
    hybrid_block(nc, *args)
    r = _run(nc, [arrays], core_ids=[0])
    return r.results[0]["out_0"]
```

```python
import concourse.bass as bass
from concourse import mybir
from concourse.alu_op_type import AluOpType as ALU
from contextlib import ExitStack

F32 = mybir.dt.float32
F32R = mybir.dt.float32r
BF16 = mybir.dt.bfloat16
I16 = mybir.dt.int16
ACT = mybir.ActivationFunctionType
AX = mybir.AxisListType

P = 128
D_MODEL, SEQ = 1024, 1024
KT = D_MODEL // P
NC = SEQ // P
POOL_W, HEADS, HD = 256, 6, 128
GDN_W = HEADS * HD
CONV = 4
D_FF = 2816
FT = D_FF // P
IN_COLS = POOL_W + 4 * GDN_W + 2 * HEADS
EPS = 1e-6
PT = POOL_W // P
QKVT = 3 * GDN_W // P
ZT = GDN_W // P
G3 = 3
GW = G3 * P
HALF = 512
LEVELS = 7
PAD = 16
SMALL_A = 3 * KT + 6 * KT
CA_C, CA_GM, CA_GF, CA_B = 0, KT, 2 * KT, 3 * KT
CB_CONV, CB_PS, CB_GG = 0, CONV * QKVT, CONV * QKVT + PT
SMALL_B = CB_GG + 1
WINDOWS = (2, 4, 8, 16)
BA_COL = IN_COLS - P
BA_ROW = P - 2 * HEADS - 96
KB = 1024
SBUF_BASE, SBUF_END = 16512, 212832


def settled(eng, value):
    return value if isinstance(value, int) else eng.compute_val(value)


class Chain:

    def __init__(self, eng, sem):
        self.eng, self.sem, self.n, self.dyn, self.n0 = eng, sem, 0, 0, 0

    def link(self, ins):
        self.n += 1
        ins.then_inc(self.sem, 1)
        self.eng.wait_ge(self.sem, self.n + self.dyn)

    def enter(self, trip, per):
        self.n0, self.dyn = self.n, trip * per

    def leave(self, trips, per):
        assert self.n - self.n0 == per, (self.n - self.n0, per)
        self.n, self.dyn = self.n0 + trips * per, 0


def hybrid_block(nc, x, c, w_ada, b_ada, norm_mix_gain, w_in, conv_w, a_log, dt_bias, gdn_gain,
                 w_pool, pool_scale, w_out, norm_ffn_gain, w_gate_up, w_down, norm_final_gain,
                 out, qkvz_d, h2_d):
    x2, out2 = x[0], out[0]
    wada, win, wout, wgu, wdn = w_ada[0], w_in[0], w_out[0], w_gate_up[0], w_down[0]

    def at(name, off, free, dt=F32):
        return nc.alloc_sbuf_tensor_at(name, [P] + list(free), dt, offset=SBUF_BASE + off)

    off = [0]

    def small(name, free, dt=F32):
        n = 2 if dt == BF16 else 4
        for f in free:
            n *= f
        t = at(name, off[0], free, dt)
        off[0] += (n + 31) // 32 * 32
        assert off[0] <= 8 * KB + 512, off
        return t

    ident = small("ident", [P])
    tri = small("tri", [P])
    below = small("below", [P])
    ones = small("ones", [P])
    lmask = small("lmask", [LEVELS, P], BF16)
    cols_a = small("cols_a", [SMALL_A])
    cols_b = small("cols_b", [SMALL_B])
    mcol = small("mcol", [2 * KT])
    gcol = small("gcol", [KT])
    fcol = small("fcol", [2 * KT])
    gcol_f = small("gcol_f", [KT])
    ba = small("ba", [NC, 2 * HEADS])
    al_b = small("al_b", [HEADS])
    dt_b = small("dt_b", [HEADS])
    spt = small("spt", [3, NC, HEADS])
    NSC = 5
    S_BETA, S_G, S_EG, S_ED, S_EL = range(NSC)
    allsc = small("allsc", [NC, NSC, HEADS])
    sc = [small(f"sc{s}", [NSC, HEADS]) for s in range(2)]
    rr = [small(f"rr{s}", [2 * HEADS]) for s in range(2)]
    ssb = small("ssb", [2 * HEADS])
    nbk = small("nbk", [HEADS])
    kdec = small("kdec", [HEADS])
    rq2 = [small(f"rq2{s}", [HEADS]) for s in range(2)]
    sso = small("sso", [HEADS])
    oc = small("oc", [4, HEADS])
    ssx = small("ssx", [NC])
    rst = small("rst", [NC])
    ssx2 = small("ssx2", [2])
    rst2 = small("rst2", [2])
    mhalf = small("mhalf", [2 * HEADS])
    epsh = small("epsh", [HEADS])
    rcnt = small("rcnt", [PT, PAD])
    ssf = small("ssf", [2 * NC])

    B0 = 8 * KB + 512
    gate_m = at("gate_m", B0, [D_MODEL])
    gate_f = at("gate_f", B0 + 4 * KB, [D_MODEL])
    C0 = B0 + 8 * KB
    D0 = C0 + 64 * KB
    hn_hi = at("hn_hi", C0, [KT, SEQ], F32R)
    hn_f = at("hn_f", C0 + 32 * KB, [KT, SEQ])
    hn_lo = at("hn_lo", C0 + 32 * KB, [KT, SEQ], F32R)
    WS = 4
    w_raw = [at(f"w_raw{s}", D0 + 8 * KB * s, [KT, P]) for s in range(WS)]
    w_lo = [at(f"w_lo{s}", D0 + 8 * KB * s, [KT, P], F32R) for s in range(WS)]
    w_hi = [at(f"w_hi{s}", D0 + 8 * KB * s + 4 * KB, [KT, P], F32R) for s in range(WS)]
    ypool = at("ypool", D0 + 32 * KB, [PT, SEQ])
    E0 = D0 + 40 * KB
    SW = PAD + SEQ
    seqb = [at(f"seqb{s}", E0 + 4 * SW * s, [SW]) for s in range(2)]
    acc = [at(f"acc{s}", E0 + 4 * SW * (2 + s), [SW]) for s in range(2)]
    E1 = E0 + 16 * SW
    act_o = [at(f"act_o{s}", E1 + 4 * KB * s, [SEQ]) for s in range(2)]
    ada_w = [at(f"ada_w{s}", E1 + 8 * KB + 8 * KB * s, [2 * D_MODEL]) for s in range(2)]
    ada_m = [at(f"ada_m{s}", C0 + 8 * KB * s, [2 * D_MODEL]) if s < 4 else ada_w[s - 4]
             for s in range(6)]
    ada_acc = at("ada_acc", E1 + 24 * KB, [4 * D_MODEL])
    x_sl = [at(f"x_sl{t}", E1 + 40 * KB + 4 * KB * t if t < 5 else
               (E1 + 4 * KB * (t - 5) if t < 7 else D0 + 32 * KB), [D_MODEL]) for t in range(NC)]
    mixed_sq = at("mixed_sq", E1 + 8 * KB, [PT, SEQ])
    wpb = at("wpb", E1 + 60 * KB, [PT, P])
    rows_a = at("rows_a", E1 + 61 * KB, [P])
    rows_b = at("rows_b", E1 + 61 * KB + 512, [P])
    assert E1 + 62 * KB <= SBUF_END
    wo_hi = at("wo_hi", C0, [KT, D_MODEL], F32R)
    wo_raw = at("wo_raw", C0 + 32 * KB, [KT, D_MODEL])
    wo_lo = at("wo_lo", C0 + 32 * KB, [KT, D_MODEL], F32R)
    h2n_f = at("h2n_f", D0, [KT, SEQ])
    h2n_lo = at("h2n_lo", D0, [KT, SEQ], F32R)
    stage = [at(f"stage{s}", E0 + 12 * KB * s, [QKVT + ZT, P]) for s in range(2)]
    pos = [E1 + 8 * KB]

    def temp(name, free=(HEADS, P), dt=F32, alias=None):
        n = 4 * free[0] * free[1]
        o = pos[0] if alias is None else alias
        t = at(name, o, list(free), dt)
        if alias is None:
            pos[0] += n
        return t, o

    QD = [temp(f"QD{s}")[0] for s in range(2)]
    Kd = [temp(f"Kd{s}")[0] for s in range(2)]
    Vb = [temp(f"Vb{s}")[0] for s in range(2)]
    KbT = [temp(f"KbT{s}")[0] for s in range(2)]
    Sm, _ = temp("Sm")
    om, _ = temp("om")
    NA, _ = temp("NA")
    assert pos[0] >= E1 + 40 * KB
    Em, _ = temp("Em")
    Rm, o_R = temp("Rm")
    Tm, o_T = temp("Tm")
    Xm, o_X = temp("Xm")
    Um = [temp(f"Um{s}")[0] for s in range(2)]
    assert pos[0] <= E1 + 60 * KB
    slg, _ = temp("slg", alias=o_T)
    kb, _ = temp("kb", alias=o_X)
    rkt, _ = temp("rkt", alias=o_R)
    y_hi, o_yh = temp("y_hi", (KT, P), F32R)
    y_lo, o_yl = temp("y_lo", (KT, P), F32R)
    xn2, _ = temp("xn2", (KT, P), alias=o_yh)
    junk2, _ = temp("junk2", (KT, P), alias=o_yl)
    xt, _ = temp("xt", (KT, P))
    assert pos[0] <= SBUF_END
    h2n_hi = at("h2n_hi", C0, [KT, SEQ], F32R)
    u_raw = [at(f"u_raw{s}", C0 + 32 * KB + 8 * KB * s, [KT, P]) for s in range(WS)]
    u_lo = [at(f"u_lo{s}", C0 + 32 * KB + 8 * KB * s, [KT, P], F32R) for s in range(WS)]
    u_hi = [at(f"u_hi{s}", C0 + 36 * KB + 8 * KB * s, [KT, P], F32R) for s in range(WS)]
    hid = at("hid", D0 + 32 * KB, [FT, SEQ])
    assert D0 + 32 * KB + 88 * KB <= SBUF_END
    silu_t = at("silu_t", B0, [SEQ])
    DS = 4
    d_off = [C0 + 36 * KB, C0, C0 + 12 * KB, C0 + 24 * KB]
    d_raw = [at(f"d_raw{s}", d_off[s], [D_MODEL]) for s in range(DS)]
    d_lo = [at(f"d_lo{s}", d_off[s], [D_MODEL], F32R) for s in range(DS)]
    d_hi = [at(f"d_hi{s}", d_off[s] + 4 * KB, [D_MODEL], F32R) for s in range(DS)]
    a_hi = [at(f"a_hi{s}", d_off[s] + 8 * KB, [HALF], F32R) for s in range(DS)]
    a_lo = [at(f"a_lo{s}", d_off[s] + 10 * KB, [HALF], F32R) for s in range(DS)]
    h_re = [at(f"h_re{s}", D0 + 4 * KB * s, [D_MODEL]) for s in range(4)]
    fin = [at(f"fin{s}", C0 + 48 * KB + 4 * KB * s, [D_MODEL]) for s in range(4)]
    fgain = at("fgain", D0 + 24 * KB, [D_MODEL])
    fjunk = at("fjunk", D0 + 28 * KB, [D_MODEL])

    ctx = ExitStack()
    with ctx:
        ps = ctx.enter_context(nc.psum_tensor("ps", [P, 8, HALF], F32))

        def sem(name):
            return ctx.enter_context(nc.semaphore(name))

        def bank2(b):
            return ps[:, b:b + 2, :].rearrange("p a n -> p (a n)")

        def grp(b):
            return ps[:, b, 0:GW]

        def grp3(b):
            return ps[:, b, 0:GW].rearrange("p (h n) -> p h n", h=G3)

        def bc(t, g):
            return t[:, G3 * g:G3 * g + G3].unsqueeze(2).to_broadcast([P, G3, P])

        def flat(t, g=None):
            v = t[:, :, :] if g is None else t[:, G3 * g:G3 * g + G3, :]
            return v.rearrange("p h n -> p (h n)")

        s_small = sem("small_loaded")
        s_x = sem("x_loaded")
        s_xsq = sem("x_tile_squared")
        s_h2sq = sem("h2_squared")
        s_fsq = sem("final_squared")
        s_xs = [sem(f"x_loaded{t}") for t in range(NC)]
        s_ada = [sem(f"ada_loaded{s}") for s in range(2)]
        s_adam = [sem(f"ada_mixer_loaded{s}") for s in range(4)] + s_ada
        s_w = [sem(f"w_in_loaded{s}") for s in range(WS)]
        s_wo = sem("w_out_loaded")
        s_const = sem("constants_ready")
        s_pool_chain = sem("pool_chain")
        s_dve_chain = sem("dve_chain")
        s_act_chain = sem("act_chain")
        s_rows_tr = sem("small_rows_transposed")
        s_cols = sem("small_columns_ready")
        s_cs = sem("c_silu_ready")
        s_ss = sem("x_square_sum_ready")
        s_rst = sem("x_rstd_ready")
        s_xn = sem("x_normalised")
        s_xtr = sem("x_transposed")
        s_xev = sem("x_transpose_evacuated")
        s_ada_used = sem("ada_piece_used")
        s_ada_mm = sem("ada_columns_summed")
        s_hf = sem("hn_modulated")
        s_hhi = sem("hn_hi_ready")
        s_hlo = sem("hn_lo_ready")
        s_wsplit = sem("w_in_split")
        s_proj = sem("projected")
        s_evac = sem("projection_evacuated")
        s_seq = sem("sequence_tile_used")
        s_conv = sem("conv_ready")
        s_aout = sem("activated_tile_ready")
        s_spill = [sem(f"tile_spilled{s}") for s in range(2)]
        s_batr = sem("ba_transposed")
        s_pmm = sem("pool_mixed")
        s_psq = sem("pool_squares_ready")
        s_pss = sem("pool_square_sums")
        s_pst = sem("pool_sum_ready")
        s_gmm = sem("gate_columns_summed")
        s_gev = sem("gate_columns_read")
        s_sp = sem("softplus_steps")
        s_spa = sem("softplus_activation")
        s_gmx = sem("decay_sums")
        s_ex = sem("decay_exponentials")
        s_scr = sem("scalars_ready")

        block = ctx.enter_context(nc.Block())

        s_stg = [sem(f"chunk_staged{s}") for s in range(2)]
        s_xin = sem("x_chunk_loaded")
        s_h2st = sem("h2_stored")
        (s_sq, s_ktr, s_vtr, s_ssr, s_rr, s_scc, s_vb, s_kbd, s_kdd, s_kbtr, s_kbT, s_slg, s_arg,
         s_exp, s_e, s_ti, s_kk, s_qk, s_na, s_qd, s_y, s_t, s_utr, s_u, s_xmm, s_xc) = [
            sem(n) for n in (
                "qk_squared", "k_transposed", "v_transposed", "square_sums_read", "norms_ready",
                "chunk_scalars_ready", "v_beta_ready", "k_beta_ready", "k_decay_ready",
                "kb_transposed", "kbT_ready", "decay_weights_ready", "decay_args", "decay_exp",
                "decay_ready", "inverse_init", "kk_products", "qk_products", "na_ready", "qd_ready",
                "level_product", "inverse_updated", "inverse_transposed", "u_ready",
                "level_x_product", "level_x_ready")]
        s_stz = [sem(f"z_staged{s}") for s in range(2)]
        s_sums0 = sem("first_square_sums")
        s_uz = sem("inverse_first_level")
        s_uf = sem("inverse_complete")
        s_oss = sem("o_square_sums_scaled")
        s_ort = sem("o_root_ready")
        s_wog = sem("w_out_gated")
        (s_s, s_ks, s_o1, s_r, s_o1c, s_vmm, s_v, s_o2, s_sd, s_o, s_sso, s_on, s_otr, s_yf,
         s_yhi, s_ylo, s_op, s_h2, s_ssx2, s_rst2, s_xn2, s_htr, s_h2n) = [
            sem(n) for n in (
                "state_ready", "k_state_product", "q_state_product", "rhs_ready", "o1_copied",
                "v_new_product", "v_new_ready", "o2_product", "state_delta", "o_ready",
                "o_square_sums", "o_normalised", "o_transposed", "y_ready", "y_hi_ready",
                "y_lo_ready", "mix_product", "h2_ready", "h2_square_sum", "h2_rstd",
                "h2_normalised", "h2_transposed", "h2_transpose_evacuated")]
        s_wosp = sem("w_out_split")
        s_wohi = sem("w_out_hi")
        s_u_ld = [sem(f"gate_up_loaded{s}") for s in range(WS)]
        s_uhi = sem("gate_up_hi")
        s_ulo = sem("gate_up_lo")
        s_f_hf = sem("ffn_modulated")
        s_f_hi = sem("ffn_hi_ready")
        s_f_lo = sem("ffn_lo_ready")
        s_gu = sem("gate_up_product")
        s_sil = sem("gate_activated")
        s_hid = sem("hidden_ready")
        s_d_ld = [sem(f"down_loaded{s}") for s in range(DS)]
        s_dhi = sem("down_hi")
        s_dlo = sem("down_lo")
        s_down = sem("down_step_done")
        s_dmm = sem("down_product")
        s_dev = sem("down_evacuated")
        s_hre = [sem(f"h2_reloaded{s}") for s in range(4)]
        s_fg = sem("final_gain_loaded")
        s_fh = sem("final_h_ready")
        s_fss = sem("final_square_sum")
        s_frs = sem("final_rstd")
        s_fin = sem("final_ready")
        s_out = sem("output_stored")

        def w_cols(t):
            return t * P if t < PT else (BA_COL if t == PT else (t - 1) * P)

        NT = PT + 1 + QKVT + ZT
        T0 = PT + 1
        spill3 = qkvz_d.rearrange("t p n -> p t n")

        @block.sync
        def _(sp):
            def x_tile(t):
                sp.dma_start(x_sl[t][:, :], x2[t * P:(t + 1) * P, :]).then_inc(s_xs[t], 16)

            for t in range(2):
                x_tile(t)
            for r, (src, n) in enumerate(((c, KT), (norm_mix_gain, KT), (norm_ffn_gain, KT))):
                sp.dma_start(rows_a[r * KT:r * KT + n, :],
                             src.rearrange("o (r p) -> (o r) p", p=P)).then_inc(s_small, 16)
            sp.dma_start(rows_a[CA_B:SMALL_A, :],
                         b_ada.rearrange("o (r p) -> (o r) p", p=P)).then_inc(s_small, 16)
            sp.dma_start(rows_b[0:CB_PS, :],
                         conv_w.rearrange("o t (r p) -> (o t r) p", p=P)).then_inc(s_small, 16)
            sp.dma_start(rows_b[CB_PS:CB_GG, :],
                         pool_scale.rearrange("o (r p) -> (o r) p", p=P)).then_inc(s_small, 16)
            sp.dma_start(rows_b[CB_GG:SMALL_B, :], gdn_gain).then_inc(s_small, 16)
            for t in range(2, NC):
                x_tile(t)
            for k in range(KT):
                if k >= 6:
                    sp.wait_ge(s_ada_used, k - 5)
                sp.dma_start(ada_m[k % 6][:, :],
                             wada[k * P:(k + 1) * P, 0:2 * D_MODEL]).then_inc(s_adam[k % 6], 16)
            for t in range(4):
                sp.dma_start(w_raw[t][:, :, :], win[:, w_cols(t):w_cols(t) + P].rearrange(
                    "(k p) n -> p k n", p=P)).then_inc(s_w[t], 16)
            sp.dma_start(al_b[:, :], a_log.to_broadcast([P, HEADS])).then_inc(s_x, 16)
            sp.dma_start(dt_b[:, :], dt_bias.to_broadcast([P, HEADS])).then_inc(s_x, 16)
            sp.dma_start(gate_m[:, :], b_ada[:, 2 * D_MODEL:3 * D_MODEL].to_broadcast(
                [P, D_MODEL])).then_inc(s_x, 16)
            sp.dma_start(gate_f[:, :], b_ada[:, 5 * D_MODEL:6 * D_MODEL].to_broadcast(
                [P, D_MODEL])).then_inc(s_x, 16)
            sp.wait_ge(s_const, 2)
            for g in range(4):
                o = 64 * (g % 2)
                sp.dma_start(wpb[o:o + 64, g // 2, o:o + 64], w_pool[0, g]).then_inc(s_x, 16)
            with_loop = (NT - 4) // 4
            with sp.Fori(0, with_loop) as i:
                for j in range(4):
                    sp.wait_ge(s_proj, i * 4 + (j + 1))
                    sp.dma_start(w_raw[j][:, :, :],
                                 win[:, bass.ds(i * (4 * P) + (j + 3) * P, P)].rearrange(
                                     "(k p) n -> p k n", p=P)).then_inc(s_w[j], 16)
            for t in range(4 + 4 * with_loop, NT):
                sp.wait_ge(s_proj, t - 3)
                sp.dma_start(w_raw[t % 4][:, :, :], win[:, w_cols(t):w_cols(t) + P].rearrange(
                    "(k p) n -> p k n", p=P)).then_inc(s_w[t % 4], 16)
            def stage_load(cc, s):
                sp.dma_start(stage[s][:, 0:QKVT, :],
                             spill3[:, 0:QKVT, bass.ds(cc * P, P)]).then_inc(s_stg[s], 16)

            def z_load(cc, s):
                sp.dma_start(stage[s][:, QKVT:, :],
                             spill3[:, QKVT:, bass.ds(cc * P, P)]).then_inc(s_stz[s], 16)

            def x_load(cc):
                sp.dma_start(xt[:, :, :].rearrange("p k n -> p (k n)"),
                             x2[bass.ds(cc * P, P), :]).then_inc(s_xin, 16)

            def h2_store(cc):
                sp.wait_ge(s_h2, cc + 1)
                sp.dma_start(h2_d[bass.ds(cc * P, P), :],
                             xt[:, :, :].rearrange("p k n -> p (k n)")).then_inc(s_h2st, 16)

            sp.wait_ge(s_aout, QKVT)
            for s in range(2):
                sp.wait_ge(s_spill[s], 16 * QKVT // 2)
            stage_load(0, 0)
            sp.wait_ge(s_proj, NT)
            sp.dma_start(wo_raw[:, :, :],
                         wout.rearrange("(k p) n -> p k n", p=P)).then_inc(s_wo, 16)
            for s in range(2):
                sp.wait_ge(s_spill[s], 16 * (QKVT + ZT) // 2)
            stage_load(1, 1)
            z_load(0, 0)
            z_load(1, 1)
            x_load(0)

            def step(cc, s):
                if s is not None:
                    sp.wait_ge(s_o1, cc * 2)
                    stage_load(cc + 1, s)
                    sp.wait_ge(s_yf, cc * 2)
                    z_load(cc + 1, s)
                h2_store(cc - 1)
                sp.wait_ge(s_h2st, cc * 16)
                sp.wait_ge(s_xn2, cc)
                x_load(cc)

            with sp.Fori(0, 3) as i:
                step(i * 2 + 1, 0)
                step(i * 2 + 2, 1)
            step(7, None)
            h2_store(7)

            def gu_load(f, s, up):
                sp.dma_start(u_raw[s][:, :, :], wgu[:, bass.ds(f * P + up * D_FF, P)].rearrange(
                    "(k p) n -> p k n", p=P)).then_inc(s_u_ld[s], 16)

            sp.wait_ge(s_op, NC)
            for f in range(2):
                for up in range(2):
                    gu_load(f, 2 * f + up, up)
            with sp.Fori(0, FT // 2 - 1) as i:
                for j in range(2):
                    sp.wait_ge(s_gu, i * 2 + (j + 1))
                    for up in range(2):
                        gu_load(i * 2 + (2 + j), 2 * j + up, up)

            def d_load(k, s):
                sp.dma_start(d_raw[s][:, :], wdn[bass.ds(k * P, P), :]).then_inc(s_d_ld[s], 16)

            sp.wait_ge(s_h2st, NC * 16)
            sp.wait_ge(s_gu, FT - 1)
            d_load(0, 0)
            sp.wait_ge(s_gu, FT)
            for k in range(1, DS):
                d_load(k, k)
            sp.dma_start(fgain[:, :], norm_final_gain.unsqueeze(0).to_broadcast(
                [P, D_MODEL])).then_inc(s_fg, 16)
            for t in range(4):
                sp.dma_start(h_re[t][:, :], h2_d[t * P:(t + 1) * P, :]).then_inc(s_hre[t], 16)
            with sp.Fori(0, 4) as i:
                for j in range(4):
                    sp.wait_ge(s_down, i * 4 + (j + 1))
                    d_load(i * 4 + (j + 4), j)
            for n in (20, 21):
                sp.wait_ge(s_down, n - 3)
                d_load(n, n % 4)
            def second_pass(first, end):
                with sp.Fori(first, end) as i:
                    for j in range(4):
                        sp.wait_ge(s_down, i * 4 + (j + 19))
                        d_load(i * 4 + j, (j + 22) % 4)

            def store(t):
                sp.wait_ge(s_fin, t + 1)
                sp.dma_start(out2[t * P:(t + 1) * P, :], fin[t % 4][:, :]).then_inc(s_out, 16)

            second_pass(0, 2)
            for t in range(4):
                store(t)
                sp.dma_start(h_re[t][:, :],
                             h2_d[(4 + t) * P:(5 + t) * P, :]).then_inc(s_hre[t], 16)
            second_pass(2, 5)
            for n in (42, 43):
                sp.wait_ge(s_down, n - 3)
                d_load(n - 22, n % 4)
            for t in range(4, NC):
                store(t)
            sp.wait_ge(s_out, 16 * NC)

        @block.gpsimd
        def _(pool):
            g = nc.gpsimd
            ch = Chain(pool, s_pool_chain)
            ch.link(g.memset(ones[:, :], 1.0))
            one = ones[:, :]
            g.affine_select(out=ident[:, :], in_=one, compare_op=ALU.is_equal, fill=0.0, base=0,
                            pattern=[[1, P]], channel_multiplier=-1)
            ch.link(g.memset(mhalf[:, :], -0.5))
            g.memset(epsh[:, :], EPS * HD)
            g.affine_select(out=tri[:, :], in_=one, compare_op=ALU.is_ge, fill=0.0, base=0,
                            pattern=[[1, P]], channel_multiplier=-1)
            g.affine_select(out=below[:, :], in_=one, compare_op=ALU.is_gt, fill=0.0, base=0,
                            pattern=[[-1, P]], channel_multiplier=1).then_inc(s_const, 1)
            ch.link(g.memset(wpb[:, :, :], 0.0))
            for t in range(NC):
                pool.wait_ge(s_ss, t + 1)
                g.tensor_tensor(rst[:, t:t + 1], ssx[:, t:t + 1], mhalf[:, 0:1],
                                ALU.pow).then_inc(s_rst, 1)

            for lv in range(LEVELS):
                b = 1 << lv
                m = lmask[:, lv, :].rearrange("p (a h r) -> p a h r", h=2, r=b)
                o = one.rearrange("p (a h r) -> p a h r", h=2, r=b)
                tr = lv in (0, LEVELS - 1)
                ch.link(g.affine_select(out=m, in_=o, compare_op=ALU.is_ge, fill=0.0,
                                        base=-2 * P if tr else -b,
                                        pattern=[[-2 * b, P // (2 * b)],
                                                 [2 * P if tr else -2 * P, 2], [0, b]],
                                        channel_multiplier=1))
                ch.link(g.affine_select(out=m, in_=m, compare_op=ALU.is_ge, fill=0.0,
                                        base=(b if tr else 2 * b) - 1,
                                        pattern=[[2 * b, P // (2 * b)], [0, 2], [0, b]],
                                        channel_multiplier=-1))
            for t in range(PT):
                for hf in range(2):
                    w = WINDOWS[2 * t + hf]
                    rows = slice(64 * hf, 64 * hf + 64)
                    for j in range(w - 1):
                        g.memset(rcnt[rows, t, j:j + 1], 1.0 / (j + 1))
                    ch.link(g.memset(rcnt[rows, t, w - 1:PAD], 1.0 / w))
            g.memset(seqb[0][:, 0:PAD], 0.0)
            g.memset(seqb[1][:, 0:PAD], 0.0).then_inc(s_const, 1)

            def split(s, count):
                count = settled(pool, count)
                pool.wait_ge(s_const, 1)
                pool.wait_ge(s_w[s], count)
                ch.link(g.tensor_copy(w_hi[s][:, :, :], w_raw[s][:, :, :]))
                g.tensor_tensor(w_lo[s][:, :, :], w_raw[s][:, :, :],
                                w_hi[s][:, :, :].bitcast(F32), ALU.subtract).then_inc(s_wsplit, 1)

            for t in range(T0):
                split(t, 16)
            with pool.Fori(0, 6) as i:
                ch.enter(i, 4)
                for j in range(4):
                    split((3 + j) % 4, i * 16 + (16 if j == 0 else 32))
            ch.leave(6, 4)
            pool.wait_ge(s_pst, 1)
            g.tensor_tensor(ssf[:, NC:2 * NC], ssf[:, 0:NC], mhalf[:, 0:NC],
                            ALU.pow).then_inc(s_psq, 1)


            def norm_root(cc, s):
                pool.wait_ge(s_ssr, cc + 1)
                g.tensor_tensor(rr[s][:, :], ssb[:, :], mhalf[:, :], ALU.pow).then_inc(s_rr, 1)

            def rk_tri(cc, s):
                pool.wait_ge(s_rr, cc + 1)
                ch.link(g.tensor_tensor(rkt[:, :, :],
                                        tri[:, :].unsqueeze(1).to_broadcast([P, HEADS, P]),
                                        rr[s][:, HEADS:].unsqueeze(2).to_broadcast(
                                            [P, HEADS, P]), ALU.mult))

            def u_init(s):
                g.tensor_copy(Um[s][:, :, :], ident[:, :].unsqueeze(1).to_broadcast(
                    [P, HEADS, P])).then_inc(s_ti, 1)

            def p_slg(cc, s):
                pool.wait_ge(s_scc, cc + 1)
                if not (isinstance(cc, int) and cc == 0):
                    pool.wait_ge(s_xmm, cc * (2 * LEVELS - 2))
                for gr in range(2):
                    g.tensor_tensor(slg[:, G3 * gr:G3 * gr + G3, :],
                                    below[:, :].unsqueeze(1).to_broadcast([P, G3, P]),
                                    bc(sc[s][:, S_G, :], gr), ALU.mult).then_inc(s_slg, 1)

            def p_e(cc, s):
                for gr in range(2):
                    e = Em[:, G3 * gr:G3 * gr + G3, :]
                    pool.wait_ge(s_exp, cc * 2 + (gr + 1))
                    g.tensor_tensor(e, e, rkt[:, G3 * gr:G3 * gr + G3, :],
                                    ALU.mult).then_inc(s_e, 1)

            def r_root(cc):
                pool.wait_ge(s_oss, cc + 1)
                g.tensor_tensor(oc[:, 2, :], oc[:, 1, :], mhalf[:, 0:HEADS],
                                ALU.pow).then_inc(s_ort, 1)

            def r_tail(cc):
                pool.wait_ge(s_ssx2, cc + 1)
                g.tensor_tensor(rst2[:, 0:1], ssx2[:, 1:2], mhalf[:, 0:1],
                                ALU.pow).then_inc(s_rst2, 1)

            def body(cc, s, first=False, last=False):
                p_slg(cc, s)
                if not first:
                    r_tail(cc - 2)
                p_e(cc, s)
                r_root(cc - 1)
                if not last:
                    norm_root(cc + 1, 1 - s)
                    u_init(1 - s)
                    rk_tri(cc + 1, 1 - s)

            norm_root(0, 0)
            u_init(0)
            u_init(1)
            rk_tri(0, 0)
            p_slg(0, 0)
            p_e(0, 0)
            pool.wait_ge(s_wo, 16)
            pool.wait_ge(s_gev, 1)
            for k in range(KT):
                g.tensor_tensor(wo_raw[:, k, :], wo_raw[:, k, :], gate_m[:, :],
                                ALU.mult).then_inc(s_wog, 1)
            norm_root(1, 1)
            rk_tri(1, 1)
            PER = 2
            body(1, 1, first=True)
            body(2, 0)
            with pool.Fori(1, 3) as i:
                ch.enter(i - 1, PER)
                body(i * 2 + 1, 1)
                body(i * 2 + 2, 0)
            ch.leave(2, PER)
            body(7, 1, last=True)
            r_tail(6)
            r_root(7)
            r_tail(7)
            for t in range(NC):
                pool.wait_ge(s_fss, t + 1)
                g.tensor_tensor(ssf[:, NC + t:NC + t + 1], ssf[:, t:t + 1], mhalf[:, 0:1],
                                ALU.pow).then_inc(s_frs, 1)

        @block.scalar
        def _(act):
            a = nc.scalar
            ch = Chain(act, s_act_chain)
            act.wait_ge(s_cols, 1)
            a.activation(cols_a[:, CA_C:CA_C + KT], cols_a[:, CA_C:CA_C + KT],
                         ACT.Silu).then_inc(s_cs, 1)
            for t in range(NC):
                act.wait_ge(s_xs[t], 16)
                if t:
                    act.wait_ge(s_xsq, t)
                a.activation(bank2(4), x_sl[t][:, :], ACT.Square,
                             accum_out=ssx[:, t:t + 1]).then_inc(s_xsq, 1)
            for t in range(NC):
                act.wait_ge(s_xtr, t + 1)
                a.activation(hn_f[:, :, t * P:(t + 1) * P],
                             bank2(2 * (t % 2)).rearrange("p (k n) -> p k n", k=KT),
                             ACT.Copy).then_inc(s_xev, 1)
            for k in range(KT):
                act.wait_ge(s_hf, k + 1)
                a.activation(hn_hi[:, k, :], hn_f[:, k, :], ACT.Copy).then_inc(s_hhi, 1)

            def evac(t, slot, used):
                act.wait_ge(s_proj, t + 1)
                if used is not None:
                    act.wait_ge(*used)
                a.activation(seqb[slot][:, PAD:], bank2(2 * slot), ACT.Copy).then_inc(s_evac, 1)

            evac(0, 0, None)
            evac(1, 1, None)
            act.wait_ge(s_proj, 3)
            act.wait_ge(s_seq, 1)
            a.activation(seqb[0][0:32, PAD:], bank2(0)[96:128, :], ACT.Copy).then_inc(s_evac, 1)

            def ada_load(k):
                for s in range(2):
                    act.wait_ge(s_ada_used, k * 2 + (KT - 1 + s))
                    act.dma_start(ada_w[s][:, :],
                                  wada[bass.ds(k * P, P), (2 + 2 * s) * D_MODEL:
                                       (4 + 2 * s) * D_MODEL]).then_inc(s_ada[s], 16)

            def spill(n, slot):
                act.dma_start(qkvz_d[bass.ds(n, 1), :, :].rearrange("a p n -> p (a n)"),
                              act_o[slot][:, :]).then_inc(s_spill[slot], 16)

            def qkv(n, guard_spill):
                t = n + T0
                slot = qkv.slot
                evac(t, slot, (s_seq, n + PT) if isinstance(n, int) and n < 2 else
                     (s_conv, n - 1))
                act.wait_ge(s_conv, n + 1)
                if guard_spill is not None:
                    act.wait_ge(s_spill[1 - slot], guard_spill)
                a.activation(act_o[1 - slot][:, :], acc[1 - slot][:, 0:SEQ],
                             ACT.Silu).then_inc(s_aout, 1)
                act.wait_ge(s_aout, n + 1)
                spill(n, 1 - slot)

            ada_load(0)
            qkv.slot = 1
            qkv(0, None)
            act.wait_ge(s_sp, 1)
            a.activation(spt[:, 0, :, :], spt[:, 0, :, :], ACT.Exp, scale=-1.0).then_inc(s_spa, 1)
            a.activation(allsc[:, :, S_BETA, :], ba[:, :, 0:HEADS], ACT.Exp,
                         scale=-1.0).then_inc(s_spa, 1)
            act.wait_ge(s_x, 128)
            a.activation(al_b[:, :], al_b[:, :], ACT.Exp).then_inc(s_spa, 1)
            qkv.slot = 0
            qkv(1, None)
            act.wait_ge(s_sp, 2)
            a.activation(spt[:, 0, :, :], spt[:, 0, :, :], ACT.Ln).then_inc(s_spa, 1)
            with act.Fori(1, 8) as i:
                ada_load(i)
                for j in range(2):
                    qkv.slot = (j + 1) % 2
                    qkv(i * 2 + j, i * 16)
            for n in range(16, 18):
                qkv.slot = (n + 1) % 2
                qkv(n, (n // 2) * 16)
            act.wait_ge(s_gmx, 1)
            n48 = NC * HEADS
            for n, dst in enumerate((S_EG, S_ED, S_EL)):
                last = a.activation(allsc[:, :, dst, :],
                                    ps[:, 6, n * n48:(n + 1) * n48].rearrange(
                                        "p (c h) -> p c h", h=HEADS), ACT.Exp)
            last.then_inc(s_ex, 1)

            def z_tile(i):
                slot, o = (i + T0 + QKVT) % 2, i % 2
                act.wait_ge(s_proj, T0 + QKVT + i + 1)
                act.wait_ge(s_spill[o], 16 * ((QKVT + i) // 2))
                a.activation(act_o[o][:, :], bank2(2 * slot), ACT.Silu).then_inc(s_evac, 1)
                act.wait_ge(s_evac, T0 + QKVT + i + 1)
                spill(QKVT + i, o)

            for i in range(3):
                z_tile(i)
            act.wait_ge(s_pmm, 1)
            for t in range(PT):
                ch.link(a.activation(ypool[:, t, :], bank2(4 + 2 * t), ACT.Copy))
                a.activation(mixed_sq[:, t, :], ypool[:, t, :], ACT.Square).then_inc(s_pss, 1)

            def squares(cc, s, dma):
                act.wait_ge(s_stg[s], dma)
                if cc is not None:
                    act.wait_ge(s_qd, cc * 2)
                    if not (isinstance(cc, int) and cc == 1):
                        act.wait_ge(s_o2, cc * 2 - 2)
                a.activation(flat(Em), stage[s][:, HEADS:2 * HEADS, :].rearrange(
                    "p h n -> p (h n)"), ACT.Square)
                a.activation(flat(Rm), stage[s][:, 0:HEADS, :].rearrange(
                    "p h n -> p (h n)"), ACT.Square).then_inc(s_sq, 1)

            def p_kbT(cc, s):
                for gr in range(2):
                    act.wait_ge(s_kbtr, cc * 2 + (gr + 1))
                    a.activation(flat(KbT[s], gr), grp(2 * gr + 1), ACT.Copy).then_inc(s_kbT, 1)

            def p_exp(cc):
                for gr in range(2):
                    act.wait_ge(s_arg, cc * 2 + (gr + 1))
                    a.activation(flat(Em, gr), grp(5 + 2 * gr), ACT.Exp).then_inc(s_exp, 1)

            def level_u(cc, s, lv):
                dst = Tm if lv == 0 else Um[s]
                for gr in range(2):
                    act.wait_ge(s_utr, cc * (2 * LEVELS - 2) + (2 * lv + gr + 1))
                    a.activation(flat(dst, gr), grp(2 * gr), ACT.Copy).then_inc(s_u, 1)

            def level_x(cc, lv):
                for gr in range(2):
                    act.wait_ge(s_xmm, cc * (2 * LEVELS - 2) + (2 * (lv - 1) + gr + 1))
                    a.activation(flat(Xm, gr), grp(2 * gr), ACT.Copy).then_inc(s_xc, 1)

            def r_o1(cc, guard):
                for gr in range(2):
                    act.wait_ge(s_o1, cc * 2 + (gr + 1))
                    if guard:
                        act.wait_ge(s_ylo, cc * 2)
                    a.activation(flat(om, gr), grp(5 + 2 * gr), ACT.Copy).then_inc(s_o1c, 1)

            def r_v(cc):
                for gr in range(2):
                    act.wait_ge(s_vmm, cc * 2 + (gr + 1))
                    a.activation(flat(Rm, gr), grp(4 + 2 * gr), ACT.Copy).then_inc(s_v, 1)

            def r_sso(cc):
                for gr in range(2):
                    act.wait_ge(s_o, cc * 2 + (gr + 1))
                    for h in range(G3 * gr, G3 * gr + G3):
                        last = a.activation(junk2[:, h, :], om[:, h, :], ACT.Square,
                                            accum_out=sso[:, h:h + 1])
                    last.then_inc(s_sso, 1)

            def r_yhi(cc):
                a.activation(y_hi[:, 0:PT, :], ypool[:, :, bass.ds(cc * P, P)],
                             ACT.Copy).then_inc(s_yhi, 1)
                for gr in range(2):
                    act.wait_ge(s_yf, cc * 2 + (gr + 1))
                    a.activation(y_hi[:, PT + G3 * gr:PT + G3 * gr + G3, :],
                                 om[:, G3 * gr:G3 * gr + G3, :], ACT.Copy).then_inc(s_yhi, 1)

            def r_ssx(cc):
                act.wait_ge(s_h2, cc + 1)
                a.activation(flat(junk2), flat(xt), ACT.Square,
                             accum_out=ssx2[:, 0:1]).then_inc(s_h2sq, 1)

            def r_h2n(cc, bank=4):
                for h in range(2):
                    act.wait_ge(s_htr, cc * 2 + (h + 1))
                    a.activation(h2n_f[:, 4 * h:4 * h + 4, bass.ds(cc * P, P)],
                                 ps[:, bank + 2 * h, :].rearrange("p (k n) -> p k n", k=4),
                                 ACT.Copy).then_inc(s_h2n, 1)

            def body(cc, s, dma, first=False):
                if not first:
                    r_ssx(cc - 2)
                p_exp(cc)
                p_kbT(cc, s)
                if not first:
                    r_h2n(cc - 2)
                level_u(cc, s, 0)
                r_o1(cc - 1, not first)
                level_x(cc, 1)
                r_v(cc - 1)
                level_u(cc, s, 1)
                level_x(cc, 2)
                r_sso(cc - 1)
                level_u(cc, s, 2)
                level_x(cc, 3)
                level_u(cc, s, 3)
                r_yhi(cc - 1)
                if dma is not None:
                    squares(cc + 1, 1 - s, dma)
                for lv in range(4, LEVELS):
                    level_x(cc, lv)
                    if lv < LEVELS - 1:
                        level_u(cc, s, lv)

            def wo_hi_copy(k):
                act.wait_ge(s_wog, k + 1)
                a.activation(wo_hi[:, k, :], wo_raw[:, k, :], ACT.Copy).then_inc(s_wohi, 1)

            z_tile(3)
            squares(None, 0, 16)
            z_tile(4)
            z_tile(5)
            p_exp(0)
            p_kbT(0, 0)
            level_u(0, 0, 0)
            for lv in range(1, LEVELS):
                level_x(0, lv)
                if lv < LEVELS - 1:
                    level_u(0, 0, lv)
                if lv == 3:
                    squares(1, 1, 16)
                for k in range(max(2 * lv - 5, 0), min(max(2 * lv - 3, 0), KT)):
                    wo_hi_copy(k)
            body(1, 1, 32, True)
            body(2, 0, 32)
            with act.Fori(1, 3) as i:
                body(i * 2 + 1, 1, i * 16 + 32)
                body(i * 2 + 2, 0, i * 16 + 32)
            body(7, 1, None)
            r_ssx(6)
            r_o1(7, True)
            r_v(7)
            r_h2n(6, 0)
            r_sso(7)
            r_yhi(7)
            r_ssx(7)
            r_h2n(7)

            def f_hi(k):
                act.wait_ge(s_f_hf, k + 1)
                a.activation(h2n_hi[:, k, :], h2n_f[:, k, :], ACT.Copy).then_inc(s_f_hi, 1)

            def u_hi_copy(s, dma):
                act.wait_ge(s_u_ld[s], dma)
                a.activation(u_hi[s][:, :, :], u_raw[s][:, :, :], ACT.Copy).then_inc(s_uhi, 1)

            u_hi_copy(0, 16)
            u_hi_copy(1, 16)
            for k in range(KT):
                f_hi(k)
            u_hi_copy(2, 16)
            u_hi_copy(3, 16)

            def silu(f, guard):
                act.wait_ge(s_gu, f + 1)
                if guard:
                    act.wait_ge(s_hid, f)
                a.activation(silu_t[:, :], bank2(silu.b), ACT.Silu).then_inc(s_sil, 1)

            silu.b = 0
            act.wait_ge(s_h2, NC)
            silu(0, False)
            u_hi_copy(0, 32)
            u_hi_copy(1, 32)
            silu.b = 4
            silu(1, True)
            u_hi_copy(2, 32)
            u_hi_copy(3, 32)
            with act.Fori(1, FT // 2 - 1) as i:
                silu.b = 0
                silu(i * 2, True)
                u_hi_copy(0, i * 16 + 32)
                u_hi_copy(1, i * 16 + 32)
                silu.b = 4
                silu(i * 2 + 1, True)
                u_hi_copy(2, i * 16 + 32)
                u_hi_copy(3, i * 16 + 32)
            silu.b = 0
            silu(FT - 2, True)

            def d_hi_copy(k, h, s, dma, used):
                act.wait_ge(s_d_ld[s], dma)
                if used is not None:
                    act.wait_ge(s_down, used)
                a.activation(d_hi[s][:, :], d_raw[s][:, :], ACT.Copy)
                a.activation(a_hi[s][:, :], hid[:, bass.ds(k, 1), h * HALF:(h + 1) * HALF].rearrange(
                    "p a n -> p (a n)"), ACT.Copy).then_inc(s_dhi, 1)

            d_hi_copy(0, 0, 0, 16, None)
            silu.b = 4
            silu(FT - 1, True)
            act.wait_ge(s_hid, FT)
            for n in range(1, 4):
                d_hi_copy(n, 0, n, 16, None)
            with act.Fori(1, 5) as i:
                for j in range(4):
                    d_hi_copy(i * 4 + j, 0, j, i * 16 + 16, i * 4 + (j - 3))
            for n in range(20, 24):
                d_hi_copy(n % FT, n // FT, n % 4, 16 * (n // 4 + 1), n - 3)

            def out_sq(t):
                act.wait_ge(s_fh, t + 1)
                a.activation(fjunk[:, :], h_re[t % 4][:, :], ACT.Square,
                             accum_out=ssf[:, t:t + 1]).then_inc(s_fsq, 1)

            for n in range(24, 28):
                d_hi_copy(n - FT, 1, n % 4, 16 * (n // 4 + 1), n - 3)
            for t in range(4):
                if t > 0:
                    act.wait_ge(s_fsq, t)
                out_sq(t)
            with act.Fori(7, 11) as i:
                for j in range(4):
                    d_hi_copy(i * 4 + (j - 22), 1, j, i * 16 + 16, i * 4 + (j - 3))
            for t in range(4, 8):
                act.wait_ge(s_fsq, t)
                out_sq(t)

        @block.vector
        def _(dve):
            v = nc.vector
            ch = Chain(dve, s_dve_chain)
            dve.wait_ge(s_rows_tr, 1)
            v.tensor_copy(cols_a[:, :], ps[:, 6, 0:SMALL_A])
            v.tensor_copy(cols_b[:, :], ps[:, 6, P:P + SMALL_B]).then_inc(s_cols, 1)
            for t in range(NC):
                dve.wait_ge(s_xsq, t + 1)
                v.tensor_scalar(ssx[:, t:t + 1], ssx[:, t:t + 1], 1.0 / D_MODEL, EPS,
                                ALU.mult, ALU.add).then_inc(s_ss, 1)
                dve.wait_ge(s_rst, t + 1)
                v.tensor_scalar(x_sl[t][:, :], x_sl[t][:, :], rst[:, t:t + 1], None,
                                ALU.mult).then_inc(s_xn, 1)
            dve.wait_ge(s_cs, 1)
            for k in range(KT):
                dve.wait_ge(s_adam[k % 6], 16 * (k // 6 + 1))
                ccol = cols_a[:, CA_C + k:CA_C + k + 1]
                if k == 0:
                    v.tensor_scalar(ada_acc[:, 0:2 * D_MODEL], ada_m[0][:, :], ccol, None,
                                    ALU.mult).then_inc(s_ada_used, 1)
                else:
                    dve.wait_ge(s_ada_used, k)
                    v.scalar_tensor_tensor(out=ada_acc[:, 0:2 * D_MODEL], in0=ada_m[k % 6][:, :],
                                           scalar=ccol, in1=ada_acc[:, 0:2 * D_MODEL],
                                           op0=ALU.mult, op1=ALU.add).then_inc(s_ada_used, 1)

            def modulation(mc, gc, base, gain, waitv):
                dve.wait_ge(s_ada_mm, waitv)
                ch.link(v.tensor_tensor(mc[:, :], ps[:, 7, 0:2 * KT],
                                        cols_a[:, CA_B + base:CA_B + base + 2 * KT], ALU.add))
                ch.link(v.scalar_tensor_tensor(out=gc[:, :], in0=mc[:, KT:2 * KT], scalar=1.0,
                                               in1=cols_a[:, gain:gain + KT], op0=ALU.add,
                                               op1=ALU.mult))

            def modulate(hf, hl, hh, mc, gc, s_f, s_h, s_l):
                for k in range(KT + 1):
                    if k < KT:
                        v.tensor_scalar(hf[:, k, :], hf[:, k, :], gc[:, k:k + 1], mc[:, k:k + 1],
                                        ALU.mult, ALU.add).then_inc(s_f, 1)
                    if k > 0:
                        dve.wait_ge(s_h, k)
                        v.tensor_tensor(hl[:, k - 1, :], hf[:, k - 1, :],
                                        hh[:, k - 1, :].bitcast(F32),
                                        ALU.subtract).then_inc(s_l, 1)

            modulation(mcol, gcol, 0, CA_GM, 1)
            dve.wait_ge(s_xev, NC)
            modulate(hn_f, hn_lo, hn_hi, mcol, gcol, s_hf, s_hhi, s_hlo)

            dve.wait_ge(s_const, 2)
            for t in range(PT):
                dve.wait_ge(s_evac, t + 1)
                u = seqb[t]
                cur = u
                rows = slice(0, P)
                done = {}
                for n, sh in enumerate((1, 2) if t == 0 else (1, 2, 4, 8)):
                    dst = acc[n % 2]
                    w = 2 * sh
                    r = rows if w <= WINDOWS[2 * t] else slice(64, P)
                    lo = w - 1
                    ch.link(v.tensor_tensor(dst[r, lo:SW], cur[r, lo:SW], cur[r, lo - sh:SW - sh],
                                            ALU.add))
                    cur = dst
                    for hf in range(2):
                        if WINDOWS[2 * t + hf] == w:
                            done[hf] = dst
                for hf in range(2):
                    w = WINDOWS[2 * t + hf]
                    r = slice(64 * hf, 64 * hf + 64)
                    s_ = done[hf]
                    v.scalar_tensor_tensor(out=ypool[r, t, PAD:SEQ], in0=s_[r, 2 * PAD:SW],
                                           scalar=1.0 / w, in1=u[r, 2 * PAD:SW], op0=ALU.mult,
                                           op1=ALU.subtract)
                    ch.link(v.tensor_tensor(ypool[r, t, 0:PAD], s_[r, PAD:2 * PAD],
                                            rcnt[r, t, :], ALU.mult))
                    last = v.tensor_tensor(ypool[r, t, 0:PAD], ypool[r, t, 0:PAD],
                                           u[r, PAD:2 * PAD], ALU.subtract)
                    if hf == 0:
                        ch.link(last)
                last.then_inc(s_seq, 1)
            dve.wait_ge(s_batr, 1)
            v.tensor_copy(ba[:, :, :], ps[:, 6, 0:32 * NC].rearrange(
                "p (c r) -> p c r", r=32)[:, :, BA_ROW:BA_ROW + 2 * HEADS]).then_inc(s_seq, 1)

            def conv(n, dyn):
                slot, o = (n + 1) % 2, n % 2
                t = dyn + (T0 + 1)
                dve.wait_ge(s_evac, t)
                if conv.guard is not None:
                    dve.wait_ge(s_aout, conv.guard)
                src, dst = seqb[slot], acc[o]

                cb = cols_b
                for j in (3, 2, 1, 0):
                    col = cb[:, bass.ds(dyn + j * QKVT, 1)]
                    s_ = src[:, PAD - 3 + j:PAD - 3 + j + SEQ]
                    if j == 3:
                        ch.link(v.tensor_scalar(dst[:, 0:SEQ], s_, col, None, ALU.mult))
                    else:
                        last = v.scalar_tensor_tensor(out=dst[:, 0:SEQ], in0=s_, scalar=col,
                                                      in1=dst[:, 0:SEQ], op0=ALU.mult,
                                                      op1=ALU.add)
                        if j > 0:
                            ch.link(last)
                last.then_inc(s_conv, 1)

            def ada_rest(k, first):
                ccol = cols_a[:, bass.ds(k + CA_C, 1)]
                for s in range(2):
                    dst = ada_acc[:, 2 * s * D_MODEL:2 * (s + 1) * D_MODEL]
                    dve.wait_ge(s_ada[s], k * 16 + 32)
                    if first:
                        v.tensor_scalar(dst, ada_w[s][:, :], ccol, None,
                                        ALU.mult).then_inc(s_ada_used, 1)
                    else:
                        dve.wait_ge(s_ada_used, k * 2 + (KT - 1 + s))
                        v.scalar_tensor_tensor(out=dst, in0=ada_w[s][:, :], scalar=ccol, in1=dst,
                                               op0=ALU.mult, op1=ALU.add).then_inc(s_ada_used, 1)

            aa = ba[:, :, HEADS:2 * HEADS]
            dve.wait_ge(s_x, 128)
            dve.wait_ge(s_seq, PT + 1)
            ch.link(v.tensor_tensor(spt[:, 1, :, :], aa,
                                    dt_b[:, :].unsqueeze(1).to_broadcast([P, NC, HEADS]), ALU.add))
            ch.link(v.tensor_scalar(spt[:, 2, :, :], spt[:, 1, :, :], -1.0, None, ALU.mult))
            v.tensor_tensor(spt[:, 0, :, :], spt[:, 1, :, :], spt[:, 2, :, :],
                            ALU.max).then_inc(s_sp, 1)
            conv.guard = None
            conv(0, 0)
            dve.wait_ge(s_spa, 3)
            ch.link(v.tensor_scalar(allsc[:, :, S_BETA, :], allsc[:, :, S_BETA, :], 1.0, None,
                                    ALU.add))
            ch.link(v.reciprocal(allsc[:, :, S_BETA, :], allsc[:, :, S_BETA, :]))
            v.tensor_scalar(spt[:, 0, :, :], spt[:, 0, :, :], 1.0, None, ALU.add).then_inc(s_sp, 1)
            ch.link(v.tensor_scalar(spt[:, 1, :, :], spt[:, 1, :, :], 0.0, None, ALU.max))
            conv(1, 1)
            dve.wait_ge(s_spa, 4)
            ch.link(v.tensor_tensor(spt[:, 2, :, :], spt[:, 1, :, :], spt[:, 0, :, :], ALU.add))
            ch.link(v.tensor_tensor(spt[:, 1, :, :], spt[:, 2, :, :],
                                    al_b[:, :].unsqueeze(1).to_broadcast([P, NC, HEADS]),
                                    ALU.mult))
            ch.link(v.tensor_scalar(spt[:, 0, :, :], spt[:, 1, :, :], -1.0, None, ALU.mult))
            v.tensor_copy(allsc[:, :, S_G, :], spt[:, 0, :, :]).then_inc(s_sp, 1)
            ada_rest(0, True)
            with dve.Fori(1, 8) as i:
                ch.enter(i - 1, 6)
                for j in range(2):
                    conv.guard = i * 2 + (j - 1)
                    conv(j, i * 2 + j)
                ada_rest(i, False)
            ch.leave(7, 6)
            for n in (16, 17):
                conv.guard = n - 1
                conv(n, n)
            modulation(fcol, gcol_f, 3 * KT, CA_GF, 2)
            dve.wait_ge(s_x, 128)
            for gt, gate in enumerate((gate_m, gate_f)):
                dve.wait_ge(s_gmm, gt + 1)
                v.tensor_tensor(gate[:, :], gate[:, :], bank2(4), ALU.add).then_inc(s_gev, 1)
            dve.wait_ge(s_pmm, 2)
            v.tensor_scalar(ssf[:, 0:NC], ps[:, 4, 0:NC], 1.0 / POOL_W, EPS, ALU.mult,
                            ALU.add).then_inc(s_pst, 1)
            dve.wait_ge(s_pmm, 3)
            for t in range(PT):
                v.scalar_tensor_tensor(out=ypool[:, t, :], in0=ypool[:, t, :],
                                              scalar=cols_b[:, CB_PS + t:CB_PS + t + 1],
                                              in1=bank2(6), op0=ALU.mult, op1=ALU.mult)
            def square_sums(bank=3):
                v.tensor_scalar(ssb[:, :], ps[:, bank, GW:GW + 2 * HEADS], EPS, None,
                                ALU.add).then_inc(s_ssr, 1)

            def scalars(cc, s):
                rk = rr[s][:, HEADS:2 * HEADS]
                rq = rr[s][:, 0:HEADS]
                ch.link(v.tensor_copy(sc[s][:, :, :], allsc[:, bass.ds(cc, 1), :, :].rearrange(
                    "p a b h -> p (a b) h")))
                dve.wait_ge(s_rr, cc + 1)
                v.scalar_tensor_tensor(out=nbk[:, :], in0=rk, scalar=-1.0,
                                       in1=sc[s][:, S_BETA, :], op0=ALU.mult, op1=ALU.mult)
                ch.link(v.tensor_tensor(kdec[:, :], rk, sc[s][:, S_ED, :], ALU.mult))
                v.scalar_tensor_tensor(out=rq2[s][:, :], in0=rq,
                                       scalar=1.0 / HD, in1=rq, op0=ALU.mult,
                                       op1=ALU.mult).then_inc(s_scc, 1)

            def p_k(cc, s):
                for gr in range(2):
                    dve.wait_ge(s_ktr, cc * 2 + (gr + 1))
                    v.tensor_tensor(kb[:, G3 * gr:G3 * gr + G3, :], grp3(2 * gr), bc(nbk, gr),
                                    ALU.mult).then_inc(s_kbd, 1)
                for gr in range(2):
                    v.tensor_tensor(Kd[s][:, G3 * gr:G3 * gr + G3, :], grp3(2 * gr),
                                    bc(kdec, gr), ALU.mult).then_inc(s_kdd, 1)

            def p_vb(cc, s):
                for gr in range(2):
                    dve.wait_ge(s_vtr, cc * 2 + (gr + 1))
                    v.tensor_tensor(Vb[s][:, G3 * gr:G3 * gr + G3, :], grp3(2 * gr + 1),
                                    bc(sc[s][:, S_BETA, :], gr), ALU.mult).then_inc(s_vb, 1)

            def p_na(cc, s):
                for gr in range(2):
                    dve.wait_ge(s_qk, cc * 2 + (gr + 1))
                    dve.wait_ge(s_e, cc * 2 + (gr + 1))
                    v.tensor_tensor(flat(QD[s], gr), grp(5 + 2 * gr), flat(Em, gr),
                                    ALU.mult).then_inc(s_qd, 1)
                for gr in range(2):
                    dve.wait_ge(s_kk, cc * 2 + (gr + 1))
                    dve.wait_ge(s_ti, cc + 1)
                    v.tensor_tensor(flat(NA, gr), grp(2 * gr), flat(Em, gr),
                                    ALU.mult).then_inc(s_na, 1)

            def masked(dst, gr, lv, src):
                h = slice(G3 * gr, G3 * gr + G3)
                return v.copy_predicated(dst[:, h, :],
                                         lmask[:, lv, :].bitcast(I16).unsqueeze(1).to_broadcast(
                                             [P, G3, P]), src)

            def level_u0(cc, s):
                for gr in range(2):
                    count = settled(dve, cc * 2 + (gr + 1))
                    dve.wait_ge(s_const, 2)
                    dve.wait_ge(s_na, count)
                    masked(Um[s], gr, 0, NA[:, G3 * gr:G3 * gr + G3, :]).then_inc(s_uz, 1)

            def level_t(cc, s, lv, sums=False):
                for gr in range(2):
                    if sums and gr == 1:
                        dve.wait_ge(s_y, cc * (2 * LEVELS - 2) + (2 * lv))
                        square_sums()
                    count = settled(dve, cc * (2 * LEVELS - 2) + (2 * lv + gr - 1))
                    dve.wait_ge(s_const, 2)
                    dve.wait_ge(s_y, count)
                    if lv < LEVELS - 1:
                        masked(Tm, gr, lv, grp3(2 * gr + 1)).then_inc(s_t, 1)
                    else:
                        masked(Um[s], gr, lv, grp3(2 * gr + 1)).then_inc(s_uf, 1)

            def r_rhs(cc, s):
                for gr in range(2):
                    dve.wait_ge(s_ks, cc * 2 + (gr + 1))
                    for n in range(G3):
                        h = G3 * gr + n
                        last = v.scalar_tensor_tensor(
                            out=Rm[:, h, :], in0=ps[:, 4 + 2 * gr, n * P:(n + 1) * P],
                            scalar=sc[s][:, S_EG, h:h + 1], in1=Vb[s][:, h, :],
                            op0=ALU.mult, op1=ALU.add)
                    last.then_inc(s_r, 1)

            def r_state(cc, s):
                for gr in range(2 if cc is not NC - 1 else 0):
                    dve.wait_ge(s_sd, cc * 2 + (gr + 1))
                    for n in range(G3):
                        h = G3 * gr + n
                        last = v.scalar_tensor_tensor(
                            out=Sm[:, h, :], in0=Sm[:, h, :], scalar=sc[s][:, S_EL, h:h + 1],
                            in1=ps[:, 4 + 2 * gr, n * P:(n + 1) * P], op0=ALU.mult, op1=ALU.add)
                    last.then_inc(s_s, 1)
                for gr in range(2):
                    dve.wait_ge(s_o2, cc * 2 + (gr + 1))
                    for n in range(G3):
                        h = G3 * gr + n
                        last = v.scalar_tensor_tensor(
                            out=om[:, h, :], in0=om[:, h, :], scalar=sc[s][:, S_EG, h:h + 1],
                            in1=ps[:, 5 + 2 * gr, n * P:(n + 1) * P], op0=ALU.mult, op1=ALU.add)
                    last.then_inc(s_o, 1)

            def r_on(cc, s):
                dve.wait_ge(s_sso, cc * 2 + 2)
                ch.link(v.tensor_tensor(oc[:, 0, :], sso[:, :], rq2[s][:, :], ALU.mult))
                v.tensor_tensor(oc[:, 1, :], oc[:, 0, :], epsh[:, :], ALU.add).then_inc(s_oss, 1)
                dve.wait_ge(s_ort, cc + 1)
                ch.link(v.tensor_tensor(oc[:, 3, :], oc[:, 2, :], rr[s][:, 0:HEADS], ALU.mult))
                for gr in range(2):
                    o = om[:, G3 * gr:G3 * gr + G3, :]
                    v.tensor_tensor(o, o, bc(oc[:, 3, :], gr), ALU.mult).then_inc(s_on, 1)

            def r_y(cc, s, z_dma):
                dve.wait_ge(s_stz[s], z_dma)
                for gr in range(2):
                    dve.wait_ge(s_otr, cc * 2 + (gr + 1))
                    z = stage[s][:, QKVT + G3 * gr:QKVT + G3 * gr + G3, :].rearrange(
                        "p h n -> p (h n)")
                    v.scalar_tensor_tensor(out=flat(om, gr), in0=grp(5 + 2 * gr),
                                           scalar=cols_b[:, CB_GG:CB_GG + 1], in1=z,
                                           op0=ALU.mult, op1=ALU.mult).then_inc(s_yf, 1)
                dve.wait_ge(s_yhi, cc * 3 + 1)
                v.tensor_tensor(y_lo[:, 0:PT, :], ypool[:, :, bass.ds(cc * P, P)],
                                y_hi[:, 0:PT, :].bitcast(F32), ALU.subtract)
                for gr in range(2):
                    dve.wait_ge(s_yhi, cc * 3 + (gr + 2))
                    r = slice(PT + G3 * gr, PT + G3 * gr + G3)
                    v.tensor_tensor(y_lo[:, r, :], om[:, G3 * gr:G3 * gr + G3, :],
                                    y_hi[:, r, :].bitcast(F32), ALU.subtract).then_inc(s_ylo, 1)

            def r_h2(cc):
                dve.wait_ge(s_op, cc + 1)
                dve.wait_ge(s_xin, cc * 16 + 16)
                x_ = flat(xt)
                v.tensor_tensor(x_[:, 0:HALF], ps[:, 4, :], x_[:, 0:HALF], ALU.add)
                v.tensor_tensor(x_[:, HALF:], ps[:, 6, :], x_[:, HALF:],
                                ALU.add).then_inc(s_h2, 1)

            def r_xn(cc):
                dve.wait_ge(s_h2sq, cc + 1)
                v.tensor_scalar(ssx2[:, 1:2], ssx2[:, 0:1], 1.0 / D_MODEL, EPS, ALU.mult,
                                ALU.add).then_inc(s_ssx2, 1)
                dve.wait_ge(s_rst2, cc + 1)
                v.tensor_scalar(flat(xn2), flat(xt), rst2[:, 0:1], None,
                                ALU.mult).then_inc(s_xn2, 1)

            def body(cc, s, z_dma, first=False, last=False):
                p_k(cc, s)
                if not first:
                    r_xn(cc - 2)
                p_na(cc, s)
                level_u0(cc, s)
                p_vb(cc, s)
                r_rhs(cc - 1, 1 - s)
                level_t(cc, s, 1)
                r_state(cc - 1, 1 - s)
                level_t(cc, s, 2)
                r_on(cc - 1, 1 - s)
                level_t(cc, s, 3)
                r_y(cc - 1, 1 - s, z_dma)
                level_t(cc, s, 4, not last)
                level_t(cc, s, 5)
                if not last:
                    scalars(cc + 1, 1 - s)
                r_h2(cc - 1)
                level_t(cc, s, 6)

            dve.wait_ge(s_sums0, 1)
            square_sums(5)
            dve.wait_ge(s_ex, 1)
            scalars(0, 0)
            v.memset(Sm[:, :, :], 0.0).then_inc(s_scr, 1)

            def wo_lo_sub(k):
                dve.wait_ge(s_wohi, k + 1)
                v.tensor_tensor(wo_lo[:, k, :], wo_raw[:, k, :], wo_hi[:, k, :].bitcast(F32),
                                ALU.subtract).then_inc(s_wosp, 1)

            p_k(0, 0)
            p_na(0, 0)
            level_u0(0, 0)
            p_vb(0, 0)
            for lv in range(1, LEVELS):
                level_t(0, 0, lv, lv == 4)
                if lv == 5:
                    scalars(1, 1)
                for k in range(max(2 * lv - 7, 0), max(2 * lv - 5, 0)):
                    wo_lo_sub(k)
            wo_lo_sub(KT - 1)
            PER = 2 * 4
            body(1, 1, 16, first=True)
            body(2, 0, 16)
            with dve.Fori(1, 3) as i:
                ch.enter(i - 1, PER)
                body(i * 2 + 1, 1, i * 16 + 16)
                body(i * 2 + 2, 0, i * 16 + 16)
            ch.leave(2, PER)
            body(7, 1, 64, last=True)
            r_rhs(7, 1)
            r_xn(6)
            r_state(7, 1)
            r_on(7, 1)
            r_y(7, 1, 64)
            r_h2(7)
            r_xn(7)

            def u_lo_sub(s, n):
                dve.wait_ge(s_uhi, n)
                v.tensor_tensor(u_lo[s][:, :, :], u_raw[s][:, :, :],
                                u_hi[s][:, :, :].bitcast(F32), ALU.subtract).then_inc(s_ulo, 1)

            u_lo_sub(0, 1)
            u_lo_sub(1, 2)
            dve.wait_ge(s_h2n, 2 * NC)
            modulate(h2n_f, h2n_lo, h2n_hi, fcol, gcol_f, s_f_hf, s_f_hi, s_f_lo)
            u_lo_sub(2, 3)
            u_lo_sub(3, 4)

            def hidden(f, b):
                dve.wait_ge(s_sil, f + 1)
                v.tensor_tensor(hid[:, bass.ds(f, 1), :].rearrange("p a n -> p (a n)"),
                                silu_t[:, :], bank2(b + 2), ALU.mult).then_inc(s_hid, 1)

            with dve.Fori(0, FT // 2 - 1) as i:
                hidden(i * 2, 0)
                u_lo_sub(0, i * 4 + 5)
                u_lo_sub(1, i * 4 + 6)
                hidden(i * 2 + 1, 4)
                u_lo_sub(2, i * 4 + 7)
                u_lo_sub(3, i * 4 + 8)
            hidden(FT - 2, 0)

            def d_lo_sub(k, h, s, n):
                dve.wait_ge(s_dhi, n)
                v.tensor_tensor(d_lo[s][:, :], d_raw[s][:, :], d_hi[s][:, :].bitcast(F32),
                                ALU.subtract)
                v.tensor_tensor(a_lo[s][:, :],
                                hid[:, bass.ds(k, 1), h * HALF:(h + 1) * HALF].rearrange(
                                    "p a n -> p (a n)"), a_hi[s][:, :].bitcast(F32),
                                ALU.subtract).then_inc(s_dlo, 1)

            d_lo_sub(0, 0, 0, 1)
            hidden(FT - 1, 4)
            for n in range(1, 4):
                d_lo_sub(n, 0, n, n + 1)
            with dve.Fori(1, 5) as i:
                for j in range(4):
                    d_lo_sub(i * 4 + j, 0, j, i * 4 + (j + 1))
            for n in range(20, 24):
                d_lo_sub(n % FT, n // FT, n % 4, n + 1)
            dve.wait_ge(s_fg, 16)


            def residual(t):
                if t % 4 < 3:
                    dve.wait_ge(s_dmm, 3 * (t // 4) + t % 4 + 1)
                else:
                    dve.wait_ge(s_down, FT * (t // 4 + 1))
                if t >= 4:
                    dve.wait_ge(s_out, 16 * 4)
                v.tensor_tensor(fin[t % 4][:, :], bank2(2 * (t % 4)), gate_f[:, :],
                                ALU.mult).then_inc(s_dev, 1)
                dve.wait_ge(s_dev, t + 1)
                dve.wait_ge(s_hre[t % 4], 16 * (t // 4 + 1))
                v.tensor_tensor(h_re[t % 4][:, :], h_re[t % 4][:, :], fin[t % 4][:, :],
                                ALU.add).then_inc(s_fh, 1)

            def finish(t):
                dve.wait_ge(s_fsq, t + 1)
                v.tensor_scalar(ssf[:, t:t + 1], ssf[:, t:t + 1], 1.0 / D_MODEL, EPS,
                                ALU.mult, ALU.add).then_inc(s_fss, 1)
                dve.wait_ge(s_frs, t + 1)
                v.scalar_tensor_tensor(out=fin[t % 4][:, :], in0=h_re[t % 4][:, :],
                                       scalar=ssf[:, NC + t:NC + t + 1], in1=fgain[:, :],
                                       op0=ALU.mult, op1=ALU.mult).then_inc(s_fin, 1)

            for t in range(4):
                residual(t)
            for n in range(24, 28):
                d_lo_sub(n - FT, 1, n % 4, n + 1)
            for t in range(4):
                finish(t)
            with dve.Fori(7, 11) as i:
                for j in range(4):
                    d_lo_sub(i * 4 + (j - 22), 1, j, i * 4 + (j + 1))
            residual(4)
            for t in range(5, NC):
                residual(t)
                finish(t - 1)
            finish(NC - 1)

        @block.tensor
        def _(pe):
            t_ = nc.tensor
            pe.wait_ge(s_small, 16 * 7)
            pe.wait_ge(s_const, 1)
            t_.transpose(ps[:, 6, 0:SMALL_A], rows_a[0:SMALL_A, :], ident[0:SMALL_A, 0:SMALL_A])
            t_.transpose(ps[:, 6, P:P + SMALL_B], rows_b[0:SMALL_B, :],
                         ident[0:SMALL_B, 0:SMALL_B]).then_inc(s_rows_tr, 1)
            for t in range(NC):
                pe.wait_ge(s_xn, t + 1)
                if t >= 2:
                    pe.wait_ge(s_xev, t - 1)
                for k in range(KT):
                    last = t_.transpose(bank2(2 * (t % 2))[:, k * P:(k + 1) * P],
                                        x_sl[t][:, k * P:(k + 1) * P], ident[:, :])
                last.then_inc(s_xtr, 1)

            def ada_columns(base):
                for n in range(2 * KT):
                    last = t_.matmul(ps[:, 7, n:n + 1],
                                     ada_acc[:, base + n * P:base + (n + 1) * P],
                                     ones[:, 0:1], start=True, stop=True)
                last.then_inc(s_ada_mm, 1)

            pe.wait_ge(s_ada_used, KT)
            ada_columns(0)

            def project(slot, bank, hi, lo):
                for k in range(KT):
                    if project.first:
                        pe.wait_ge(s_hlo, k + 1)
                    for n, (w, h) in enumerate(((w_lo, hi), (w_hi, lo), (w_hi, hi))):
                        for b in range(2):
                            last = t_.matmul(ps[:, bank + b, :], w[slot][:, k, :],
                                             h[:, k, b * HALF:(b + 1) * HALF],
                                             start=(k == 0 and n == 0),
                                             stop=(k == KT - 1 and n == 2))
                project.first = False
                last.then_inc(s_proj, 1)

            project.first = True
            for t in range(T0):
                pe.wait_ge(s_wsplit, t + 1)
                if t >= 2:
                    pe.wait_ge(s_evac, t - 1)
                elif t == 0:
                    pe.wait_ge(s_xev, NC)
                project(t, 2 * (t % 2), hn_hi, hn_lo)
            pe.wait_ge(s_evac, 3)
            for cc in range(NC):
                last = t_.transpose(ps[:, 6, 32 * cc:32 * cc + 32],
                                    seqb[0][0:32, PAD + cc * P:PAD + (cc + 1) * P],
                                    ident[0:32, 0:32])
            last.then_inc(s_batr, 1)

            def tile(t):
                pe.wait_ge(s_wsplit, t + 1)
                pe.wait_ge(s_evac, t - 1)
                project(t % 4, 2 * (t % 2), hn_hi, hn_lo)

            for t in range(T0, T0 + 4):
                tile(t)
            pe.wait_ge(s_sp, 3)
            n48 = NC * HEADS
            for n, m in enumerate((tri, below, ones)):
                last = t_.matmul(ps[:, 6, n * n48:(n + 1) * n48], m[:, :],
                                 spt[:, 0, :, :].rearrange("p c h -> p (c h)"),
                                 start=True, stop=True)
            last.then_inc(s_gmx, 1)
            with pe.Fori(1, 4) as i:
                for j in range(4):
                    pe.wait_ge(s_wsplit, i * 4 + (T0 + j + 1))
                    pe.wait_ge(s_evac, i * 4 + (T0 + j - 1))
                    project((T0 + j) % 4, 2 * ((T0 + j) % 2), hn_hi, hn_lo)
            TZ = T0 + QKVT
            for t in range(T0 + 16, TZ + 1):
                tile(t)
            pe.wait_ge(s_ada_used, 3 * KT)
            ada_columns(D_MODEL)
            def gate(gt):
                for b in range(2):
                    last = t_.matmul(ps[:, 4 + b, :], ones[:, :],
                                     ada_acc[:, gt * 3 * D_MODEL + b * HALF:
                                             gt * 3 * D_MODEL + (b + 1) * HALF],
                                     start=True, stop=True)
                last.then_inc(s_gmm, 1)

            gate(0)
            tile(TZ + 1)
            pe.wait_ge(s_gev, 1)
            gate(1)
            tile(TZ + 2)
            pe.wait_ge(s_gev, 2)
            pe.wait_ge(s_ex, 1)
            pe.wait_ge(s_x, 128)
            for t in range(PT):
                for b in range(2):
                    last = t_.matmul(ps[:, 4 + 2 * t + b, :], wpb[:, t, :],
                                     ypool[:, t, b * HALF:(b + 1) * HALF], start=True, stop=True)
            last.then_inc(s_pmm, 1)
            tile(TZ + 3)
            pe.wait_ge(s_pss, PT)
            for n in range(NC):
                for t in range(PT):
                    last = t_.matmul(ps[:, 4, n:n + 1],
                                     mixed_sq[:, t, n * P:(n + 1) * P], ones[:, 0:1],
                                     start=(t == 0), stop=(t == PT - 1))
            last.then_inc(s_pmm, 1)
            tile(TZ + 4)
            pe.wait_ge(s_psq, 1)
            for n in range(NC):
                last = t_.matmul(bank2(6)[:, n * P:(n + 1) * P],
                                 ssf[:, NC + n:NC + n + 1].to_broadcast([P, P]), ident[:, :],
                                 start=True, stop=True)
            last.then_inc(s_pmm, 1)

            def square_sums(cc, bank=3):
                pe.wait_ge(s_sq, cc + 1)
                for h in range(2 * HEADS):
                    src = Rm if h < HEADS else Em
                    last = t_.matmul(ps[:, bank, GW + h:GW + h + 1], src[:, h % HEADS, :],
                                     ones[:, 0:1], start=True, stop=True)
                return last

            def p_arg(cc):
                for gr in range(2):
                    pe.wait_ge(s_slg, cc * 2 + (gr + 1))
                    for n in range(G3):
                        last = t_.matmul(ps[:, 5 + 2 * gr, n * P:(n + 1) * P],
                                         slg[:, G3 * gr + n, :], tri[:, :], start=True, stop=True)
                    last.then_inc(s_arg, 1)

            def p_ktr(cc, s):
                for gr in range(2):
                    if not (isinstance(cc, int) and cc == 0):
                        pe.wait_ge(s_xc, cc * (2 * LEVELS - 2) + (gr - 1))
                    for n in range(G3):
                        last = t_.transpose(ps[:, 2 * gr, n * P:(n + 1) * P],
                                            stage[s][:, HEADS + G3 * gr + n, :], ident[:, :])
                    last.then_inc(s_ktr, 1)

            def p_qk(cc, s):
                for gr in range(2):
                    pe.wait_ge(s_exp, cc * 2 + (gr + 1))
                    for n in range(G3):
                        h = G3 * gr + n
                        last = t_.matmul(ps[:, 5 + 2 * gr, n * P:(n + 1) * P],
                                         stage[s][:, HEADS + h, :], stage[s][:, h, :],
                                         start=True, stop=True)
                    last.then_inc(s_qk, 1)

            def p_kb(cc):
                for gr in range(2):
                    pe.wait_ge(s_kbd, cc * 2 + (gr + 1))
                    for n in range(G3):
                        last = t_.transpose(ps[:, 2 * gr + 1, n * P:(n + 1) * P],
                                            kb[:, G3 * gr + n, :], ident[:, :])
                    last.then_inc(s_kbtr, 1)

            def p_kk(cc, s):
                for gr in range(2):
                    pe.wait_ge(s_kdd, cc * 2 + (gr + 1))
                    pe.wait_ge(s_kbT, cc * 2 + (gr + 1))
                    for n in range(G3):
                        h = G3 * gr + n
                        last = t_.matmul(ps[:, 2 * gr, n * P:(n + 1) * P],
                                         stage[s][:, HEADS + h, :], KbT[s][:, h, :],
                                         start=True, stop=True)
                    last.then_inc(s_kk, 1)

            def p_vtr(cc, s):
                for gr in range(2):
                    for n in range(G3):
                        last = t_.transpose(ps[:, 2 * gr + 1, n * P:(n + 1) * P],
                                            stage[s][:, 2 * HEADS + G3 * gr + n, :], ident[:, :])
                    last.then_inc(s_vtr, 1)

            def level_0(cc, s):
                for gr in range(2):
                    pe.wait_ge(s_uz, cc * 2 + (gr + 1))
                    for n in range(G3):
                        last = t_.transpose(ps[:, 2 * gr, n * P:(n + 1) * P],
                                            Um[s][:, G3 * gr + n, :], ident[:, :])
                    last.then_inc(s_utr, 1)

            def level_x(cc, lv):
                for gr in range(2):
                    pe.wait_ge(s_u, cc * (2 * LEVELS - 2) + (2 * (lv - 1) + gr + 1))
                    for n in range(G3):
                        h = G3 * gr + n
                        last = t_.matmul(ps[:, 2 * gr, n * P:(n + 1) * P], NA[:, h, :],
                                         Tm[:, h, :], start=True, stop=True)
                    last.then_inc(s_xmm, 1)

            def level_y(cc, s, lv, sums=False):
                for gr in range(2):
                    if sums and gr == 1:
                        square_sums(cc + 1)
                    pe.wait_ge(s_xc, cc * (2 * LEVELS - 2) + (2 * (lv - 1) + gr + 1))
                    if lv == 1:
                        pe.wait_ge(s_vb, cc * 2 + (gr + 1))
                    for n in range(G3):
                        h = G3 * gr + n
                        u_, x_ = Um[s][:, h, :], Xm[:, h, :]
                        if lv == LEVELS - 1:
                            u_, x_ = x_, u_
                        last = t_.matmul(ps[:, 2 * gr + 1, n * P:(n + 1) * P], u_, x_,
                                         start=True, stop=True)
                    last.then_inc(s_y, 1)

            def level_tr(cc, lv):
                for gr in range(2):
                    pe.wait_ge(s_t, cc * (2 * LEVELS - 4) + (2 * (lv - 1) + gr + 1))
                    for n in range(G3):
                        last = t_.transpose(ps[:, 2 * gr, n * P:(n + 1) * P],
                                            Tm[:, G3 * gr + n, :], ident[:, :])
                    last.then_inc(s_utr, 1)

            def r1_ks(cc, s, first, last_chunk=False):
                for gr in range(2):
                    if last_chunk:
                        pe.wait_ge(s_s, cc * 2 + (gr - 1))
                        pe.wait_ge(s_h2, cc)
                    elif not first:
                        pe.wait_ge(s_s, cc * 2 + (gr - 1))
                        pe.wait_ge(s_h2n, cc * 2)
                    for n in range(G3):
                        h = G3 * gr + n
                        last = t_.matmul(ps[:, 4 + 2 * gr, n * P:(n + 1) * P], KbT[s][:, h, :],
                                         Sm[:, h, :], start=True, stop=True)
                    last.then_inc(s_ks, 1)

            def r1_o1(cc, s, last_chunk=False):
                for gr in range(2):
                    if not last_chunk:
                        pe.wait_ge(s_qd, cc * 2 + (gr + 3))
                    for n in range(G3):
                        h = G3 * gr + n
                        last = t_.matmul(ps[:, 5 + 2 * gr, n * P:(n + 1) * P], stage[s][:, h, :],
                                         Sm[:, h, :], start=True, stop=True)
                    last.then_inc(s_o1, 1)

            def r2(cc, s):
                for gr in range(2):
                    pe.wait_ge(s_uf, cc * 2 + (gr + 1))
                    pe.wait_ge(s_r, cc * 2 + (gr + 1))
                    for n in range(G3):
                        h = G3 * gr + n
                        last = t_.matmul(ps[:, 4 + 2 * gr, n * P:(n + 1) * P], Um[s][:, h, :],
                                         Rm[:, h, :], start=True, stop=True)
                    last.then_inc(s_vmm, 1)

            def r3(cc, s, state=True):
                for gr in range(2):
                    pe.wait_ge(s_v, cc * 2 + (gr + 1))
                    for n in range(G3 if state else 0):
                        h = G3 * gr + n
                        last = t_.matmul(ps[:, 4 + 2 * gr, n * P:(n + 1) * P], Kd[s][:, h, :],
                                         Rm[:, h, :], start=True, stop=True)
                    if state:
                        last.then_inc(s_sd, 1)
                for gr in range(2):
                    pe.wait_ge(s_o1c, cc * 2 + (gr + 1))
                    for n in range(G3):
                        h = G3 * gr + n
                        last = t_.matmul(ps[:, 5 + 2 * gr, n * P:(n + 1) * P], QD[s][:, h, :],
                                         Rm[:, h, :], start=True, stop=True)
                    last.then_inc(s_o2, 1)

            def r4(cc):
                for gr in range(2):
                    pe.wait_ge(s_on, cc * 2 + (gr + 1))
                    for n in range(G3):
                        last = t_.transpose(ps[:, 5 + 2 * gr, n * P:(n + 1) * P],
                                            om[:, G3 * gr + n, :], ident[:, :])
                    last.then_inc(s_otr, 1)

            def mix(cc, k):
                if k == 0:
                    pe.wait_ge(s_ylo, cc * 2 + 2)
                    if cc is not mix.last:
                        pe.wait_ge(s_s, cc * 2 + 2)
                if cc is mix.first:
                    pe.wait_ge(s_wosp, k + 1)
                for n, (y, w) in enumerate(((y_lo, wo_hi), (y_hi, wo_lo), (y_hi, wo_hi))):
                    for b in range(2):
                        last = t_.matmul(ps[:, 4 + 2 * b, :], y[:, k, :],
                                         w[:, k, b * HALF:(b + 1) * HALF],
                                         start=(k == 0 and n == 0),
                                         stop=(k == KT - 1 and n == 2))
                if k == KT - 1:
                    last.then_inc(s_op, 1)

            def r6(cc, bank=4):
                pe.wait_ge(s_xn2, cc + 1)
                for h in range(2):
                    for n in range(4):
                        last = t_.transpose(ps[:, bank + 2 * h, n * P:(n + 1) * P],
                                            xn2[:, 4 * h + n, :], ident[:, :])
                    last.then_inc(s_htr, 1)

            def body(cc, s, first=False, last=False):
                p_arg(cc)
                p_ktr(cc, s)
                p_qk(cc, s)
                p_kb(cc)
                p_kk(cc, s)
                p_vtr(cc, s)
                if not first:
                    r6(cc - 2)
                r1_ks(cc - 1, 1 - s, first)
                level_0(cc, s)
                r1_o1(cc - 1, 1 - s)
                level_x(cc, 1)
                r2(cc - 1, 1 - s)
                level_y(cc, s, 1)
                level_tr(cc, 1)
                r3(cc - 1, 1 - s)
                level_x(cc, 2)
                level_y(cc, s, 2)
                level_tr(cc, 2)
                level_x(cc, 3)
                level_y(cc, s, 3)
                r4(cc - 1)
                level_tr(cc, 3)
                for lv in (4, 5):
                    level_x(cc, lv)
                    mix(cc - 1, 3 * lv - 12)
                    level_y(cc, s, lv, lv == 4 and not last)
                    mix(cc - 1, 3 * lv - 11)
                    level_tr(cc, lv)
                    mix(cc - 1, 3 * lv - 10)
                level_x(cc, 6)
                mix(cc - 1, 6)
                mix(cc - 1, 7)
                level_y(cc, s, 6)

            mix.first, mix.last = 0, NC - 1
            square_sums(0, 5).then_inc(s_sums0, 1)
            tile(TZ + 5)
            pe.wait_ge(s_scr, 1)
            p_arg(0)
            pe.wait_ge(s_evac, NT)
            p_ktr(0, 0)
            p_qk(0, 0)
            p_kb(0)
            p_kk(0, 0)
            p_vtr(0, 0)
            level_0(0, 0)
            for lv in range(1, LEVELS):
                level_x(0, lv)
                level_y(0, 0, lv, lv == 4)
                if lv < LEVELS - 1:
                    level_tr(0, lv)
            body(1, 1, first=True)
            body(2, 0)
            with pe.Fori(1, 3) as i:
                body(i * 2 + 1, 1)
                body(i * 2 + 2, 0)
            body(7, 1, last=True)
            r1_ks(7, 1, False, True)
            r1_o1(7, 1, True)
            r2(7, 1)
            r6(6, 0)
            r3(7, 1, False)
            r4(7)
            for k in range(KT):
                mix(7, k)
            r6(7)

            def gate_up(f, b, s0, lo_n, first):
                for up in range(2):
                    pe.wait_ge(s_ulo, lo_n + up)
                    for k in range(KT):
                        if first and up == 0:
                            pe.wait_ge(s_f_lo, k + 1)
                        for n, (w, h) in enumerate(((u_lo, h2n_hi), (u_hi, h2n_lo),
                                                    (u_hi, h2n_hi))):
                            for c2 in range(2):
                                last = t_.matmul(ps[:, b + 2 * up + c2, :],
                                                 w[s0 + up][:, k, :],
                                                 h[:, k, c2 * HALF:(c2 + 1) * HALF],
                                                 start=(k == 0 and n == 0),
                                                 stop=(k == KT - 1 and n == 2))
                last.then_inc(s_gu, 1)

            gate_up(0, 0, 0, 1, True)
            pe.wait_ge(s_h2n, 2 * NC)
            gate_up(1, 4, 2, 3, False)
            with pe.Fori(1, FT // 2) as i:
                for j in range(2):
                    pe.wait_ge(s_hid, i * 2 + (j - 1))
                    gate_up(i * 2 + j, 4 * j, 2 * j, i * 4 + (2 * j + 1), False)

            def down(n, s, first, last_k, waits):
                pe.wait_ge(s_dlo, n + 1)
                for tt in range(4):
                    if first and waits is None and tt == 2:
                        pe.wait_ge(s_hid, FT)
                    if waits is not None:
                        pe.wait_ge(s_dev, waits + tt)
                    for m, (h, w) in enumerate(((a_lo, d_hi), (a_hi, d_lo), (a_hi, d_hi))):
                        for b in range(2):
                            ins = t_.matmul(ps[:, 2 * tt + b, :], h[s][:, tt * P:(tt + 1) * P],
                                            w[s][:, b * HALF:(b + 1) * HALF],
                                            start=(first and m == 0), stop=(last_k and m == 2))
                    if last_k and tt < 3:
                        ins.then_inc(s_dmm, 1)
                ins.then_inc(s_down, 1)

            pe.wait_ge(s_hid, FT - 1)
            down(0, 0, True, False, None)
            for n in range(1, 4):
                down(n, n, False, False, None)
            with pe.Fori(1, 5) as i:
                for j in range(4):
                    down(i * 4 + j, j, False, False, None)
            down(20, 0, False, False, None)
            down(21, 1, False, True, None)
            down(22, 2, True, False, 1)
            down(23, 3, False, False, None)
            with pe.Fori(6, 10) as i:
                for j in range(4):
                    down(i * 4 + j, j, False, False, None)
            for n in range(40, 43):
                down(n, n % 4, False, False, None)
            down(43, 3, False, True, None)


_INS = ["x", "c", "w_ada", "b_ada", "norm_mix_gain", "w_in", "conv_w", "a_log", "dt_bias",
        "gdn_norm_gain", "w_pool", "pool_scale", "w_out", "norm_ffn_gain", "w_gate_up", "w_down",
        "norm_final_gain"]


def kernel(**inputs):
    import numpy as _np
    import concourse.bacc as _bacc
    from concourse.bass_utils import run_bass_kernel_spmd as _run

    nc = _bacc.Bacc("TRN2", target_bir_lowering=False, num_devices=1)
    arrays, args = {}, []
    for name in _INS:
        arr = _np.ascontiguousarray(inputs[name])
        arrays[f"in_{name}"] = arr
        args.append(nc.dram_tensor(f"in_{name}", arr.shape, F32, kind="ExternalInput").ap())
    args.append(nc.dram_tensor("out_0", (1, SEQ, D_MODEL), F32, kind="ExternalOutput").ap())
    args.append(nc.dram_tensor("qkvz_spill", (QKVT + ZT, P, SEQ), F32).ap())
    args.append(nc.dram_tensor("h2_spill", (SEQ, D_MODEL), F32).ap())
    hybrid_block(nc, *args)
    r = _run(nc, [arrays], core_ids=[0])
    return r.results[0]["out_0"]
```

```python
import concourse.bass as bass
from concourse import mybir
from concourse.alu_op_type import AluOpType as ALU
from contextlib import ExitStack

F32 = mybir.dt.float32
F32R = mybir.dt.float32r
BF16 = mybir.dt.bfloat16
I16 = mybir.dt.int16
ACT = mybir.ActivationFunctionType
AX = mybir.AxisListType

P = 128
D_MODEL, SEQ = 1024, 1024
KT = D_MODEL // P
NC = SEQ // P
POOL_W, HEADS, HD = 256, 6, 128
GDN_W = HEADS * HD
CONV = 4
D_FF = 2816
FT = D_FF // P
IN_COLS = POOL_W + 4 * GDN_W + 2 * HEADS
EPS = 1e-6
PT = POOL_W // P
QKVT = 3 * GDN_W // P
ZT = GDN_W // P
G3 = 3
GW = G3 * P
HALF = 512
LEVELS = 7
PAD = 16
SMALL_A = 3 * KT + 6 * KT
CA_C, CA_GM, CA_GF, CA_B = 0, KT, 2 * KT, 3 * KT
CB_CONV, CB_PS, CB_GG = 0, CONV * QKVT, CONV * QKVT + PT
SMALL_B = CB_GG + 1
WINDOWS = (2, 4, 8, 16)
BA_COL = IN_COLS - P
BA_ROW = P - 2 * HEADS - 96
KB = 1024
SBUF_BASE, SBUF_END = 16512, 212832


def settled(eng, value):
    return value if isinstance(value, int) else eng.compute_val(value)


class Chain:

    def __init__(self, eng, sem):
        self.eng, self.sem, self.n, self.dyn, self.n0 = eng, sem, 0, 0, 0

    def link(self, ins):
        self.n += 1
        ins.then_inc(self.sem, 1)
        self.eng.wait_ge(self.sem, self.n + self.dyn)

    def enter(self, trip, per):
        self.n0, self.dyn = self.n, trip * per

    def leave(self, trips, per):
        assert self.n - self.n0 == per, (self.n - self.n0, per)
        self.n, self.dyn = self.n0 + trips * per, 0


def hybrid_block(nc, x, c, w_ada, b_ada, norm_mix_gain, w_in, conv_w, a_log, dt_bias, gdn_gain,
                 w_pool, pool_scale, w_out, norm_ffn_gain, w_gate_up, w_down, norm_final_gain,
                 out, qkvz_d, h2_d):
    x2, out2 = x[0], out[0]
    wada, win, wout, wgu, wdn = w_ada[0], w_in[0], w_out[0], w_gate_up[0], w_down[0]

    def at(name, off, free, dt=F32):
        return nc.alloc_sbuf_tensor_at(name, [P] + list(free), dt, offset=SBUF_BASE + off)

    off = [0]

    def small(name, free, dt=F32):
        n = 2 if dt == BF16 else 4
        for f in free:
            n *= f
        t = at(name, off[0], free, dt)
        off[0] += (n + 31) // 32 * 32
        assert off[0] <= 8 * KB + 512, off
        return t

    ident = small("ident", [P])
    tri = small("tri", [P])
    below = small("below", [P])
    ones = small("ones", [P])
    lmask = small("lmask", [LEVELS, P], BF16)
    cols_a = small("cols_a", [SMALL_A])
    cols_b = small("cols_b", [SMALL_B])
    mcol = small("mcol", [2 * KT])
    gcol = small("gcol", [KT])
    fcol = small("fcol", [2 * KT])
    gcol_f = small("gcol_f", [KT])
    fsum = small("fsum", [2 * KT])
    ba = small("ba", [NC, 2 * HEADS])
    al_b = small("al_b", [HEADS])
    dt_b = small("dt_b", [HEADS])
    spt = small("spt", [3, NC, HEADS])
    NSC = 5
    S_BETA, S_G, S_EG, S_ED, S_EL = range(NSC)
    allsc = small("allsc", [NC, NSC, HEADS])
    sc = [small(f"sc{s}", [NSC, HEADS]) for s in range(2)]
    rr = [small(f"rr{s}", [2 * HEADS]) for s in range(2)]
    ssq = small("ssq", [2 * HEADS])
    ssb = small("ssb", [2 * HEADS])
    nbk = small("nbk", [HEADS])
    kdec = small("kdec", [HEADS])
    rq2 = [small(f"rq2{s}", [HEADS]) for s in range(2)]
    sso = small("sso", [HEADS])
    oc = small("oc", [4, HEADS])
    ssx = small("ssx", [NC])
    rst = small("rst", [NC])
    ssx2 = small("ssx2", [2])
    rst2 = small("rst2", [2])
    mhalf = small("mhalf", [2 * HEADS])
    epsh = small("epsh", [HEADS])
    rcnt = small("rcnt", [PT, PAD])
    ssf = small("ssf", [2 * NC])

    B0 = 8 * KB + 512
    gate_m = at("gate_m", B0, [D_MODEL])
    gate_f = at("gate_f", B0 + 4 * KB, [D_MODEL])
    C0 = B0 + 8 * KB
    D0 = C0 + 64 * KB
    hn_hi = at("hn_hi", C0, [KT, SEQ], F32R)
    hn_f = at("hn_f", C0 + 32 * KB, [KT, SEQ])
    hn_lo = at("hn_lo", C0 + 32 * KB, [KT, SEQ], F32R)
    WS = 4
    w_raw = [at(f"w_raw{s}", D0 + 8 * KB * s, [KT, P]) for s in range(WS)]
    w_lo = [at(f"w_lo{s}", D0 + 8 * KB * s, [KT, P], F32R) for s in range(WS)]
    w_hi = [at(f"w_hi{s}", D0 + 8 * KB * s + 4 * KB, [KT, P], F32R) for s in range(WS)]
    ypool = at("ypool", D0 + 32 * KB, [PT, SEQ])
    E0 = D0 + 40 * KB
    SW = PAD + SEQ
    seqb = [at(f"seqb{s}", E0 + 4 * SW * s, [SW]) for s in range(2)]
    acc = [at(f"acc{s}", E0 + 4 * SW * (2 + s), [SW]) for s in range(2)]
    E1 = E0 + 16 * SW
    act_o = [at(f"act_o{s}", E1 + 4 * KB * s, [SEQ]) for s in range(2)]
    ada_w = [at(f"ada_w{s}", E1 + 8 * KB + 8 * KB * s, [2 * D_MODEL]) for s in range(2)]
    ada_m = [at(f"ada_m{s}", C0 + 8 * KB * s, [2 * D_MODEL]) if s < 4 else ada_w[s - 4]
             for s in range(6)]
    ada_acc = at("ada_acc", E1 + 24 * KB, [4 * D_MODEL])
    x_sl = [at(f"x_sl{t}", E1 + 40 * KB + 4 * KB * t if t < 5 else
               (E1 + 4 * KB * (t - 5) if t < 7 else D0 + 32 * KB), [D_MODEL]) for t in range(NC)]
    mixed_sq = at("mixed_sq", E1 + 8 * KB, [NC, POOL_W])
    wpb = at("wpb", E1 + 60 * KB, [PT, P])
    rows_a = at("rows_a", E1 + 61 * KB, [P])
    rows_b = at("rows_b", E1 + 61 * KB + 512, [P])
    assert E1 + 62 * KB <= SBUF_END
    wo_hi = at("wo_hi", C0, [KT, D_MODEL], F32R)
    wo_raw = at("wo_raw", C0 + 32 * KB, [KT, D_MODEL])
    wo_lo = at("wo_lo", C0 + 32 * KB, [KT, D_MODEL], F32R)
    h2n_f = at("h2n_f", D0, [KT, SEQ])
    h2n_lo = at("h2n_lo", D0, [KT, SEQ], F32R)
    stage = [at(f"stage{s}", E0 + 12 * KB * s, [QKVT + ZT, P]) for s in range(2)]
    pos = [E1 + 8 * KB]

    def temp(name, free=(HEADS, P), dt=F32, alias=None):
        n = 4 * free[0] * free[1]
        o = pos[0] if alias is None else alias
        t = at(name, o, list(free), dt)
        if alias is None:
            pos[0] += n
        return t, o

    QD = [temp(f"QD{s}")[0] for s in range(2)]
    Kd = [temp(f"Kd{s}")[0] for s in range(2)]
    Vb = [temp(f"Vb{s}")[0] for s in range(2)]
    KbT = [temp(f"KbT{s}")[0] for s in range(2)]
    Sm, _ = temp("Sm")
    om, _ = temp("om")
    NA, _ = temp("NA")
    assert pos[0] >= E1 + 40 * KB
    Em, _ = temp("Em")
    Rm, o_R = temp("Rm")
    Tm, o_T = temp("Tm")
    Xm, o_X = temp("Xm")
    Um = [temp(f"Um{s}")[0] for s in range(2)]
    assert pos[0] <= E1 + 60 * KB
    slg, _ = temp("slg", alias=o_T)
    kb, _ = temp("kb", alias=o_X)
    rkt, _ = temp("rkt", alias=o_R)
    y_hi, o_yh = temp("y_hi", (KT, P), F32R)
    y_lo, o_yl = temp("y_lo", (KT, P), F32R)
    xn2, _ = temp("xn2", (KT, P), alias=o_yh)
    junk2, _ = temp("junk2", (KT, P), alias=o_yl)
    xt, _ = temp("xt", (KT, P))
    assert pos[0] <= SBUF_END
    h2n_hi = at("h2n_hi", C0, [KT, SEQ], F32R)
    u_raw = [at(f"u_raw{s}", C0 + 32 * KB + 8 * KB * s, [KT, P]) for s in range(WS)]
    u_lo = [at(f"u_lo{s}", C0 + 32 * KB + 8 * KB * s, [KT, P], F32R) for s in range(WS)]
    u_hi = [at(f"u_hi{s}", C0 + 36 * KB + 8 * KB * s, [KT, P], F32R) for s in range(WS)]
    f_raw = [at(f"f_raw{s}", E0 + 8 * KB * s, [KT, P]) for s in range(2)]
    f_lo = [at(f"f_lo{s}", E0 + 8 * KB * s, [KT, P], F32R) for s in range(2)]
    f_hi = [at(f"f_hi{s}", E0 + 8 * KB * s + 4 * KB, [KT, P], F32R) for s in range(2)]
    hid = at("hid", D0 + 32 * KB, [FT, SEQ])
    assert D0 + 32 * KB + 88 * KB <= SBUF_END
    silu_t = at("silu_t", B0, [SEQ])
    DS = 4
    d_off = [C0 + 36 * KB, C0, C0 + 12 * KB, C0 + 24 * KB]
    d_raw = [at(f"d_raw{s}", d_off[s], [D_MODEL]) for s in range(DS)]
    d_lo = [at(f"d_lo{s}", d_off[s], [D_MODEL], F32R) for s in range(DS)]
    d_hi = [at(f"d_hi{s}", d_off[s] + 4 * KB, [D_MODEL], F32R) for s in range(DS)]
    a_hi = [at(f"a_hi{s}", d_off[s] + 8 * KB, [HALF], F32R) for s in range(DS)]
    a_lo = [at(f"a_lo{s}", d_off[s] + 10 * KB, [HALF], F32R) for s in range(DS)]
    h_re = [at(f"h_re{s}", D0 + 4 * KB * s, [D_MODEL]) for s in range(4)]
    fin = [at(f"fin{s}", C0 + 48 * KB + 4 * KB * s, [D_MODEL]) for s in range(4)]
    fgain = at("fgain", D0 + 24 * KB, [D_MODEL])
    fjunk = at("fjunk", D0 + 28 * KB, [D_MODEL])

    ctx = ExitStack()
    with ctx:
        ps = ctx.enter_context(nc.psum_tensor("ps", [P, 8, HALF], F32))

        def sem(name):
            return ctx.enter_context(nc.semaphore(name))

        def bank2(b):
            return ps[:, b:b + 2, :].rearrange("p a n -> p (a n)")

        def grp(b):
            return ps[:, b, 0:GW]

        def grp3(b):
            return ps[:, b, 0:GW].rearrange("p (h n) -> p h n", h=G3)

        def bc(t, g):
            return t[:, G3 * g:G3 * g + G3].unsqueeze(2).to_broadcast([P, G3, P])

        def flat(t, g=None):
            v = t[:, :, :] if g is None else t[:, G3 * g:G3 * g + G3, :]
            return v.rearrange("p h n -> p (h n)")

        s_small = sem("small_loaded")
        s_x = sem("x_loaded")
        s_xsq = sem("x_tile_squared")
        s_h2sq = sem("h2_squared")
        s_fsq = sem("final_squared")
        s_xs = [sem(f"x_loaded{t}") for t in range(NC)]
        s_ada = [sem(f"ada_loaded{s}") for s in range(2)]
        s_adam = [sem(f"ada_mixer_loaded{s}") for s in range(4)] + s_ada
        s_w = [sem(f"w_in_loaded{s}") for s in range(WS)]
        s_wo = sem("w_out_loaded")
        s_const = sem("constants_ready")
        s_pool_chain = sem("pool_chain")
        s_dve_chain = sem("dve_chain")
        s_act_chain = sem("act_chain")
        s_rows_tr = sem("small_rows_transposed")
        s_cols = sem("small_columns_ready")
        s_cs = sem("c_silu_ready")
        s_ss = sem("x_square_sum_ready")
        s_rst = sem("x_rstd_ready")
        s_xn = sem("x_normalised")
        s_xtr = sem("x_transposed")
        s_xev = sem("x_transpose_evacuated")
        s_ada_used = sem("ada_piece_used")
        s_ada_mm = sem("ada_columns_summed")
        s_hf = sem("hn_modulated")
        s_hhi = sem("hn_hi_ready")
        s_hlo = sem("hn_lo_ready")
        s_wsplit = sem("w_in_split")
        s_proj = sem("projected")
        s_evac = sem("projection_evacuated")
        s_seq = sem("sequence_tile_used")
        s_conv = sem("conv_ready")
        s_aout = sem("activated_tile_ready")
        s_spill = [sem(f"tile_spilled{s}") for s in range(2)]
        s_batr = sem("ba_transposed")
        s_pmm = sem("pool_mixed")
        s_prt = sem("pool_roots_ready")
        s_pss = sem("pool_copied_and_summed")
        s_pst = sem("pool_sum_ready")
        s_fsum = sem("ffn_columns_summed")
        s_gmm = sem("gate_columns_summed")
        s_gev = sem("gate_columns_read")
        s_sp = sem("softplus_steps")
        s_spa = sem("softplus_activation")
        s_gmx = sem("decay_sums")
        s_ex = sem("decay_exponentials")
        s_scr = sem("scalars_ready")

        block = ctx.enter_context(nc.Block())

        s_stg = [sem(f"chunk_staged{s}") for s in range(2)]
        s_xin = sem("x_chunk_loaded")
        s_h2st = sem("h2_stored")
        (s_sq, s_ktr, s_vtr, s_ssr, s_rr, s_scc, s_vb, s_kbd, s_kdd, s_kbtr, s_kbT, s_slg, s_arg,
         s_exp, s_e, s_ti, s_kk, s_qk, s_na, s_qd, s_y, s_t, s_utr, s_u, s_xmm, s_xc) = [
            sem(n) for n in (
                "qk_squared", "k_transposed", "v_transposed", "square_sums_read", "norms_ready",
                "chunk_scalars_ready", "v_beta_ready", "k_beta_ready", "k_decay_ready",
                "kb_transposed", "kbT_ready", "decay_weights_ready", "decay_args", "decay_exp",
                "decay_ready", "inverse_init", "kk_products", "qk_products", "na_ready", "qd_ready",
                "level_product", "inverse_updated", "inverse_transposed", "u_ready",
                "level_x_product", "level_x_ready")]
        s_stz = [sem(f"z_staged{s}") for s in range(2)]
        s_ntr = sem("norm_transposes")
        s_uz = sem("inverse_first_level")
        s_uf = sem("inverse_complete")
        s_oss = sem("o_square_sums_scaled")
        s_ort = sem("o_root_ready")
        s_wog = sem("w_out_gated")
        (s_s, s_ks, s_o1, s_r, s_o1c, s_vmm, s_v, s_o2, s_sd, s_o, s_sso, s_on, s_otr, s_yf,
         s_yhi, s_ylo, s_op, s_h2, s_ssx2, s_rst2, s_xn2, s_htr, s_h2n) = [
            sem(n) for n in (
                "state_ready", "k_state_product", "q_state_product", "rhs_ready", "o1_copied",
                "v_new_product", "v_new_ready", "o2_product", "state_delta", "o_ready",
                "o_square_sums", "o_normalised", "o_transposed", "y_ready", "y_hi_ready",
                "y_lo_ready", "mix_product", "h2_ready", "h2_square_sum", "h2_rstd",
                "h2_normalised", "h2_transposed", "h2_transpose_evacuated")]
        s_wosp = sem("w_out_split")
        s_wohi = sem("w_out_hi")
        s_u_ld = [sem(f"gate_up_loaded{s}") for s in range(WS)]
        s_uhi = sem("gate_up_hi")
        s_ulo = sem("gate_up_lo")
        s_f_hf = sem("ffn_modulated")
        s_f_hi = sem("ffn_hi_ready")
        s_f_lo = sem("ffn_lo_ready")
        s_gu = sem("gate_up_product")
        s_sil = sem("gate_activated")
        s_hid = sem("hidden_ready")
        s_d_ld = [sem(f"down_loaded{s}") for s in range(DS)]
        s_dhi = sem("down_hi")
        s_dlo = sem("down_lo")
        s_down = sem("down_step_done")
        s_dmm = sem("down_product")
        s_dev = sem("down_evacuated")
        s_hre = [sem(f"h2_reloaded{s}") for s in range(4)]
        s_fg = sem("final_gain_loaded")
        s_fh = sem("final_h_ready")
        s_fss = sem("final_square_sum")
        s_frs = sem("final_rstd")
        s_fin = sem("final_ready")
        s_out = sem("output_stored")

        def w_cols(t):
            return t * P if t < PT else (BA_COL if t == PT else (t - 1) * P)

        NT = PT + 1 + QKVT + ZT
        T0 = PT + 1
        spill3 = qkvz_d.rearrange("t p n -> p t n")

        @block.sync
        def _(sp):
            def x_tile(t):
                sp.dma_start(x_sl[t][:, :], x2[t * P:(t + 1) * P, :]).then_inc(s_xs[t], 16)

            for t in range(2):
                x_tile(t)
            for r, (src, n) in enumerate(((c, KT), (norm_mix_gain, KT), (norm_ffn_gain, KT))):
                sp.dma_start(rows_a[r * KT:r * KT + n, :],
                             src.rearrange("o (r p) -> (o r) p", p=P)).then_inc(s_small, 16)
            sp.dma_start(rows_a[CA_B:SMALL_A, :],
                         b_ada.rearrange("o (r p) -> (o r) p", p=P)).then_inc(s_small, 16)
            sp.dma_start(rows_b[0:CB_PS, :],
                         conv_w.rearrange("o t (r p) -> (o t r) p", p=P)).then_inc(s_small, 16)
            sp.dma_start(rows_b[CB_PS:CB_GG, :],
                         pool_scale.rearrange("o (r p) -> (o r) p", p=P)).then_inc(s_small, 16)
            sp.dma_start(rows_b[CB_GG:SMALL_B, :], gdn_gain).then_inc(s_small, 16)
            for t in range(2, NC):
                x_tile(t)
            for k in range(KT):
                if k >= 6:
                    sp.wait_ge(s_ada_used, k - 5)
                sp.dma_start(ada_m[k % 6][:, :],
                             wada[k * P:(k + 1) * P, 0:2 * D_MODEL]).then_inc(s_adam[k % 6], 16)
            for t in range(4):
                sp.dma_start(w_raw[t][:, :, :], win[:, w_cols(t):w_cols(t) + P].rearrange(
                    "(k p) n -> p k n", p=P)).then_inc(s_w[t], 16)
            sp.dma_start(al_b[:, :], a_log.to_broadcast([P, HEADS])).then_inc(s_x, 16)
            sp.dma_start(dt_b[:, :], dt_bias.to_broadcast([P, HEADS])).then_inc(s_x, 16)
            sp.dma_start(gate_m[:, :], b_ada[:, 2 * D_MODEL:3 * D_MODEL].to_broadcast(
                [P, D_MODEL])).then_inc(s_x, 16)
            sp.dma_start(gate_f[:, :], b_ada[:, 5 * D_MODEL:6 * D_MODEL].to_broadcast(
                [P, D_MODEL])).then_inc(s_x, 16)
            sp.wait_ge(s_const, 2)
            for g in range(4):
                o = 64 * (g % 2)
                sp.dma_start(wpb[o:o + 64, g // 2, o:o + 64], w_pool[0, g]).then_inc(s_x, 16)
            with_loop = (NT - 4) // 4
            with sp.Fori(0, with_loop) as i:
                for j in range(4):
                    sp.wait_ge(s_proj, i * 4 + (j + 1))
                    sp.dma_start(w_raw[j][:, :, :],
                                 win[:, bass.ds(i * (4 * P) + (j + 3) * P, P)].rearrange(
                                     "(k p) n -> p k n", p=P)).then_inc(s_w[j], 16)
            for t in range(4 + 4 * with_loop, NT):
                sp.wait_ge(s_proj, t - 3)
                sp.dma_start(w_raw[t % 4][:, :, :], win[:, w_cols(t):w_cols(t) + P].rearrange(
                    "(k p) n -> p k n", p=P)).then_inc(s_w[t % 4], 16)
            def stage_load(cc, s):
                sp.dma_start(stage[s][:, 0:QKVT, :],
                             spill3[:, 0:QKVT, bass.ds(cc * P, P)]).then_inc(s_stg[s], 16)

            def z_load(cc, s):
                sp.dma_start(stage[s][:, QKVT:, :],
                             spill3[:, QKVT:, bass.ds(cc * P, P)]).then_inc(s_stz[s], 16)

            def x_load(cc):
                sp.dma_start(xt[:, :, :].rearrange("p k n -> p (k n)"),
                             x2[bass.ds(cc * P, P), :]).then_inc(s_xin, 16)

            def h2_store(cc):
                sp.wait_ge(s_h2, cc + 1)
                sp.dma_start(h2_d[bass.ds(cc * P, P), :],
                             xt[:, :, :].rearrange("p k n -> p (k n)")).then_inc(s_h2st, 16)

            sp.wait_ge(s_aout, QKVT)
            for s in range(2):
                sp.wait_ge(s_spill[s], 16 * QKVT // 2)
            stage_load(0, 0)
            sp.wait_ge(s_proj, NT)
            sp.dma_start(wo_raw[:, :, :],
                         wout.rearrange("(k p) n -> p k n", p=P)).then_inc(s_wo, 16)
            for s in range(2):
                sp.wait_ge(s_spill[s], 16 * (QKVT + ZT) // 2)
            stage_load(1, 1)
            z_load(0, 0)
            z_load(1, 1)
            x_load(0)

            def step(cc, s):
                if s is not None:
                    sp.wait_ge(s_o1, cc * 2)
                    stage_load(cc + 1, s)
                    sp.wait_ge(s_yf, cc * 2)
                    z_load(cc + 1, s)
                h2_store(cc - 1)
                sp.wait_ge(s_h2st, cc * 16)
                sp.wait_ge(s_xn2, cc)
                x_load(cc)

            with sp.Fori(0, 3) as i:
                step(i * 2 + 1, 0)
                step(i * 2 + 2, 1)
            step(7, None)
            sp.wait_ge(s_o1, 2 * NC)
            for up in range(2):
                sp.dma_start(f_raw[up][:, :, :],
                             wgu[:, up * D_FF:up * D_FF + P].rearrange(
                                 "(k p) n -> p k n", p=P)).then_inc(s_u_ld[up], 16)
            h2_store(7)

            def gu_load(f, s, up):
                sp.dma_start(u_raw[s][:, :, :], wgu[:, bass.ds(f * P + up * D_FF, P)].rearrange(
                    "(k p) n -> p k n", p=P)).then_inc(s_u_ld[s], 16)

            sp.wait_ge(s_op, NC)
            sp.wait_ge(s_uhi, 2)
            for f in (1, 2):
                for up in range(2):
                    gu_load(f, 2 * (f % 2) + up, up)
            sp.wait_ge(s_gu, 2)
            for up in range(2):
                gu_load(3, 2 + up, up)
            with sp.Fori(1, FT // 2 - 1) as i:
                for j in range(2):
                    sp.wait_ge(s_gu, i * 2 + (j + 1))
                    for up in range(2):
                        gu_load(i * 2 + (2 + j), 2 * j + up, up)

            def d_load(k, s):
                sp.dma_start(d_raw[s][:, :], wdn[bass.ds(k * P, P), :]).then_inc(s_d_ld[s], 16)

            sp.wait_ge(s_h2st, NC * 16)
            sp.wait_ge(s_gu, FT - 1)
            d_load(0, 0)
            sp.wait_ge(s_gu, FT)
            for k in range(1, DS):
                d_load(k, k)
            sp.dma_start(fgain[:, :], norm_final_gain.unsqueeze(0).to_broadcast(
                [P, D_MODEL])).then_inc(s_fg, 16)
            for t in range(4):
                sp.dma_start(h_re[t][:, :], h2_d[t * P:(t + 1) * P, :]).then_inc(s_hre[t], 16)
            with sp.Fori(0, 4) as i:
                for j in range(4):
                    sp.wait_ge(s_down, i * 4 + (j + 1))
                    d_load(i * 4 + (j + 4), j)
            for n in (20, 21):
                sp.wait_ge(s_down, n - 3)
                d_load(n, n % 4)
            def second_pass(first, end):
                with sp.Fori(first, end) as i:
                    for j in range(4):
                        sp.wait_ge(s_down, i * 4 + (j + 19))
                        d_load(i * 4 + j, (j + 22) % 4)

            def store(t):
                sp.wait_ge(s_fin, t + 1)
                sp.dma_start(out2[t * P:(t + 1) * P, :], fin[t % 4][:, :]).then_inc(s_out, 16)

            second_pass(0, 2)
            for t in range(4):
                store(t)
                sp.dma_start(h_re[t][:, :],
                             h2_d[(4 + t) * P:(5 + t) * P, :]).then_inc(s_hre[t], 16)
            second_pass(2, 5)
            for n in (42, 43):
                sp.wait_ge(s_down, n - 3)
                d_load(n - 22, n % 4)
            for t in range(4, NC):
                store(t)
            sp.wait_ge(s_out, 16 * NC)

        @block.gpsimd
        def _(pool):
            g = nc.gpsimd
            ch = Chain(pool, s_pool_chain)
            ch.link(g.memset(ones[:, :], 1.0))
            one = ones[:, :]
            g.affine_select(out=ident[:, :], in_=one, compare_op=ALU.is_equal, fill=0.0, base=0,
                            pattern=[[1, P]], channel_multiplier=-1)
            ch.link(g.memset(mhalf[:, :], -0.5))
            g.memset(epsh[:, :], EPS * HD)
            g.affine_select(out=tri[:, :], in_=one, compare_op=ALU.is_ge, fill=0.0, base=0,
                            pattern=[[1, P]], channel_multiplier=-1)
            g.affine_select(out=below[:, :], in_=one, compare_op=ALU.is_gt, fill=0.0, base=0,
                            pattern=[[-1, P]], channel_multiplier=1).then_inc(s_const, 1)
            ch.link(g.memset(wpb[:, :, :], 0.0))
            for t in range(NC):
                pool.wait_ge(s_ss, t + 1)
                g.tensor_tensor(rst[:, t:t + 1], ssx[:, t:t + 1], mhalf[:, 0:1],
                                ALU.pow).then_inc(s_rst, 1)

            for lv in range(LEVELS):
                b = 1 << lv
                m = lmask[:, lv, :].rearrange("p (a h r) -> p a h r", h=2, r=b)
                o = one.rearrange("p (a h r) -> p a h r", h=2, r=b)
                tr = lv in (0, LEVELS - 1)
                ch.link(g.affine_select(out=m, in_=o, compare_op=ALU.is_ge, fill=0.0,
                                        base=-2 * P if tr else -b,
                                        pattern=[[-2 * b, P // (2 * b)],
                                                 [2 * P if tr else -2 * P, 2], [0, b]],
                                        channel_multiplier=1))
                ch.link(g.affine_select(out=m, in_=m, compare_op=ALU.is_ge, fill=0.0,
                                        base=(b if tr else 2 * b) - 1,
                                        pattern=[[2 * b, P // (2 * b)], [0, 2], [0, b]],
                                        channel_multiplier=-1))
            for t in range(PT):
                for hf in range(2):
                    w = WINDOWS[2 * t + hf]
                    rows = slice(64 * hf, 64 * hf + 64)
                    for j in range(w - 1):
                        g.memset(rcnt[rows, t, j:j + 1], 1.0 / (j + 1))
                    ch.link(g.memset(rcnt[rows, t, w - 1:PAD], 1.0 / w))
            g.memset(seqb[0][:, 0:PAD], 0.0)
            g.memset(seqb[1][:, 0:PAD], 0.0).then_inc(s_const, 1)

            def split(s, count):
                count = settled(pool, count)
                pool.wait_ge(s_const, 1)
                pool.wait_ge(s_w[s], count)
                ch.link(g.tensor_copy(w_hi[s][:, :, :], w_raw[s][:, :, :]))
                g.tensor_tensor(w_lo[s][:, :, :], w_raw[s][:, :, :],
                                w_hi[s][:, :, :].bitcast(F32), ALU.subtract).then_inc(s_wsplit, 1)

            for t in range(T0):
                split(t, 16)
            with pool.Fori(0, 6) as i:
                ch.enter(i, 4)
                for j in range(4):
                    split((3 + j) % 4, i * 16 + (16 if j == 0 else 32))
            ch.leave(6, 4)
            for s in range(2):
                g.tensor_copy(Um[s][:, :, :], ident[:, :].unsqueeze(1).to_broadcast(
                    [P, HEADS, P])).then_inc(s_ti, 1)
            pool.wait_ge(s_pst, 1)
            g.tensor_tensor(ssf[:, NC:2 * NC], ssf[:, 0:NC], mhalf[:, 0:NC],
                            ALU.pow).then_inc(s_prt, 1)


            def norm_root(cc, s, q):
                r = slice(0, HEADS) if q else slice(HEADS, 2 * HEADS)
                pool.wait_ge(s_ssr, cc * 2 + 1 + q)
                g.tensor_tensor(rr[s][:, r], ssb[:, r], mhalf[:, r], ALU.pow).then_inc(s_rr, 1)

            def rk_tri(cc, s):
                pool.wait_ge(s_rr, cc * 2 + 1)
                ch.link(g.tensor_tensor(rkt[:, :, :],
                                        tri[:, :].unsqueeze(1).to_broadcast([P, HEADS, P]),
                                        rr[s][:, HEADS:].unsqueeze(2).to_broadcast(
                                            [P, HEADS, P]), ALU.mult))

            def u_init(s):
                g.tensor_copy(Um[s][:, :, :], ident[:, :].unsqueeze(1).to_broadcast(
                    [P, HEADS, P])).then_inc(s_ti, 1)

            def p_slg(cc, s):
                pool.wait_ge(s_scc, cc + 1)
                if not (isinstance(cc, int) and cc == 0):
                    pool.wait_ge(s_xmm, cc * (2 * LEVELS - 2))
                for gr in range(2):
                    g.tensor_tensor(slg[:, G3 * gr:G3 * gr + G3, :],
                                    below[:, :].unsqueeze(1).to_broadcast([P, G3, P]),
                                    bc(sc[s][:, S_G, :], gr), ALU.mult).then_inc(s_slg, 1)

            def p_e(cc, s):
                for gr in range(2):
                    e = Em[:, G3 * gr:G3 * gr + G3, :]
                    pool.wait_ge(s_exp, cc * 2 + (gr + 1))
                    g.tensor_tensor(e, e, rkt[:, G3 * gr:G3 * gr + G3, :],
                                    ALU.mult).then_inc(s_e, 1)

            def r_root(cc):
                pool.wait_ge(s_oss, cc + 1)
                g.tensor_tensor(oc[:, 2, :], oc[:, 1, :], mhalf[:, 0:HEADS],
                                ALU.pow).then_inc(s_ort, 1)

            def r_tail(cc):
                pool.wait_ge(s_ssx2, cc + 1)
                g.tensor_tensor(rst2[:, 0:1], ssx2[:, 1:2], mhalf[:, 0:1],
                                ALU.pow).then_inc(s_rst2, 1)

            def r_mod(cc):
                h = h2n_f[:, :, bass.ds(cc * P, P)]
                count = settled(pool, cc * 2 + 2)
                pool.wait_ge(s_const, 1)
                pool.wait_ge(s_h2n, count)
                g.tensor_tensor(h, h, gcol_f[:, :].unsqueeze(2).to_broadcast([P, KT, P]),
                                ALU.mult).then_inc(s_f_hf, 1)
                count = settled(pool, cc * 2 + 1)
                pool.wait_ge(s_const, 1)
                pool.wait_ge(s_f_hf, count)
                g.tensor_tensor(h, h, fcol[:, 0:KT].unsqueeze(2).to_broadcast([P, KT, P]),
                                ALU.add).then_inc(s_f_hf, 1)

            def body(cc, s, first=False, last=False):
                p_slg(cc, s)
                if not first:
                    r_tail(cc - 2)
                p_e(cc, s)
                if not first:
                    r_mod(cc - 2)
                r_root(cc - 1)
                if not last:
                    u_init(1 - s)
                    norm_root(cc + 1, 1 - s, 0)
                    rk_tri(cc + 1, 1 - s)
                    norm_root(cc + 1, 1 - s, 1)

            norm_root(0, 0, 0)
            rk_tri(0, 0)
            p_slg(0, 0)
            p_e(0, 0)
            norm_root(0, 0, 1)
            pool.wait_ge(s_wo, 16)
            pool.wait_ge(s_gev, 1)
            for k in range(KT):
                g.tensor_tensor(wo_raw[:, k, :], wo_raw[:, k, :], gate_m[:, :],
                                ALU.mult).then_inc(s_wog, 1)
            norm_root(1, 1, 0)
            rk_tri(1, 1)
            norm_root(1, 1, 1)
            PER = 2
            body(1, 1, first=True)
            body(2, 0)
            with pool.Fori(1, 3) as i:
                ch.enter(i - 1, PER)
                body(i * 2 + 1, 1)
                body(i * 2 + 2, 0)
            ch.leave(2, PER)
            body(7, 1, last=True)
            r_tail(6)
            r_root(7)
            r_mod(6)
            r_tail(7)
            for t in range(NC):
                pool.wait_ge(s_fss, t + 1)
                g.tensor_tensor(ssf[:, NC + t:NC + t + 1], ssf[:, t:t + 1], mhalf[:, 0:1],
                                ALU.pow).then_inc(s_frs, 1)

        @block.scalar
        def _(act):
            a = nc.scalar
            ch = Chain(act, s_act_chain)
            act.wait_ge(s_cols, 1)
            a.activation(cols_a[:, CA_C:CA_C + KT], cols_a[:, CA_C:CA_C + KT],
                         ACT.Silu).then_inc(s_cs, 1)
            for t in range(NC):
                act.wait_ge(s_xs[t], 16)
                if t:
                    act.wait_ge(s_xsq, t)
                a.activation(bank2(4), x_sl[t][:, :], ACT.Square,
                             accum_out=ssx[:, t:t + 1]).then_inc(s_xsq, 1)
            for t in range(NC):
                act.wait_ge(s_xtr, t + 1)
                a.activation(hn_f[:, :, t * P:(t + 1) * P],
                             bank2(2 * (t % 2)).rearrange("p (k n) -> p k n", k=KT),
                             ACT.Copy).then_inc(s_xev, 1)
            for k in range(KT):
                act.wait_ge(s_hf, k + 1)
                a.activation(hn_hi[:, k, :], hn_f[:, k, :], ACT.Copy).then_inc(s_hhi, 1)

            def evac(t, slot, used):
                act.wait_ge(s_proj, t + 1)
                if used is not None:
                    act.wait_ge(*used)
                a.activation(seqb[slot][:, PAD:], bank2(2 * slot), ACT.Copy).then_inc(s_evac, 1)

            evac(0, 0, None)
            evac(1, 1, None)
            act.wait_ge(s_proj, 3)
            act.wait_ge(s_seq, 1)
            a.activation(seqb[0][0:32, PAD:], bank2(0)[96:128, :], ACT.Copy).then_inc(s_evac, 1)

            def ada_load(k):
                for s in range(2):
                    act.wait_ge(s_ada_used, k * 2 + (KT - 1 + s))
                    act.dma_start(ada_w[s][:, :],
                                  wada[bass.ds(k * P, P), (2 + 2 * s) * D_MODEL:
                                       (4 + 2 * s) * D_MODEL]).then_inc(s_ada[s], 16)

            def spill(n, slot):
                act.dma_start(qkvz_d[bass.ds(n, 1), :, :].rearrange("a p n -> p (a n)"),
                              act_o[slot][:, :]).then_inc(s_spill[slot], 16)

            def qkv(n, guard_spill):
                t = n + T0
                slot = qkv.slot
                evac(t, slot, (s_seq, n + PT) if isinstance(n, int) and n < 2 else
                     (s_conv, n - 1))
                act.wait_ge(s_conv, n + 1)
                if guard_spill is not None:
                    act.wait_ge(s_spill[1 - slot], guard_spill)
                a.activation(act_o[1 - slot][:, :], acc[1 - slot][:, 0:SEQ],
                             ACT.Silu).then_inc(s_aout, 1)
                act.wait_ge(s_aout, n + 1)
                spill(n, 1 - slot)

            ada_load(0)
            qkv.slot = 1
            qkv(0, None)
            act.wait_ge(s_sp, 1)
            a.activation(spt[:, 0, :, :], spt[:, 0, :, :], ACT.Exp, scale=-1.0).then_inc(s_spa, 1)
            a.activation(allsc[:, :, S_BETA, :], ba[:, :, 0:HEADS], ACT.Exp,
                         scale=-1.0).then_inc(s_spa, 1)
            act.wait_ge(s_x, 128)
            a.activation(al_b[:, :], al_b[:, :], ACT.Exp).then_inc(s_spa, 1)
            qkv.slot = 0
            qkv(1, None)
            act.wait_ge(s_sp, 2)
            a.activation(spt[:, 0, :, :], spt[:, 0, :, :], ACT.Ln).then_inc(s_spa, 1)
            with act.Fori(1, 8) as i:
                for j in range(2):
                    qkv.slot = (j + 1) % 2
                    qkv(i * 2 + j, i * 16)
                    if j == 0:
                        ada_load(i)
            for n in range(16, 18):
                qkv.slot = (n + 1) % 2
                qkv(n, (n // 2) * 16)
            act.wait_ge(s_gmx, 1)
            n48 = NC * HEADS
            for n, dst in enumerate((S_EG, S_ED, S_EL)):
                last = a.activation(allsc[:, :, dst, :],
                                    ps[:, 6, n * n48:(n + 1) * n48].rearrange(
                                        "p (c h) -> p c h", h=HEADS), ACT.Exp)
            last.then_inc(s_ex, 1)

            def z_tile(i):
                slot, o = (i + T0 + QKVT) % 2, i % 2
                act.wait_ge(s_proj, T0 + QKVT + i + 1)
                act.wait_ge(s_spill[o], 16 * ((QKVT + i) // 2))
                a.activation(act_o[o][:, :], bank2(2 * slot), ACT.Silu).then_inc(s_evac, 1)
                act.wait_ge(s_evac, T0 + QKVT + i + 1)
                spill(QKVT + i, o)

            z_tile(0)
            act.wait_ge(s_ada_mm, 2)
            for n in range(2 * KT):
                last = a.activation(mixed_sq[:, n % NC, 0:P],
                                    ps[:, 4 + n // 4, (n % 4) * P:(n % 4 + 1) * P],
                                    ACT.Copy, accum_out=fsum[:, n:n + 1])
                if n == NC - 1:
                    ch.link(last)
            last.then_inc(s_fsum, 1)
            for i in range(1, 3):
                z_tile(i)
            act.wait_ge(s_pmm, 1)
            for t in range(PT):
                a.activation(ypool[:, t, :], bank2(4 + 2 * t), ACT.Copy).then_inc(s_pss, 1)

            def squares(cc, q, bank):
                if not (isinstance(cc, int) and cc == 0):
                    act.wait_ge(s_qd, cc * 2)
                for gr in range(2):
                    act.wait_ge(s_ntr, cc * 4 + (2 * q + gr + 1))
                    for n in range(G3):
                        h = G3 * gr + n
                        c0 = h if q else HEADS + h
                        last = a.activation(Em[:, h, :],
                                            ps[:, bank[gr], n * P:(n + 1) * P], ACT.Square,
                                            accum_out=ssq[:, c0:c0 + 1])
                    last.then_inc(s_sq, 1)

            def p_kbT(cc, s):
                for gr in range(2):
                    act.wait_ge(s_kbtr, cc * 2 + (gr + 1))
                    a.activation(flat(KbT[s], gr), grp(2 * gr + 1), ACT.Copy).then_inc(s_kbT, 1)

            def p_exp(cc):
                for gr in range(2):
                    act.wait_ge(s_arg, cc * 2 + (gr + 1))
                    a.activation(flat(Em, gr), grp(5 + 2 * gr), ACT.Exp).then_inc(s_exp, 1)

            def level_u(cc, s, lv):
                dst = Tm if lv == 0 else Um[s]
                for gr in range(2):
                    act.wait_ge(s_utr, cc * (2 * LEVELS - 2) + (2 * lv + gr + 1))
                    a.activation(flat(dst, gr), grp(2 * gr), ACT.Copy).then_inc(s_u, 1)

            def level_x(cc, lv):
                for gr in range(2):
                    act.wait_ge(s_xmm, cc * (2 * LEVELS - 2) + (2 * (lv - 1) + gr + 1))
                    a.activation(flat(Xm, gr), grp(2 * gr), ACT.Copy).then_inc(s_xc, 1)

            def r_o1(cc, guard):
                for gr in range(2):
                    act.wait_ge(s_o1, cc * 2 + (gr + 1))
                    if guard:
                        act.wait_ge(s_ylo, cc * 3)
                    a.activation(flat(om, gr), grp(5 + 2 * gr), ACT.Copy).then_inc(s_o1c, 1)

            def r_v(cc):
                for gr in range(2):
                    act.wait_ge(s_vmm, cc * 2 + (gr + 1))
                    a.activation(flat(Rm, gr), grp(4 + 2 * gr), ACT.Copy).then_inc(s_v, 1)

            def r_sso(cc):
                for gr in range(2):
                    act.wait_ge(s_o, cc * 2 + (gr + 1))
                    for h in range(G3 * gr, G3 * gr + G3):
                        last = a.activation(junk2[:, PT + h, :], om[:, h, :], ACT.Square,
                                            accum_out=sso[:, h:h + 1])
                    last.then_inc(s_sso, 1)

            def r_yhi_pool(cc):
                a.activation(y_hi[:, 0:PT, :], ypool[:, :, bass.ds(cc * P, P)],
                             ACT.Copy).then_inc(s_yhi, 1)

            def r_yhi(cc):
                for gr in range(2):
                    act.wait_ge(s_yf, cc * 2 + (gr + 1))
                    a.activation(y_hi[:, PT + G3 * gr:PT + G3 * gr + G3, :],
                                 om[:, G3 * gr:G3 * gr + G3, :], ACT.Copy).then_inc(s_yhi, 1)

            def r_ssx(cc):
                act.wait_ge(s_h2, cc + 1)
                a.activation(flat(junk2), flat(xt), ACT.Square,
                             accum_out=ssx2[:, 0:1]).then_inc(s_h2sq, 1)

            def r_h2n(cc, bank=4):
                for h in range(2):
                    act.wait_ge(s_htr, cc * 2 + (h + 1))
                    a.activation(h2n_f[:, 4 * h:4 * h + 4, bass.ds(cc * P, P)],
                                 ps[:, bank + 2 * h, :].rearrange("p (k n) -> p k n", k=4),
                                 ACT.Copy).then_inc(s_h2n, 1)

            def body(cc, s, first=False, last=False):
                if not first:
                    r_ssx(cc - 2)
                p_exp(cc)
                p_kbT(cc, s)
                if not first:
                    r_h2n(cc - 2)
                level_u(cc, s, 0)
                r_o1(cc - 1, not first)
                level_x(cc, 1)
                if first:
                    wo_hi_copy(4)
                r_v(cc - 1)
                level_u(cc, s, 1)
                r_yhi_pool(cc - 1)
                if first:
                    wo_hi_copy(5)
                level_x(cc, 2)
                r_sso(cc - 1)
                level_u(cc, s, 2)
                if first:
                    wo_hi_copy(6)
                    wo_hi_copy(7)
                level_x(cc, 3)
                r_yhi(cc - 1)
                level_u(cc, s, 3)
                for lv in range(4, LEVELS):
                    level_x(cc, lv)
                    if lv < 6 and not last:
                        squares(cc + 1, lv - 4, (5, 7))
                    if lv < LEVELS - 1:
                        level_u(cc, s, lv)

            def u_hi_copy(hi, raw, s, dma):
                act.wait_ge(s_u_ld[s], dma)
                a.activation(hi[:, :, :], raw[:, :, :], ACT.Copy).then_inc(s_uhi, 1)

            def wo_hi_copy(k):
                act.wait_ge(s_wog, k + 1)
                a.activation(wo_hi[:, k, :], wo_raw[:, k, :], ACT.Copy).then_inc(s_wohi, 1)

            z_tile(3)
            act.wait_ge(s_pmm, 2)
            for n in range(NC):
                last = a.activation(mixed_sq[:, n, :],
                                    ps[:, 4 + n // 2, (n % 2) * POOL_W:(n % 2 + 1) * POOL_W],
                                    ACT.Square, accum_out=ssf[:, NC + n:NC + n + 1])
            last.then_inc(s_pss, 1)
            z_tile(4)
            squares(0, 0, (4, 5))
            squares(0, 1, (4, 5))
            z_tile(5)
            p_exp(0)
            p_kbT(0, 0)
            level_u(0, 0, 0)
            for lv in range(1, LEVELS):
                level_x(0, lv)
                if lv in (4, 5):
                    squares(1, lv - 4, (5, 7))
                if lv < LEVELS - 1:
                    level_u(0, 0, lv)
                if lv > 2:
                    wo_hi_copy(lv - 3)
            body(1, 1, first=True)
            body(2, 0)
            with act.Fori(1, 3) as i:
                body(i * 2 + 1, 1)
                body(i * 2 + 2, 0)
            body(7, 1, last=True)
            r_ssx(6)
            r_o1(7, True)
            r_v(7)
            r_h2n(6, 0)
            r_yhi_pool(7)
            r_sso(7)
            u_hi_copy(f_hi[0], f_raw[0], 0, 16)
            r_yhi(7)
            u_hi_copy(f_hi[1], f_raw[1], 1, 16)

            def f_hi_copy(k, half):
                r = slice(half * HALF, (half + 1) * HALF)
                a.activation(h2n_hi[:, k, r], h2n_f[:, k, r], ACT.Copy).then_inc(s_f_hi, 1)

            act.wait_ge(s_op, NC)
            act.wait_ge(s_f_hf, 2 * (NC // 2))
            for k in range(2):
                f_hi_copy(k, 0)
            r_ssx(7)
            for k in range(2, KT):
                f_hi_copy(k, 0)
            act.wait_ge(s_f_hf, 2 * (NC - 1))
            act.wait_ge(s_h2n, 2 * NC)
            for k in range(KT):
                f_hi_copy(k, 1)

            for up in range(2):
                u_hi_copy(u_hi[2 + up], u_raw[2 + up], 2 + up, 16)

            def silu(f, guard):
                act.wait_ge(s_gu, f + 1)
                if guard:
                    act.wait_ge(s_hid, f)
                a.activation(silu_t[:, :], bank2(silu.b), ACT.Silu).then_inc(s_sil, 1)

            silu.b = 0
            act.wait_ge(s_h2, NC)
            silu(0, False)
            u_hi_copy(u_hi[0], u_raw[0], 0, 32)
            u_hi_copy(u_hi[1], u_raw[1], 1, 32)
            silu.b = 4
            silu(1, True)
            u_hi_copy(u_hi[2], u_raw[2], 2, 32)
            u_hi_copy(u_hi[3], u_raw[3], 3, 32)
            with act.Fori(1, FT // 2 - 1) as i:
                silu.b = 0
                silu(i * 2, True)
                u_hi_copy(u_hi[0], u_raw[0], 0, i * 16 + 32)
                u_hi_copy(u_hi[1], u_raw[1], 1, i * 16 + 32)
                silu.b = 4
                silu(i * 2 + 1, True)
                u_hi_copy(u_hi[2], u_raw[2], 2, i * 16 + 32)
                u_hi_copy(u_hi[3], u_raw[3], 3, i * 16 + 32)
            silu.b = 0
            silu(FT - 2, True)

            def d_hi_copy(k, h, s, dma, used):
                act.wait_ge(s_d_ld[s], dma)
                if used is not None:
                    act.wait_ge(s_down, used)
                a.activation(d_hi[s][:, :], d_raw[s][:, :], ACT.Copy)
                a.activation(a_hi[s][:, :], hid[:, bass.ds(k, 1), h * HALF:(h + 1) * HALF].rearrange(
                    "p a n -> p (a n)"), ACT.Copy).then_inc(s_dhi, 1)

            d_hi_copy(0, 0, 0, 16, None)
            silu.b = 4
            silu(FT - 1, True)
            act.wait_ge(s_hid, FT)
            for n in range(1, 4):
                d_hi_copy(n, 0, n, 16, None)
            with act.Fori(1, 5) as i:
                for j in range(4):
                    d_hi_copy(i * 4 + j, 0, j, i * 16 + 16, i * 4 + (j - 3))
            for n in range(20, 24):
                d_hi_copy(n % FT, n // FT, n % 4, 16 * (n // 4 + 1), n - 3)

            def out_sq(t):
                act.wait_ge(s_fh, t + 1)
                a.activation(fjunk[:, :], h_re[t % 4][:, :], ACT.Square,
                             accum_out=ssf[:, t:t + 1]).then_inc(s_fsq, 1)

            for n in range(24, 28):
                d_hi_copy(n - FT, 1, n % 4, 16 * (n // 4 + 1), n - 3)
            for t in range(4):
                if t > 0:
                    act.wait_ge(s_fsq, t)
                out_sq(t)
            with act.Fori(7, 11) as i:
                for j in range(4):
                    d_hi_copy(i * 4 + (j - 22), 1, j, i * 16 + 16, i * 4 + (j - 3))
            for t in range(4, 8):
                act.wait_ge(s_fsq, t)
                out_sq(t)

        @block.vector
        def _(dve):
            v = nc.vector
            ch = Chain(dve, s_dve_chain)
            dve.wait_ge(s_rows_tr, 1)
            v.tensor_copy(cols_a[:, :], ps[:, 6, 0:SMALL_A])
            v.tensor_copy(cols_b[:, :], ps[:, 6, P:P + SMALL_B]).then_inc(s_cols, 1)
            for t in range(NC):
                dve.wait_ge(s_xsq, t + 1)
                v.tensor_scalar(ssx[:, t:t + 1], ssx[:, t:t + 1], 1.0 / D_MODEL, EPS,
                                ALU.mult, ALU.add).then_inc(s_ss, 1)
                dve.wait_ge(s_rst, t + 1)
                v.tensor_scalar(x_sl[t][:, :], x_sl[t][:, :], rst[:, t:t + 1], None,
                                ALU.mult).then_inc(s_xn, 1)
            dve.wait_ge(s_cs, 1)
            for k in range(KT):
                dve.wait_ge(s_adam[k % 6], 16 * (k // 6 + 1))
                ccol = cols_a[:, CA_C + k:CA_C + k + 1]
                if k == 0:
                    v.tensor_scalar(ada_acc[:, 0:2 * D_MODEL], ada_m[0][:, :], ccol, None,
                                    ALU.mult).then_inc(s_ada_used, 1)
                else:
                    dve.wait_ge(s_ada_used, k)
                    v.scalar_tensor_tensor(out=ada_acc[:, 0:2 * D_MODEL], in0=ada_m[k % 6][:, :],
                                           scalar=ccol, in1=ada_acc[:, 0:2 * D_MODEL],
                                           op0=ALU.mult, op1=ALU.add).then_inc(s_ada_used, 1)

            def modulation(mc, gc, base, gain, src):
                ch.link(v.tensor_tensor(mc[:, :], src,
                                        cols_a[:, CA_B + base:CA_B + base + 2 * KT], ALU.add))
                ch.link(v.scalar_tensor_tensor(out=gc[:, :], in0=mc[:, KT:2 * KT], scalar=1.0,
                                               in1=cols_a[:, gain:gain + KT], op0=ALU.add,
                                               op1=ALU.mult))

            def modulate(hf, hl, hh, mc, gc, s_f, s_h, s_l):
                for k in range(KT + 1):
                    if k < KT:
                        v.tensor_scalar(hf[:, k, :], hf[:, k, :], gc[:, k:k + 1], mc[:, k:k + 1],
                                        ALU.mult, ALU.add).then_inc(s_f, 1)
                    if k > 0:
                        dve.wait_ge(s_h, k)
                        v.tensor_tensor(hl[:, k - 1, :], hf[:, k - 1, :],
                                        hh[:, k - 1, :].bitcast(F32),
                                        ALU.subtract).then_inc(s_l, 1)

            dve.wait_ge(s_ada_mm, 1)
            modulation(mcol, gcol, 0, CA_GM, ps[:, 7, 0:2 * KT])
            dve.wait_ge(s_xev, NC)
            modulate(hn_f, hn_lo, hn_hi, mcol, gcol, s_hf, s_hhi, s_hlo)

            dve.wait_ge(s_const, 2)
            for t in range(PT):
                dve.wait_ge(s_evac, t + 1)
                u = seqb[t]
                cur = u
                rows = slice(0, P)
                done = {}
                for n, sh in enumerate((1, 2) if t == 0 else (1, 2, 4, 8)):
                    dst = acc[n % 2]
                    w = 2 * sh
                    r = rows if w <= WINDOWS[2 * t] else slice(64, P)
                    lo = w - 1
                    ch.link(v.tensor_tensor(dst[r, lo:SW], cur[r, lo:SW], cur[r, lo - sh:SW - sh],
                                            ALU.add))
                    cur = dst
                    for hf in range(2):
                        if WINDOWS[2 * t + hf] == w:
                            done[hf] = dst
                for hf in range(2):
                    w = WINDOWS[2 * t + hf]
                    r = slice(64 * hf, 64 * hf + 64)
                    s_ = done[hf]
                    v.scalar_tensor_tensor(out=ypool[r, t, PAD:SEQ], in0=s_[r, 2 * PAD:SW],
                                           scalar=1.0 / w, in1=u[r, 2 * PAD:SW], op0=ALU.mult,
                                           op1=ALU.subtract)
                    ch.link(v.tensor_tensor(ypool[r, t, 0:PAD], s_[r, PAD:2 * PAD],
                                            rcnt[r, t, :], ALU.mult))
                    last = v.tensor_tensor(ypool[r, t, 0:PAD], ypool[r, t, 0:PAD],
                                           u[r, PAD:2 * PAD], ALU.subtract)
                    if hf == 0:
                        ch.link(last)
                last.then_inc(s_seq, 1)
            dve.wait_ge(s_batr, 1)
            v.tensor_copy(ba[:, :, :], ps[:, 6, 0:32 * NC].rearrange(
                "p (c r) -> p c r", r=32)[:, :, BA_ROW:BA_ROW + 2 * HEADS]).then_inc(s_seq, 1)

            def conv(n, dyn):
                slot, o = (n + 1) % 2, n % 2
                t = dyn + (T0 + 1)
                dve.wait_ge(s_evac, t)
                if conv.guard is not None:
                    dve.wait_ge(s_aout, conv.guard)
                src, dst = seqb[slot], acc[o]

                cb = cols_b
                for j in (3, 2, 1, 0):
                    col = cb[:, bass.ds(dyn + j * QKVT, 1)]
                    s_ = src[:, PAD - 3 + j:PAD - 3 + j + SEQ]
                    if j == 3:
                        ch.link(v.tensor_scalar(dst[:, 0:SEQ], s_, col, None, ALU.mult))
                    else:
                        last = v.scalar_tensor_tensor(out=dst[:, 0:SEQ], in0=s_, scalar=col,
                                                      in1=dst[:, 0:SEQ], op0=ALU.mult,
                                                      op1=ALU.add)
                        if j > 0:
                            ch.link(last)
                last.then_inc(s_conv, 1)

            def ada_rest(k, first):
                ccol = cols_a[:, bass.ds(k + CA_C, 1)]
                for s in range(2):
                    dst = ada_acc[:, 2 * s * D_MODEL:2 * (s + 1) * D_MODEL]
                    dve.wait_ge(s_ada[s], k * 16 + 32)
                    if first:
                        v.tensor_scalar(dst, ada_w[s][:, :], ccol, None,
                                        ALU.mult).then_inc(s_ada_used, 1)
                    else:
                        dve.wait_ge(s_ada_used, k * 2 + (KT - 1 + s))
                        v.scalar_tensor_tensor(out=dst, in0=ada_w[s][:, :], scalar=ccol, in1=dst,
                                               op0=ALU.mult, op1=ALU.add).then_inc(s_ada_used, 1)

            aa = ba[:, :, HEADS:2 * HEADS]
            dve.wait_ge(s_x, 128)
            dve.wait_ge(s_seq, PT + 1)
            ch.link(v.tensor_tensor(spt[:, 1, :, :], aa,
                                    dt_b[:, :].unsqueeze(1).to_broadcast([P, NC, HEADS]), ALU.add))
            ch.link(v.tensor_scalar(spt[:, 2, :, :], spt[:, 1, :, :], -1.0, None, ALU.mult))
            v.tensor_tensor(spt[:, 0, :, :], spt[:, 1, :, :], spt[:, 2, :, :],
                            ALU.max).then_inc(s_sp, 1)
            conv.guard = None
            conv(0, 0)
            dve.wait_ge(s_spa, 3)
            ch.link(v.tensor_scalar(allsc[:, :, S_BETA, :], allsc[:, :, S_BETA, :], 1.0, None,
                                    ALU.add))
            ch.link(v.reciprocal(allsc[:, :, S_BETA, :], allsc[:, :, S_BETA, :]))
            v.tensor_scalar(spt[:, 0, :, :], spt[:, 0, :, :], 1.0, None, ALU.add).then_inc(s_sp, 1)
            ch.link(v.tensor_scalar(spt[:, 1, :, :], spt[:, 1, :, :], 0.0, None, ALU.max))
            conv(1, 1)
            dve.wait_ge(s_spa, 4)
            ch.link(v.tensor_tensor(spt[:, 2, :, :], spt[:, 1, :, :], spt[:, 0, :, :], ALU.add))
            ch.link(v.tensor_tensor(spt[:, 1, :, :], spt[:, 2, :, :],
                                    al_b[:, :].unsqueeze(1).to_broadcast([P, NC, HEADS]),
                                    ALU.mult))
            ch.link(v.tensor_scalar(spt[:, 0, :, :], spt[:, 1, :, :], -1.0, None, ALU.mult))
            v.tensor_copy(allsc[:, :, S_G, :], spt[:, 0, :, :]).then_inc(s_sp, 1)
            ada_rest(0, True)
            with dve.Fori(1, 8) as i:
                ch.enter(i - 1, 6)
                for j in range(2):
                    conv.guard = i * 2 + (j - 1)
                    conv(j, i * 2 + j)
                ada_rest(i, False)
            ch.leave(7, 6)
            for n in (16, 17):
                conv.guard = n - 1
                conv(n, n)
            dve.wait_ge(s_fsum, 1)
            modulation(fcol, gcol_f, 3 * KT, CA_GF, fsum[:, :])
            dve.wait_ge(s_x, 128)
            for gt, gate in enumerate((gate_m, gate_f)):
                dve.wait_ge(s_gmm, gt + 1)
                v.tensor_tensor(gate[:, :], gate[:, :], bank2(4 + 2 * gt), ALU.add).then_inc(s_gev, 1)
            dve.wait_ge(s_pss, PT + 1)
            v.tensor_scalar(ssf[:, 0:NC], ssf[:, NC:2 * NC], 1.0 / POOL_W, EPS, ALU.mult,
                            ALU.add).then_inc(s_pst, 1)
            dve.wait_ge(s_pmm, 3)
            for t in range(PT):
                v.scalar_tensor_tensor(out=ypool[:, t, :], in0=ypool[:, t, :],
                                              scalar=cols_b[:, CB_PS + t:CB_PS + t + 1],
                                              in1=bank2(6), op0=ALU.mult, op1=ALU.mult)
            def square_sums(cc, q):
                r = slice(0, HEADS) if q else slice(HEADS, 2 * HEADS)
                dve.wait_ge(s_sq, cc * 4 + (2 * q + 2))
                v.tensor_scalar(ssb[:, r], ssq[:, r], EPS, None, ALU.add).then_inc(s_ssr, 1)

            def scalars(cc, s):
                rk = rr[s][:, HEADS:2 * HEADS]
                ch.link(v.tensor_copy(sc[s][:, :, :], allsc[:, bass.ds(cc, 1), :, :].rearrange(
                    "p a b h -> p (a b) h")))
                dve.wait_ge(s_rr, cc * 2 + 1)
                v.scalar_tensor_tensor(out=nbk[:, :], in0=rk, scalar=-1.0,
                                       in1=sc[s][:, S_BETA, :], op0=ALU.mult, op1=ALU.mult)
                v.tensor_tensor(kdec[:, :], rk, sc[s][:, S_ED, :], ALU.mult).then_inc(s_scc, 1)

            def q_scalars(cc, s):
                rq = rr[s][:, 0:HEADS]
                dve.wait_ge(s_rr, cc * 2 + 2)
                ch.link(v.scalar_tensor_tensor(out=rq2[s][:, :], in0=rq, scalar=1.0 / HD, in1=rq,
                                               op0=ALU.mult, op1=ALU.mult))

            def p_k(cc, s):
                dve.wait_ge(s_scc, cc + 1)
                for gr in range(2):
                    dve.wait_ge(s_ktr, cc * 2 + (gr + 1))
                    v.tensor_tensor(kb[:, G3 * gr:G3 * gr + G3, :], grp3(2 * gr), bc(nbk, gr),
                                    ALU.mult).then_inc(s_kbd, 1)
                for gr in range(2):
                    v.tensor_tensor(Kd[s][:, G3 * gr:G3 * gr + G3, :], grp3(2 * gr),
                                    bc(kdec, gr), ALU.mult).then_inc(s_kdd, 1)

            def p_vb(cc, s):
                for gr in range(2):
                    dve.wait_ge(s_vtr, cc * 2 + (gr + 1))
                    v.tensor_tensor(Vb[s][:, G3 * gr:G3 * gr + G3, :], grp3(2 * gr + 1),
                                    bc(sc[s][:, S_BETA, :], gr), ALU.mult).then_inc(s_vb, 1)

            def p_na(cc, s):
                for gr in range(2):
                    dve.wait_ge(s_qk, cc * 2 + (gr + 1))
                    dve.wait_ge(s_e, cc * 2 + (gr + 1))
                    v.tensor_tensor(flat(QD[s], gr), grp(5 + 2 * gr), flat(Em, gr),
                                    ALU.mult).then_inc(s_qd, 1)
                for gr in range(2):
                    dve.wait_ge(s_kk, cc * 2 + (gr + 1))
                    dve.wait_ge(s_ti, cc + 1)
                    v.tensor_tensor(flat(NA, gr), grp(2 * gr), flat(Em, gr),
                                    ALU.mult).then_inc(s_na, 1)

            def masked(dst, gr, lv, src):
                h = slice(G3 * gr, G3 * gr + G3)
                return v.copy_predicated(dst[:, h, :],
                                         lmask[:, lv, :].bitcast(I16).unsqueeze(1).to_broadcast(
                                             [P, G3, P]), src)

            def level_u0(cc, s):
                for gr in range(2):
                    count = settled(dve, cc * 2 + (gr + 1))
                    dve.wait_ge(s_const, 2)
                    dve.wait_ge(s_na, count)
                    masked(Um[s], gr, 0, NA[:, G3 * gr:G3 * gr + G3, :]).then_inc(s_uz, 1)

            def level_t(cc, s, lv):
                for gr in range(2):
                    count = settled(dve, cc * (2 * LEVELS - 2) + (2 * lv + gr - 1))
                    dve.wait_ge(s_const, 2)
                    dve.wait_ge(s_y, count)
                    if lv < LEVELS - 1:
                        masked(Tm, gr, lv, grp3(2 * gr + 1)).then_inc(s_t, 1)
                    else:
                        masked(Um[s], gr, lv, grp3(2 * gr + 1)).then_inc(s_uf, 1)

            def r_rhs(cc, s):
                for gr in range(2):
                    dve.wait_ge(s_ks, cc * 2 + (gr + 1))
                    for n in range(G3):
                        h = G3 * gr + n
                        last = v.scalar_tensor_tensor(
                            out=Rm[:, h, :], in0=ps[:, 4 + 2 * gr, n * P:(n + 1) * P],
                            scalar=sc[s][:, S_EG, h:h + 1], in1=Vb[s][:, h, :],
                            op0=ALU.mult, op1=ALU.add)
                    last.then_inc(s_r, 1)

            def r_state(cc, s):
                for gr in range(2):
                    dve.wait_ge(s_sd, cc * 2 + (gr + 1))
                    for n in range(G3):
                        h = G3 * gr + n
                        last = v.scalar_tensor_tensor(
                            out=Sm[:, h, :], in0=Sm[:, h, :], scalar=sc[s][:, S_EL, h:h + 1],
                            in1=ps[:, 4 + 2 * gr, n * P:(n + 1) * P], op0=ALU.mult, op1=ALU.add)
                    last.then_inc(s_s, 1)

            def r_o(cc, s):
                for gr in range(2):
                    dve.wait_ge(s_o2, cc * 2 + (gr + 1))
                    for n in range(G3):
                        h = G3 * gr + n
                        last = v.scalar_tensor_tensor(
                            out=om[:, h, :], in0=om[:, h, :], scalar=sc[s][:, S_EG, h:h + 1],
                            in1=ps[:, 5 + 2 * gr, n * P:(n + 1) * P], op0=ALU.mult, op1=ALU.add)
                    last.then_inc(s_o, 1)

            def r_on(cc, s):
                dve.wait_ge(s_sso, cc * 2 + 2)
                ch.link(v.tensor_tensor(oc[:, 0, :], sso[:, :], rq2[s][:, :], ALU.mult))
                v.tensor_tensor(oc[:, 1, :], oc[:, 0, :], epsh[:, :], ALU.add).then_inc(s_oss, 1)
                dve.wait_ge(s_ort, cc + 1)
                ch.link(v.tensor_tensor(oc[:, 3, :], oc[:, 2, :], rr[s][:, 0:HEADS], ALU.mult))
                for gr in range(2):
                    o = om[:, G3 * gr:G3 * gr + G3, :]
                    v.tensor_tensor(o, o, bc(oc[:, 3, :], gr), ALU.mult).then_inc(s_on, 1)

            def r_ylo_pool(cc):
                count = settled(dve, cc * 3 + 1)
                dve.wait_ge(s_const, 2)
                dve.wait_ge(s_yhi, count)
                v.tensor_tensor(y_lo[:, 0:PT, :], ypool[:, :, bass.ds(cc * P, P)],
                                y_hi[:, 0:PT, :].bitcast(F32), ALU.subtract).then_inc(s_ylo, 1)

            def r_y(cc, s, z_dma):
                dve.wait_ge(s_stz[s], z_dma)
                for gr in range(2):
                    dve.wait_ge(s_otr, cc * 2 + (gr + 1))
                    z = stage[s][:, QKVT + G3 * gr:QKVT + G3 * gr + G3, :].rearrange(
                        "p h n -> p (h n)")
                    v.scalar_tensor_tensor(out=flat(om, gr), in0=grp(5 + 2 * gr),
                                           scalar=cols_b[:, CB_GG:CB_GG + 1], in1=z,
                                           op0=ALU.mult, op1=ALU.mult).then_inc(s_yf, 1)

            def r_ylo(cc):
                for gr in range(2):
                    dve.wait_ge(s_yhi, cc * 3 + (gr + 2))
                    r = slice(PT + G3 * gr, PT + G3 * gr + G3)
                    v.tensor_tensor(y_lo[:, r, :], om[:, G3 * gr:G3 * gr + G3, :],
                                    y_hi[:, r, :].bitcast(F32), ALU.subtract).then_inc(s_ylo, 1)

            def r_h2(cc):
                dve.wait_ge(s_op, cc + 1)
                dve.wait_ge(s_xin, cc * 16 + 16)
                x_ = flat(xt)
                v.tensor_tensor(x_[:, 0:HALF], ps[:, 4, :], x_[:, 0:HALF], ALU.add)
                v.tensor_tensor(x_[:, HALF:], ps[:, 6, :], x_[:, HALF:],
                                ALU.add).then_inc(s_h2, 1)

            def r_mean(cc):
                dve.wait_ge(s_h2sq, cc + 1)
                v.tensor_scalar(ssx2[:, 1:2], ssx2[:, 0:1], 1.0 / D_MODEL, EPS, ALU.mult,
                                ALU.add).then_inc(s_ssx2, 1)

            def r_xn(cc):
                dve.wait_ge(s_rst2, cc + 1)
                v.tensor_scalar(flat(xn2), flat(xt), rst2[:, 0:1], None,
                                ALU.mult).then_inc(s_xn2, 1)

            def body(cc, s, z_dma, first=False, last=False):
                if not first:
                    r_mean(cc - 2)
                p_k(cc, s)
                if not first:
                    r_xn(cc - 2)
                p_na(cc, s)
                level_u0(cc, s)
                p_vb(cc, s)
                q_scalars(cc, s)
                r_rhs(cc - 1, 1 - s)
                if first:
                    wo_lo_sub(3)
                level_t(cc, s, 1)
                if first:
                    wo_lo_sub(4)
                r_state(cc - 1, 1 - s)
                r_o(cc - 1, 1 - s)
                r_ylo_pool(cc - 1)
                level_t(cc, s, 2)
                if first:
                    wo_lo_sub(5)
                r_on(cc - 1, 1 - s)
                r_y(cc - 1, 1 - s, z_dma)
                level_t(cc, s, 3)
                r_ylo(cc - 1)
                if first:
                    wo_lo_sub(6)
                    wo_lo_sub(7)
                level_t(cc, s, 4)
                if not last:
                    square_sums(cc + 1, 0)
                level_t(cc, s, 5)
                if not last:
                    scalars(cc + 1, 1 - s)
                    square_sums(cc + 1, 1)
                r_h2(cc - 1)
                level_t(cc, s, 6)

            square_sums(0, 0)
            dve.wait_ge(s_ex, 1)
            scalars(0, 0)
            v.memset(Sm[:, :, :], 0.0).then_inc(s_scr, 1)

            def wo_lo_sub(k):
                dve.wait_ge(s_wohi, k + 1)
                v.tensor_tensor(wo_lo[:, k, :], wo_raw[:, k, :], wo_hi[:, k, :].bitcast(F32),
                                ALU.subtract).then_inc(s_wosp, 1)

            p_k(0, 0)
            p_na(0, 0)
            level_u0(0, 0)
            p_vb(0, 0)
            square_sums(0, 1)
            for lv in range(1, LEVELS):
                level_t(0, 0, lv)
                if lv == 3:
                    q_scalars(0, 0)
                if lv == 4:
                    square_sums(1, 0)
                if lv == 5:
                    square_sums(1, 1)
                if lv == 6:
                    scalars(1, 1)
                if lv > 3:
                    wo_lo_sub(lv - 4)
            PER = 2 * 4
            body(1, 1, 16, first=True)
            body(2, 0, 16)
            with dve.Fori(1, 3) as i:
                ch.enter(i - 1, PER)
                body(i * 2 + 1, 1, i * 16 + 16)
                body(i * 2 + 2, 0, i * 16 + 16)
            ch.leave(2, PER)
            body(7, 1, 64, last=True)
            def lo_sub(lo, raw, hi, n):
                dve.wait_ge(s_uhi, n)
                v.tensor_tensor(lo[:, :, :], raw[:, :, :], hi[:, :, :].bitcast(F32),
                                ALU.subtract).then_inc(s_ulo, 1)

            def u_lo_sub(s, n):
                lo_sub(u_lo[s], u_raw[s], u_hi[s], n)

            def f_lo_sub(k, half):
                r = slice(half * HALF, (half + 1) * HALF)
                dve.wait_ge(s_f_hi, half * KT + k + 1)
                v.tensor_tensor(h2n_lo[:, k, r], h2n_f[:, k, r], h2n_hi[:, k, r].bitcast(F32),
                                ALU.subtract).then_inc(s_f_lo, 1)

            r_mean(6)
            r_rhs(7, 1)
            r_xn(6)
            r_o(7, 1)
            r_ylo_pool(7)
            r_on(7, 1)
            r_y(7, 1, 64)
            r_ylo(7)
            lo_sub(f_lo[0], f_raw[0], f_hi[0], 1)
            lo_sub(f_lo[1], f_raw[1], f_hi[1], 2)
            r_h2(7)

            for k in range(2):
                f_lo_sub(k, 0)
            r_mean(7)
            r_xn(7)
            for k in range(2, 4):
                f_lo_sub(k, 0)
            for k in range(KT):
                if k % 4 == 0:
                    dve.wait_ge(s_htr, 2 * NC - 1 + k // 4)
                last = v.tensor_scalar(h2n_f[:, k, SEQ - P:SEQ],
                                       ps[:, 4 + 2 * (k // 4), (k % 4) * P:(k % 4 + 1) * P],
                                       gcol_f[:, k:k + 1], fcol[:, k:k + 1], ALU.mult, ALU.add)
                if k % 4 == 3:
                    last.then_inc(s_h2n, 1)
            for k in range(4, KT):
                f_lo_sub(k, 0)
            for k in range(KT):
                f_lo_sub(k, 1)
            u_lo_sub(2, 3)
            u_lo_sub(3, 4)

            def hidden(f, b):
                dve.wait_ge(s_sil, f + 1)
                v.tensor_tensor(hid[:, bass.ds(f, 1), :].rearrange("p a n -> p (a n)"),
                                silu_t[:, :], bank2(b + 2), ALU.mult).then_inc(s_hid, 1)

            with dve.Fori(0, FT // 2 - 1) as i:
                hidden(i * 2, 0)
                u_lo_sub(0, i * 4 + 5)
                u_lo_sub(1, i * 4 + 6)
                hidden(i * 2 + 1, 4)
                u_lo_sub(2, i * 4 + 7)
                u_lo_sub(3, i * 4 + 8)
            hidden(FT - 2, 0)

            def d_lo_sub(k, h, s, n):
                dve.wait_ge(s_dhi, n)
                v.tensor_tensor(d_lo[s][:, :], d_raw[s][:, :], d_hi[s][:, :].bitcast(F32),
                                ALU.subtract)
                v.tensor_tensor(a_lo[s][:, :],
                                hid[:, bass.ds(k, 1), h * HALF:(h + 1) * HALF].rearrange(
                                    "p a n -> p (a n)"), a_hi[s][:, :].bitcast(F32),
                                ALU.subtract).then_inc(s_dlo, 1)

            d_lo_sub(0, 0, 0, 1)
            hidden(FT - 1, 4)
            for n in range(1, 4):
                d_lo_sub(n, 0, n, n + 1)
            with dve.Fori(1, 5) as i:
                for j in range(4):
                    d_lo_sub(i * 4 + j, 0, j, i * 4 + (j + 1))
            for n in range(20, 24):
                d_lo_sub(n % FT, n // FT, n % 4, n + 1)
            dve.wait_ge(s_fg, 16)


            def residual(t):
                if t % 4 < 3:
                    dve.wait_ge(s_dmm, 3 * (t // 4) + t % 4 + 1)
                else:
                    dve.wait_ge(s_down, FT if t < 4 else 2 * FT - 3 + 1)
                if t >= 4:
                    dve.wait_ge(s_out, 16 * 4)
                v.tensor_tensor(fin[t % 4][:, :], bank2(2 * (t % 4)), gate_f[:, :],
                                ALU.mult).then_inc(s_dev, 1)
                dve.wait_ge(s_dev, t + 1)
                dve.wait_ge(s_hre[t % 4], 16 * (t // 4 + 1))
                v.tensor_tensor(h_re[t % 4][:, :], h_re[t % 4][:, :], fin[t % 4][:, :],
                                ALU.add).then_inc(s_fh, 1)

            def finish(t):
                dve.wait_ge(s_fsq, t + 1)
                v.tensor_scalar(ssf[:, t:t + 1], ssf[:, t:t + 1], 1.0 / D_MODEL, EPS,
                                ALU.mult, ALU.add).then_inc(s_fss, 1)
                dve.wait_ge(s_frs, t + 1)
                v.scalar_tensor_tensor(out=fin[t % 4][:, :], in0=h_re[t % 4][:, :],
                                       scalar=ssf[:, NC + t:NC + t + 1], in1=fgain[:, :],
                                       op0=ALU.mult, op1=ALU.mult).then_inc(s_fin, 1)

            for t in range(4):
                residual(t)
            for n in range(24, 28):
                d_lo_sub(n - FT, 1, n % 4, n + 1)
            for t in range(4):
                finish(t)
            with dve.Fori(7, 11) as i:
                for j in range(4):
                    d_lo_sub(i * 4 + (j - 22), 1, j, i * 4 + (j + 1))
            residual(4)
            for t in range(5, NC):
                residual(t)
                finish(t - 1)
            finish(NC - 1)

        @block.tensor
        def _(pe):
            t_ = nc.tensor
            pe.wait_ge(s_small, 16 * 7)
            pe.wait_ge(s_const, 1)
            t_.transpose(ps[:, 6, 0:SMALL_A], rows_a[0:SMALL_A, :], ident[0:SMALL_A, 0:SMALL_A])
            t_.transpose(ps[:, 6, P:P + SMALL_B], rows_b[0:SMALL_B, :],
                         ident[0:SMALL_B, 0:SMALL_B]).then_inc(s_rows_tr, 1)
            for t in range(NC):
                pe.wait_ge(s_xn, t + 1)
                if t >= 2:
                    pe.wait_ge(s_xev, t - 1)
                for k in range(KT):
                    last = t_.transpose(bank2(2 * (t % 2))[:, k * P:(k + 1) * P],
                                        x_sl[t][:, k * P:(k + 1) * P], ident[:, :])
                last.then_inc(s_xtr, 1)

            def ada_columns(base):
                for n in range(2 * KT):
                    last = t_.matmul(ps[:, 7, n:n + 1],
                                     ada_acc[:, base + n * P:base + (n + 1) * P],
                                     ones[:, 0:1], start=True, stop=True)
                last.then_inc(s_ada_mm, 1)

            pe.wait_ge(s_ada_used, KT)
            ada_columns(0)

            def project(slot, bank, hi, lo, between=None):
                for k in range(KT):
                    if between is not None and k == KT // 2:
                        between()
                    if project.first:
                        pe.wait_ge(s_hlo, k + 1)
                    for n, (w, h) in enumerate(((w_lo, hi), (w_hi, lo), (w_hi, hi))):
                        for b in range(2):
                            last = t_.matmul(ps[:, bank + b, :], w[slot][:, k, :],
                                             h[:, k, b * HALF:(b + 1) * HALF],
                                             start=(k == 0 and n == 0),
                                             stop=(k == KT - 1 and n == 2))
                project.first = False
                last.then_inc(s_proj, 1)

            project.first = True
            for t in range(T0):
                pe.wait_ge(s_wsplit, t + 1)
                if t >= 2:
                    pe.wait_ge(s_evac, t - 1)
                elif t == 0:
                    pe.wait_ge(s_xev, NC)
                project(t, 2 * (t % 2), hn_hi, hn_lo)
            pe.wait_ge(s_evac, 3)
            for cc in range(NC):
                last = t_.transpose(ps[:, 6, 32 * cc:32 * cc + 32],
                                    seqb[0][0:32, PAD + cc * P:PAD + (cc + 1) * P],
                                    ident[0:32, 0:32])
            last.then_inc(s_batr, 1)

            def tile(t, between=None):
                pe.wait_ge(s_wsplit, t + 1)
                pe.wait_ge(s_evac, t - 1)
                project(t % 4, 2 * (t % 2), hn_hi, hn_lo, between)

            for t in range(T0, T0 + 4):
                tile(t)
            pe.wait_ge(s_sp, 3)
            n48 = NC * HEADS
            for n, m in enumerate((tri, below, ones)):
                last = t_.matmul(ps[:, 6, n * n48:(n + 1) * n48], m[:, :],
                                 spt[:, 0, :, :].rearrange("p c h -> p (c h)"),
                                 start=True, stop=True)
            last.then_inc(s_gmx, 1)
            with pe.Fori(1, 4) as i:
                for j in range(4):
                    pe.wait_ge(s_wsplit, i * 4 + (T0 + j + 1))
                    pe.wait_ge(s_evac, i * 4 + (T0 + j - 1))
                    project((T0 + j) % 4, 2 * ((T0 + j) % 2), hn_hi, hn_lo)
            TZ = T0 + QKVT
            for t in range(T0 + 16, TZ + 1):
                tile(t)
            pe.wait_ge(s_ada_used, 3 * KT)
            pe.wait_ge(s_ex, 1)
            for n in range(2 * KT):
                last = t_.transpose(ps[:, 4 + n // 4, (n % 4) * P:(n % 4 + 1) * P],
                                    ada_acc[:, D_MODEL + n * P:D_MODEL + (n + 1) * P],
                                    ident[:, :])
            last.then_inc(s_ada_mm, 1)
            def gate(gt):
                for b in range(2):
                    last = t_.matmul(ps[:, 4 + 2 * gt + b, :], ones[:, :],
                                     ada_acc[:, gt * 3 * D_MODEL + b * HALF:
                                             gt * 3 * D_MODEL + (b + 1) * HALF],
                                     start=True, stop=True)
                last.then_inc(s_gmm, 1)

            tile(TZ + 1)
            pe.wait_ge(s_fsum, 1)
            gate(0)
            gate(1)
            tile(TZ + 2)
            pe.wait_ge(s_gev, 2)
            pe.wait_ge(s_x, 128)
            for t in range(PT):
                for b in range(2):
                    last = t_.matmul(ps[:, 4 + 2 * t + b, :], wpb[:, t, :],
                                     ypool[:, t, b * HALF:(b + 1) * HALF], start=True, stop=True)
            last.then_inc(s_pmm, 1)
            tile(TZ + 3)
            pe.wait_ge(s_pss, PT)
            for n in range(NC):
                for t in range(PT):
                    o = (n % 2) * POOL_W + t * P
                    last = t_.transpose(ps[:, 4 + n // 2, o:o + P],
                                        ypool[:, t, n * P:(n + 1) * P], ident[:, :])
            last.then_inc(s_pmm, 1)
            tile(TZ + 4)
            pe.wait_ge(s_prt, 1)
            for n in range(NC):
                last = t_.matmul(bank2(6)[:, n * P:(n + 1) * P],
                                 ssf[:, NC + n:NC + n + 1].to_broadcast([P, P]), ident[:, :],
                                 start=True, stop=True)
            last.then_inc(s_pmm, 1)

            def norm_tr(cc, s, q, bank, dma):
                if q == 0:
                    pe.wait_ge(s_stg[s], dma)
                for gr in range(2):
                    if q:
                        pe.wait_ge(s_sq, cc * 4 + (gr + 1))
                    for n in range(G3):
                        last = t_.transpose(ps[:, bank[gr], n * P:(n + 1) * P],
                                            stage[s][:, (0 if q else HEADS) + G3 * gr + n, :],
                                            ident[:, :])
                    last.then_inc(s_ntr, 1)

            def p_arg(cc):
                pe.wait_ge(s_sq, cc * 4 + 4)
                for gr in range(2):
                    pe.wait_ge(s_slg, cc * 2 + (gr + 1))
                    for n in range(G3):
                        last = t_.matmul(ps[:, 5 + 2 * gr, n * P:(n + 1) * P],
                                         slg[:, G3 * gr + n, :], tri[:, :], start=True, stop=True)
                    last.then_inc(s_arg, 1)

            def p_ktr(cc, s):
                for gr in range(2):
                    if not (isinstance(cc, int) and cc == 0):
                        pe.wait_ge(s_xc, cc * (2 * LEVELS - 2) + (gr - 1))
                    for n in range(G3):
                        last = t_.transpose(ps[:, 2 * gr, n * P:(n + 1) * P],
                                            stage[s][:, HEADS + G3 * gr + n, :], ident[:, :])
                    last.then_inc(s_ktr, 1)

            def p_qk(cc, s):
                for gr in range(2):
                    pe.wait_ge(s_exp, cc * 2 + (gr + 1))
                    for n in range(G3):
                        h = G3 * gr + n
                        last = t_.matmul(ps[:, 5 + 2 * gr, n * P:(n + 1) * P],
                                         stage[s][:, HEADS + h, :], stage[s][:, h, :],
                                         start=True, stop=True)
                    last.then_inc(s_qk, 1)

            def p_kb(cc):
                for gr in range(2):
                    pe.wait_ge(s_kbd, cc * 2 + (gr + 1))
                    for n in range(G3):
                        last = t_.transpose(ps[:, 2 * gr + 1, n * P:(n + 1) * P],
                                            kb[:, G3 * gr + n, :], ident[:, :])
                    last.then_inc(s_kbtr, 1)

            def p_kk(cc, s):
                for gr in range(2):
                    pe.wait_ge(s_kdd, cc * 2 + (gr + 1))
                    pe.wait_ge(s_kbT, cc * 2 + (gr + 1))
                    for n in range(G3):
                        h = G3 * gr + n
                        last = t_.matmul(ps[:, 2 * gr, n * P:(n + 1) * P],
                                         stage[s][:, HEADS + h, :], KbT[s][:, h, :],
                                         start=True, stop=True)
                    last.then_inc(s_kk, 1)

            def p_vtr(cc, s):
                for gr in range(2):
                    for n in range(G3):
                        last = t_.transpose(ps[:, 2 * gr + 1, n * P:(n + 1) * P],
                                            stage[s][:, 2 * HEADS + G3 * gr + n, :], ident[:, :])
                    last.then_inc(s_vtr, 1)

            def level_0(cc, s):
                for gr in range(2):
                    pe.wait_ge(s_uz, cc * 2 + (gr + 1))
                    for n in range(G3):
                        last = t_.transpose(ps[:, 2 * gr, n * P:(n + 1) * P],
                                            Um[s][:, G3 * gr + n, :], ident[:, :])
                    last.then_inc(s_utr, 1)

            def level_x(cc, lv):
                for gr in range(2):
                    pe.wait_ge(s_u, cc * (2 * LEVELS - 2) + (2 * (lv - 1) + gr + 1))
                    for n in range(G3):
                        h = G3 * gr + n
                        last = t_.matmul(ps[:, 2 * gr, n * P:(n + 1) * P], NA[:, h, :],
                                         Tm[:, h, :], start=True, stop=True)
                    last.then_inc(s_xmm, 1)

            def level_y(cc, s, lv):
                for gr in range(2):
                    pe.wait_ge(s_xc, cc * (2 * LEVELS - 2) + (2 * (lv - 1) + gr + 1))
                    if lv == 1:
                        pe.wait_ge(s_vb, cc * 2 + (gr + 1))
                    for n in range(G3):
                        h = G3 * gr + n
                        u_, x_ = Um[s][:, h, :], Xm[:, h, :]
                        if lv == LEVELS - 1:
                            u_, x_ = x_, u_
                        last = t_.matmul(ps[:, 2 * gr + 1, n * P:(n + 1) * P], u_, x_,
                                         start=True, stop=True)
                    last.then_inc(s_y, 1)

            def level_tr(cc, lv):
                for gr in range(2):
                    pe.wait_ge(s_t, cc * (2 * LEVELS - 4) + (2 * (lv - 1) + gr + 1))
                    for n in range(G3):
                        last = t_.transpose(ps[:, 2 * gr, n * P:(n + 1) * P],
                                            Tm[:, G3 * gr + n, :], ident[:, :])
                    last.then_inc(s_utr, 1)

            def r1_ks(cc, s, first, last_chunk=False):
                for gr in range(2):
                    if last_chunk:
                        pe.wait_ge(s_s, cc * 2 + (gr - 1))
                        pe.wait_ge(s_h2, cc)
                    elif not first:
                        pe.wait_ge(s_s, cc * 2 + (gr - 1))
                        pe.wait_ge(s_h2n, cc * 2)
                    for n in range(G3):
                        h = G3 * gr + n
                        last = t_.matmul(ps[:, 4 + 2 * gr, n * P:(n + 1) * P], KbT[s][:, h, :],
                                         Sm[:, h, :], start=True, stop=True)
                    last.then_inc(s_ks, 1)

            def r1_o1(cc, s, last_chunk=False, groups=(0, 1)):
                for gr in groups:
                    if not last_chunk:
                        pe.wait_ge(s_qd, cc * 2 + (gr + 3))
                    for n in range(G3):
                        h = G3 * gr + n
                        last = t_.matmul(ps[:, 5 + 2 * gr, n * P:(n + 1) * P], stage[s][:, h, :],
                                         Sm[:, h, :], start=True, stop=True)
                    last.then_inc(s_o1, 1)

            def r2(cc, s):
                for gr in range(2):
                    pe.wait_ge(s_uf, cc * 2 + (gr + 1))
                    pe.wait_ge(s_r, cc * 2 + (gr + 1))
                    for n in range(G3):
                        h = G3 * gr + n
                        last = t_.matmul(ps[:, 4 + 2 * gr, n * P:(n + 1) * P], Um[s][:, h, :],
                                         Rm[:, h, :], start=True, stop=True)
                    last.then_inc(s_vmm, 1)

            def r3_state(cc, s):
                for gr in range(2):
                    pe.wait_ge(s_v, cc * 2 + (gr + 1))
                    for n in range(G3):
                        h = G3 * gr + n
                        last = t_.matmul(ps[:, 4 + 2 * gr, n * P:(n + 1) * P], Kd[s][:, h, :],
                                         Rm[:, h, :], start=True, stop=True)
                    last.then_inc(s_sd, 1)

            def r3_o2(cc, s):
                for gr in range(2):
                    pe.wait_ge(s_v, cc * 2 + (gr + 1))
                    pe.wait_ge(s_o1c, cc * 2 + (gr + 1))
                    for n in range(G3):
                        h = G3 * gr + n
                        last = t_.matmul(ps[:, 5 + 2 * gr, n * P:(n + 1) * P], QD[s][:, h, :],
                                         Rm[:, h, :], start=True, stop=True)
                    last.then_inc(s_o2, 1)

            def r4(cc):
                for gr in range(2):
                    pe.wait_ge(s_on, cc * 2 + (gr + 1))
                    for n in range(G3):
                        last = t_.transpose(ps[:, 5 + 2 * gr, n * P:(n + 1) * P],
                                            om[:, G3 * gr + n, :], ident[:, :])
                    last.then_inc(s_otr, 1)

            def mix(cc, k):
                if k == 0:
                    pe.wait_ge(s_ylo, cc * 3 + 1)
                    if cc is not mix.last:
                        pe.wait_ge(s_s, cc * 2 + 2)
                if k == PT:
                    pe.wait_ge(s_ylo, cc * 3 + 3)
                if cc is mix.first:
                    pe.wait_ge(s_wosp, k + 1)
                for n, (y, w) in enumerate(((y_lo, wo_hi), (y_hi, wo_lo), (y_hi, wo_hi))):
                    for b in range(2):
                        last = t_.matmul(ps[:, 4 + 2 * b, :], y[:, k, :],
                                         w[:, k, b * HALF:(b + 1) * HALF],
                                         start=(k == 0 and n == 0),
                                         stop=(k == KT - 1 and n == 2))
                if k == KT - 1:
                    last.then_inc(s_op, 1)

            def r6(cc, bank=4):
                pe.wait_ge(s_xn2, cc + 1)
                for h in range(2):
                    for n in range(4):
                        last = t_.transpose(ps[:, bank + 2 * h, n * P:(n + 1) * P],
                                            xn2[:, 4 * h + n, :], ident[:, :])
                    last.then_inc(s_htr, 1)

            def body(cc, s, dma, first=False, last=False):
                p_ktr(cc, s)
                p_arg(cc)
                p_qk(cc, s)
                p_kb(cc)
                if not first:
                    r6(cc - 2)
                p_kk(cc, s)
                p_vtr(cc, s)
                r1_ks(cc - 1, 1 - s, first)
                r1_o1(cc - 1, 1 - s, groups=(0,))
                level_0(cc, s)
                r1_o1(cc - 1, 1 - s, groups=(1,))
                level_x(cc, 1)
                r2(cc - 1, 1 - s)
                level_y(cc, s, 1)
                r3_state(cc - 1, 1 - s)
                level_tr(cc, 1)
                r3_o2(cc - 1, 1 - s)
                level_x(cc, 2)
                level_y(cc, s, 2)
                mix(cc - 1, 0)
                level_tr(cc, 2)
                level_x(cc, 3)
                r4(cc - 1)
                mix(cc - 1, 1)
                level_y(cc, s, 3)
                level_tr(cc, 3)
                for lv in (4, 5):
                    level_x(cc, lv)
                    if not last:
                        norm_tr(cc + 1, 1 - s, lv - 4, (5, 7), dma)
                    mix(cc - 1, 3 * lv - 10)
                    level_y(cc, s, lv)
                    mix(cc - 1, 3 * lv - 9)
                    level_tr(cc, lv)
                    mix(cc - 1, 3 * lv - 8)
                level_x(cc, 6)
                level_y(cc, s, 6)

            mix.first, mix.last = 0, NC - 1
            norm_tr(0, 0, 0, (4, 5), 16)
            tile(TZ + 5, lambda: norm_tr(0, 0, 1, (4, 5), 16))
            pe.wait_ge(s_scr, 1)
            p_arg(0)
            pe.wait_ge(s_evac, NT)
            p_ktr(0, 0)
            p_qk(0, 0)
            p_kb(0)
            p_kk(0, 0)
            p_vtr(0, 0)
            level_0(0, 0)
            for lv in range(1, LEVELS):
                level_x(0, lv)
                if lv in (4, 5):
                    norm_tr(1, 1, lv - 4, (5, 7), 16)
                level_y(0, 0, lv)
                if lv < LEVELS - 1:
                    level_tr(0, lv)
            body(1, 1, 32, first=True)
            body(2, 0, 32)
            with pe.Fori(1, 3) as i:
                body(i * 2 + 1, 1, i * 16 + 32)
                body(i * 2 + 2, 0, i * 16 + 32)
            body(7, 1, None, last=True)
            r1_ks(7, 1, False, True)
            r1_o1(7, 1, True)
            r2(7, 1)
            r6(6, 0)
            r3_o2(7, 1)
            for k in range(PT):
                mix(7, k)
            r4(7)
            for k in range(PT, KT):
                mix(7, k)

            for half in range(2):
                r = slice(half * HALF, (half + 1) * HALF)
                for k in range(KT):
                    pe.wait_ge(s_f_lo, half * KT + k + 1)
                    for up in range(2):
                        if half == 0 and k == 0:
                            pe.wait_ge(s_ulo, up + 1)
                        for n, (w, h) in enumerate(((f_lo, h2n_hi), (f_hi, h2n_lo),
                                                    (f_hi, h2n_hi))):
                            last = t_.matmul(ps[:, 2 * up + half, :], w[up][:, k, :],
                                             h[:, k, r], start=(k == 0 and n == 0),
                                             stop=(k == KT - 1 and n == 2))
                    if half == 0 and k == 1:
                        r6(7)
            last.then_inc(s_gu, 1)

            def gate_up(f, b, s0, lo_n):
                for up in range(2):
                    pe.wait_ge(s_ulo, lo_n + up)
                    for k in range(KT):
                        for n, (w, h) in enumerate(((u_lo, h2n_hi), (u_hi, h2n_lo),
                                                    (u_hi, h2n_hi))):
                            for c2 in range(2):
                                last = t_.matmul(ps[:, b + 2 * up + c2, :],
                                                 w[s0 + up][:, k, :],
                                                 h[:, k, c2 * HALF:(c2 + 1) * HALF],
                                                 start=(k == 0 and n == 0),
                                                 stop=(k == KT - 1 and n == 2))
                last.then_inc(s_gu, 1)

            pe.wait_ge(s_h2n, 2 * NC)
            gate_up(1, 4, 2, 3)
            with pe.Fori(1, FT // 2) as i:
                for j in range(2):
                    pe.wait_ge(s_hid, i * 2 + (j - 1))
                    gate_up(i * 2 + j, 4 * j, 2 * j, i * 4 + (2 * j + 1))

            def down_tile(tt, s, first, last_k):
                for m, (h, w) in enumerate(((a_lo, d_hi), (a_hi, d_lo), (a_hi, d_hi))):
                    for b in range(2):
                        ins = t_.matmul(ps[:, 2 * tt + b, :], h[s][:, tt * P:(tt + 1) * P],
                                        w[s][:, b * HALF:(b + 1) * HALF],
                                        start=(first and m == 0), stop=(last_k and m == 2))
                return ins

            def down(n, s, first, last_k, waits):
                pe.wait_ge(s_dlo, n + 1)
                for tt in range(4):
                    if first and waits is None and tt == 2:
                        pe.wait_ge(s_hid, FT)
                    if waits is not None:
                        pe.wait_ge(s_dev, waits + tt)
                    ins = down_tile(tt, s, first, last_k)
                    if last_k and tt < 3:
                        ins.then_inc(s_dmm, 1)
                ins.then_inc(s_down, 1)

            pe.wait_ge(s_hid, FT - 1)
            down(0, 0, True, False, None)
            for n in range(1, 4):
                down(n, n, False, False, None)
            with pe.Fori(1, 5) as i:
                for j in range(4):
                    down(i * 4 + j, j, False, False, None)
            down(20, 0, False, False, None)
            down(21, 1, False, True, None)
            down(22, 2, True, False, 1)
            down(23, 3, False, False, None)
            with pe.Fori(6, 10) as i:
                for j in range(4):
                    down(i * 4 + j, j, False, False, None)
            down(40, 0, False, False, None)
            for tt in range(4):
                for n in range(41, 44):
                    if tt == 0:
                        pe.wait_ge(s_dlo, n + 1)
                    ins = down_tile(tt, n % 4, False, n == 43)
                ins.then_inc(s_dmm if tt < 3 else s_down, 1)


_INS = ["x", "c", "w_ada", "b_ada", "norm_mix_gain", "w_in", "conv_w", "a_log", "dt_bias",
        "gdn_norm_gain", "w_pool", "pool_scale", "w_out", "norm_ffn_gain", "w_gate_up", "w_down",
        "norm_final_gain"]


def kernel(**inputs):
    import numpy as _np
    import concourse.bacc as _bacc
    from concourse.bass_utils import run_bass_kernel_spmd as _run

    nc = _bacc.Bacc("TRN2", target_bir_lowering=False, num_devices=1)
    arrays, args = {}, []
    for name in _INS:
        arr = _np.ascontiguousarray(inputs[name])
        arrays[f"in_{name}"] = arr
        args.append(nc.dram_tensor(f"in_{name}", arr.shape, F32, kind="ExternalInput").ap())
    args.append(nc.dram_tensor("out_0", (1, SEQ, D_MODEL), F32, kind="ExternalOutput").ap())
    args.append(nc.dram_tensor("qkvz_spill", (QKVT + ZT, P, SEQ), F32).ap())
    args.append(nc.dram_tensor("h2_spill", (SEQ, D_MODEL), F32).ap())
    hybrid_block(nc, *args)
    r = _run(nc, [arrays], core_ids=[0])
    return r.results[0]["out_0"]
```
